# Optimizing a Trainium2 kernel written in Bass

```python
import math
import jax, jax.numpy as jnp
from jax import lax
import numpy as np

D_MODEL = 1024
BATCH = 1
SEQ = 1024
DEPTH = 1
DEC_BATCH = 1
DEC_SEQ = 512
PAST_LEN = 128

GRID_W = 64
N_BRANCH = 3
BRANCH_W = D_MODEL // 2
NA_HEAD_DIM = 64
NA_HEADS = BRANCH_W // NA_HEAD_DIM
NA_KH = 8
NA_KW = 16
NA_QC = 16
NA_KB = NA_QC + NA_KW
NA_NCB = GRID_W // NA_QC
DN_HEAD_DIM = 128
DN_HEADS = BRANCH_W // DN_HEAD_DIM
DN_CHUNK = 64
CONV_W = 4
LRU_WIDTH = BRANCH_W
LRU_BLOCKS = 8
LRU_BLOCK_W = LRU_WIDTH // LRU_BLOCKS
LRU_C = 8.0
D_FF = 4 * D_MODEL
SPLIT_SIZES = (3 * BRANCH_W, 3 * BRANCH_W, BRANCH_W, 2 * DN_HEADS, 2 * DN_HEADS, LRU_WIDTH, LRU_WIDTH, N_BRANCH * D_MODEL)
D_IN_PROJ = sum(SPLIT_SIZES)
NORM_EPS = 1e-6

kernel_name = "hybrid_na_gdn_rglru_encoder"

def _rmsnorm(x, g):
    xf = x.astype(jnp.float32)
    y = xf * lax.rsqrt(jnp.mean(xf * xf, axis=-1, keepdims=True) + NORM_EPS)
    return (y * g.astype(jnp.float32)).astype(x.dtype)

def _l2norm(t):
    return t * lax.rsqrt(jnp.sum(t * t, axis=-1, keepdims=True) + 1e-6)

def _centred_dwconv(x, w):
    c = x.shape[-1]
    pad_l = CONV_W // 2
    return lax.conv_general_dilated(
        x, w[:, None, :].astype(x.dtype), window_strides=(1,),
        padding=[(pad_l, CONV_W - 1 - pad_l)],
        dimension_numbers=("NWC", "WIO", "NWC"), feature_group_count=c)

def _neighbourhood_attention(qkv, rpb):
    B, T, _ = qkv.shape
    rows = T // GRID_W
    kh = min(NA_KH, rows)
    q, k, v = jnp.split(qkv, 3, axis=-1)
    q = (q * NA_HEAD_DIM ** -0.5).reshape(B, rows, NA_NCB, NA_QC, NA_HEADS, NA_HEAD_DIM)
    q = jnp.moveaxis(q, 1, 0)
    k = k.reshape(B, rows, GRID_W, NA_HEADS, NA_HEAD_DIM)
    v = v.reshape(B, rows, GRID_W, NA_HEADS, NA_HEAD_DIM)
    qcol = np.arange(GRID_W).reshape(NA_NCB, NA_QC)
    win_c0 = np.clip(qcol - NA_KW // 2, 0, GRID_W - NA_KW)
    blk_c0 = np.clip(np.arange(NA_NCB) * NA_QC - NA_KW // 2, 0, GRID_W - NA_KB)
    kcol = blk_c0[:, None] + np.arange(NA_KB)
    col_ok = (kcol[:, None, :] >= win_c0[..., None]) & (kcol[:, None, :] < win_c0[..., None] + NA_KW)
    dc_idx = np.clip(kcol[:, None, :] - qcol[:, :, None] + NA_KW - 1, 0, 2 * NA_KW - 2)
    rpb = rpb.astype(jnp.float32)

    def row_block(args):
        r, q_r = args
        r0 = jnp.clip(r - kh // 2, 0, rows - kh)
        k_r = lax.dynamic_slice_in_dim(k, r0, kh, axis=1)[:, :, kcol]
        v_r = lax.dynamic_slice_in_dim(v, r0, kh, axis=1)[:, :, kcol]
        s = jnp.einsum("bjqhd,bijkhd->bhjqik", q_r, k_r).astype(jnp.float32)
        dr_idx = r0 + jnp.arange(kh) - r + NA_KH - 1
        bias = rpb[:, dr_idx[None, None, :, None], dc_idx[:, :, None, :]]
        s = jnp.where(col_ok[:, :, None, :], s + bias, -jnp.inf)
        p = jax.nn.softmax(s.reshape(s.shape[:4] + (kh * NA_KB,)), axis=-1).reshape(s.shape)
        return jnp.einsum("bhjqik,bijkhd->bjqhd", p.astype(v.dtype), v_r)

    o = lax.map(row_block, (jnp.arange(rows), q))
    return jnp.moveaxis(o, 0, 1).reshape(B, T, BRANCH_W)

def _delta_rule_chunked(q, k, v, beta, g):
    B, T, H, DK = q.shape
    DV = v.shape[-1]
    C = DN_CHUNK
    N = T // C

    def to_chunks(t):
        t = jnp.moveaxis(t, 2, 1)
        return t.reshape((B, H, N, C) + t.shape[3:])

    q, k, v = to_chunks(q), to_chunks(k), to_chunks(v)
    beta, g = to_chunks(beta), to_chunks(g)
    g = jnp.cumsum(g, axis=-1)
    idx = jnp.arange(C)
    incl = idx[:, None] >= idx[None, :]
    strict = idx[:, None] > idx[None, :]
    decay = jnp.exp(jnp.where(incl, g[..., :, None] - g[..., None, :], -jnp.inf))
    k_beta = k * beta[..., None]
    a_mat = jnp.einsum("bhnid,bhnjd->bhnij", k_beta, k) * jnp.where(strict, decay, 0.0)
    eye = jnp.eye(C, dtype=q.dtype)
    rhs = jnp.concatenate([v * beta[..., None], k_beta * jnp.exp(g)[..., None]], axis=-1)
    sol = lax.linalg.triangular_solve(eye + a_mat, rhs, left_side=True, lower=True, unit_diagonal=True)
    u, w = sol[..., :DV], sol[..., DV:]
    qk = jnp.einsum("bhnid,bhnjd->bhnij", q, k) * decay
    g_last = g[..., -1:]
    q_dec = q * jnp.exp(g)[..., None]
    k_dec = k * jnp.exp(g_last - g)[..., None]

    def step(s, xs):
        qk_c, u_c, w_c, qd_c, kd_c, gl_c = xs
        v_new = u_c - jnp.einsum("bhck,bhkv->bhcv", w_c, s)
        o = jnp.einsum("bhck,bhkv->bhcv", qd_c, s) + jnp.einsum("bhij,bhjv->bhiv", qk_c, v_new)
        s = s * jnp.exp(gl_c)[..., None] + jnp.einsum("bhck,bhcv->bhkv", kd_c, v_new)
        return s, o

    xs = (jnp.moveaxis(qk, 2, 0), jnp.moveaxis(u, 2, 0), jnp.moveaxis(w, 2, 0),
          jnp.moveaxis(q_dec, 2, 0), jnp.moveaxis(k_dec, 2, 0), jnp.moveaxis(g_last, 2, 0))
    s0 = jnp.zeros((B, H, DK, DV), q.dtype)
    _, o = lax.scan(step, s0, xs)
    o = jnp.moveaxis(o, 0, 2).reshape(B, H, T, DV)
    return jnp.moveaxis(o, 1, 2)

def _gated_deltanet(qkv, z, b_logit, a_logit, conv_w, a_log, dt_bias, norm_w):
    B, T, _ = qkv.shape
    out_dtype = qkv.dtype
    f32 = jnp.float32
    qkv = jax.nn.silu(_centred_dwconv(qkv, conv_w)).astype(f32)
    q, k, v = jnp.split(qkv, 3, axis=-1)
    q = _l2norm(q.reshape(B, T, DN_HEADS, DN_HEAD_DIM)) * DN_HEAD_DIM ** -0.5
    k = _l2norm(k.reshape(B, T, DN_HEADS, DN_HEAD_DIM))
    v = v.reshape(B, T, DN_HEADS, DN_HEAD_DIM)
    beta = jax.nn.sigmoid(b_logit.astype(f32)).reshape(B, T, 2, DN_HEADS)
    g = -jnp.exp(a_log.astype(f32)) * jax.nn.softplus(a_logit.astype(f32).reshape(B, T, 2, DN_HEADS) + dt_bias.astype(f32))
    o_fwd = _delta_rule_chunked(q, k, v, beta[:, :, 0], g[:, :, 0])
    flip = lambda t: jnp.flip(t, axis=1)
    o_bwd = flip(_delta_rule_chunked(flip(q), flip(k), flip(v), flip(beta[:, :, 1]), flip(g[:, :, 1])))
    o = o_fwd + o_bwd
    o = o * lax.rsqrt(jnp.mean(o * o, axis=-1, keepdims=True) + NORM_EPS) * norm_w.astype(f32)
    o = o * jax.nn.silu(z.astype(f32).reshape(B, T, DN_HEADS, DN_HEAD_DIM))
    return o.reshape(B, T, BRANCH_W).astype(out_dtype)

def _combine(left, right):
    a_l, b_l = left
    a_r, b_r = right
    return a_l * a_r, a_r * b_l + b_r

def _linear_scan(a, b, reverse):
    _, h = lax.associative_scan(_combine, (a, b), reverse=reverse, axis=1)
    return h

def _rglru_branch(xb, gate, conv_w, conv_b, w_r, b_r, w_i, b_i, lam):
    B, T, _ = xb.shape
    f32 = jnp.float32
    xc = (_centred_dwconv(xb, conv_w) + conv_b).astype(f32)
    xblk = xc.reshape(B, T, LRU_BLOCKS, LRU_BLOCK_W)
    r = jax.nn.sigmoid(jnp.einsum("btnc,dncm->btdnm", xblk, w_r.astype(f32)).reshape(B, T, 2, LRU_WIDTH) + b_r.astype(f32))
    i = jax.nn.sigmoid(jnp.einsum("btnc,dncm->btdnm", xblk, w_i.astype(f32)).reshape(B, T, 2, LRU_WIDTH) + b_i.astype(f32))
    log_a = -LRU_C * r * jax.nn.softplus(-lam.astype(f32))
    a = jnp.exp(log_a)
    b = jnp.sqrt(-jnp.expm1(2.0 * log_a)) * i * xc[:, :, None, :]
    h = _linear_scan(a[:, :, 0], b[:, :, 0], False) + _linear_scan(a[:, :, 1], b[:, :, 1], True)
    return (h * jax.nn.gelu(gate.astype(f32))).astype(xb.dtype)

def _hybrid_mixer(u, w_in, na_rpb, dn_conv_w, dn_a_log, dn_dt_bias, dn_norm, lru_conv_w, lru_conv_b,
                  lru_w_r, lru_b_r, lru_w_i, lru_b_i, lru_lam, w_br, w_out):
    B, T, _ = u.shape
    proj = u @ w_in
    na_qkv, dn_qkv, dn_z, dn_b, dn_a, lru_x, lru_gate, merge_logits = jnp.split(
        proj, np.cumsum(SPLIT_SIZES)[:-1].tolist(), axis=-1)
    o_na = _neighbourhood_attention(na_qkv, na_rpb)
    o_dn = _gated_deltanet(dn_qkv, dn_z, dn_b, dn_a, dn_conv_w, dn_a_log, dn_dt_bias, dn_norm)
    o_lru = _rglru_branch(lru_x, lru_gate, lru_conv_w, lru_conv_b, lru_w_r, lru_b_r, lru_w_i, lru_b_i, lru_lam)
    branches = jnp.stack([o_na, o_dn.astype(u.dtype), o_lru], axis=2)
    y = jnp.einsum("btnc,ncd->btnd", branches, w_br)
    gates = jax.nn.sigmoid(merge_logits.reshape(B, T, N_BRANCH, D_MODEL))
    merged = jnp.sum(gates * y, axis=2)
    return merged @ w_out

def _sq_relu_mlp(u, w1, w2):
    return jnp.square(jax.nn.relu(u @ w1)) @ w2

def _trunk(x, norm1, w_in, na_rpb, dn_conv_w, dn_a_log, dn_dt_bias, dn_norm, lru_conv_w, lru_conv_b,
           lru_w_r, lru_b_r, lru_w_i, lru_b_i, lru_lam, w_br, w_out, norm2, w_mlp1, w_mlp2, norm_f):
    for l in range(DEPTH):
        u = _rmsnorm(x, norm1[l])
        x = x + _hybrid_mixer(u, w_in[l], na_rpb[l], dn_conv_w[l], dn_a_log[l], dn_dt_bias[l], dn_norm[l],
                              lru_conv_w[l], lru_conv_b[l], lru_w_r[l], lru_b_r[l], lru_w_i[l], lru_b_i[l],
                              lru_lam[l], w_br[l], w_out[l])
        u = _rmsnorm(x, norm2[l])
        x = x + _sq_relu_mlp(u, w_mlp1[l], w_mlp2[l])
    return _rmsnorm(x, norm_f)

def setup_inputs(seed: int = 0) -> dict:
    key = jax.random.key(seed)
    ks = jax.random.split(key, 24)
    f32 = jnp.float32

    def nrm(k, shape, scale):
        return scale * jax.random.normal(k, shape, f32)

    x_prompt = nrm(ks[0], (BATCH, SEQ, D_MODEL), 1.0)
    x_sample = nrm(ks[1], (DEC_BATCH, DEC_SEQ, D_MODEL), 1.0)
    norm1 = 1.0 + nrm(ks[2], (DEPTH, D_MODEL), 0.02)
    w_in = nrm(ks[3], (DEPTH, D_MODEL, D_IN_PROJ), D_MODEL ** -0.5)
    na_rpb = nrm(ks[4], (DEPTH, NA_HEADS, 2 * NA_KH - 1, 2 * NA_KW - 1), 0.1)
    dn_conv_w = nrm(ks[5], (DEPTH, CONV_W, 3 * BRANCH_W), CONV_W ** -0.5)
    dn_a_log = jnp.log(jax.random.uniform(ks[6], (DEPTH, 2, DN_HEADS), f32, 1.0, 16.0))
    dt = jnp.exp(jax.random.uniform(ks[7], (DEPTH, 2, DN_HEADS), f32, math.log(1e-3), math.log(1e-1)))
    dn_dt_bias = dt + jnp.log(-jnp.expm1(-dt))
    dn_norm = 1.0 + nrm(ks[8], (DEPTH, DN_HEAD_DIM), 0.02)
    lru_conv_w = nrm(ks[9], (DEPTH, CONV_W, LRU_WIDTH), CONV_W ** -0.5)
    lru_conv_b = nrm(ks[10], (DEPTH, LRU_WIDTH), 0.02)
    lru_w_r = nrm(ks[11], (DEPTH, 2, LRU_BLOCKS, LRU_BLOCK_W, LRU_BLOCK_W), LRU_BLOCK_W ** -0.5)
    lru_b_r = nrm(ks[12], (DEPTH, 2, LRU_WIDTH), 0.02)
    lru_w_i = nrm(ks[13], (DEPTH, 2, LRU_BLOCKS, LRU_BLOCK_W, LRU_BLOCK_W), LRU_BLOCK_W ** -0.5)
    lru_b_i = nrm(ks[14], (DEPTH, 2, LRU_WIDTH), 0.02)
    a_c = jax.random.uniform(ks[15], (DEPTH, 2, LRU_WIDTH), f32, 0.9, 0.999)
    a0 = a_c ** (1.0 / LRU_C)
    lru_lam = jnp.log(a0) - jnp.log1p(-a0)
    w_br = nrm(ks[16], (DEPTH, N_BRANCH, BRANCH_W, D_MODEL), BRANCH_W ** -0.5)
    w_out = nrm(ks[17], (DEPTH, D_MODEL, D_MODEL), D_MODEL ** -0.5)
    norm2 = 1.0 + nrm(ks[18], (DEPTH, D_MODEL), 0.02)
    w_mlp1 = nrm(ks[19], (DEPTH, D_MODEL, D_FF), D_MODEL ** -0.5)
    w_mlp2 = nrm(ks[20], (DEPTH, D_FF, D_MODEL), D_FF ** -0.5)
    norm_f = 1.0 + nrm(ks[21], (D_MODEL,), 0.02)
    return {"x_prompt": x_prompt, "x_sample": x_sample, "norm1": norm1, "w_in": w_in, "na_rpb": na_rpb,
            "dn_conv_w": dn_conv_w, "dn_a_log": dn_a_log, "dn_dt_bias": dn_dt_bias, "dn_norm": dn_norm,
            "lru_conv_w": lru_conv_w, "lru_conv_b": lru_conv_b, "lru_w_r": lru_w_r, "lru_b_r": lru_b_r,
            "lru_w_i": lru_w_i, "lru_b_i": lru_b_i, "lru_lam": lru_lam, "w_br": w_br, "w_out": w_out,
            "norm2": norm2, "w_mlp1": w_mlp1, "w_mlp2": w_mlp2, "norm_f": norm_f}

def reference(x_prompt, x_sample, norm1, w_in, na_rpb, dn_conv_w, dn_a_log, dn_dt_bias, dn_norm,
              lru_conv_w, lru_conv_b, lru_w_r, lru_b_r, lru_w_i, lru_b_i, lru_lam, w_br, w_out,
              norm2, w_mlp1, w_mlp2, norm_f):
    y_prompt = _trunk(x_prompt, norm1, w_in, na_rpb, dn_conv_w, dn_a_log, dn_dt_bias, dn_norm,
                      lru_conv_w, lru_conv_b, lru_w_r, lru_b_r, lru_w_i, lru_b_i, lru_lam, w_br, w_out,
                      norm2, w_mlp1, w_mlp2, norm_f)
    y_sample = _trunk(x_sample, norm1, w_in, na_rpb, dn_conv_w, dn_a_log, dn_dt_bias, dn_norm,
                      lru_conv_w, lru_conv_b, lru_w_r, lru_b_r, lru_w_i, lru_b_i, lru_lam, w_br, w_out,
                      norm2, w_mlp1, w_mlp2, norm_f)
    return (y_prompt, y_sample)


_drawn_inputs = setup_inputs


def setup_inputs(seed=0):
    import zlib

    import numpy as np

    out = dict(_drawn_inputs(seed))
    spreads = {}
    factors = {'norm1': 3.857,
     'na_rpb': 38.064,
     'dn_norm': 23.831,
     'lru_b_r': 34.926,
     'lru_b_i': 32.745,
     'norm2': 12.698,
     'norm_f': 21.203,
     'lru_conv_b': 6.148}
    for name, (base, spread) in spreads.items():
        noise = np.random.default_rng([zlib.crc32(name.encode()), seed]).standard_normal(out[name].shape)
        drawn = base * np.exp(spread * noise) if base else spread * noise
        out[name] = __import__('jax').numpy.asarray(drawn.astype(out[name].dtype))
    for name, factor in factors.items():
        out[name] = (out[name] * factor).astype(out[name].dtype)
    return out
```

```python
from contextlib import ExitStack

import concourse.bass as bass
import numpy as np
from concourse import mybir

F32 = mybir.dt.float32
F32R = mybir.dt.float32r
U8 = mybir.dt.uint8
ACT = mybir.ActivationFunctionType
ALU = mybir.AluOpType
AX = mybir.AxisListType

P = 128
D = 1024
KD = D // P
SEG = [(0, 1024), (1024, 512)]
T = 1536
NT = T // P
TB = 512
NTB = T // TB
EPS = 1e-6
BW = 512
CW = 4

GRID = 64
NA_HD = 64
NA_KH = 8
NA_KW = 16
NDR = 2 * NA_KH - 1
NDC = 2 * NA_KW - 1
NEG = -1e30

HEADS = 4
LEVELS = 7
FF = 4096

COL_BA = 3584
COL_LRU = 3600
COL_GATE = 4624
TILE_DN = 12
TILE_Z = 24
TILE_BA = 28
TILE_LRU = 29
N_MIX = 37
N_GATE = 24


def dsl(i, n=1):
    return bass.ds(i * n, n)


class Space:

    def __init__(self, nc, name):
        self.nc, self.name, self.ctx, self.sems = nc, name, ExitStack(), []

    def __enter__(self):
        return self

    def __exit__(self, *e):
        self.ctx.__exit__(*e)
        if e[0] is None:
            self.nc.clear_and_free_semaphores(self.sems)
            self.nc.all_engine_barrier()

    def sb(self, name, shape, dt=F32):
        return self.ctx.enter_context(self.nc.sbuf_tensor(f"{self.name}_{name}", [P] + list(shape), dt))

    def ps(self, name, shape):
        return self.ctx.enter_context(self.nc.psum_tensor(f"{self.name}_{name}", [P] + list(shape), F32))

    def sem(self, name):
        self.sems.append(self.nc.alloc_semaphore(name=f"{self.name}_{name}"))
        return self.sems[-1]

    def block(self):
        return self.ctx.enter_context(self.nc.Block())


def mm3(pe, out, w_hi, w_lo, x_hi, x_lo, first, last):
    pe.matmul(out, w_hi, x_hi, start=first, stop=False)
    pe.matmul(out, w_hi, x_lo, start=False, stop=False)
    return pe.matmul(out, w_lo, x_hi, start=False, stop=last)


def constants(nc, ident, ones):
    with Space(nc, "c") as s:
        made, cut = s.sem("made"), s.sem("cut")
        block = s.block()

        @block.gpsimd
        def _(pool):
            pool.memset(ones[:], 1.0).then_inc(made, 1)
            pool.memset(ident[:], 0.0).then_inc(made, 1)
            pool.wait_ge(made, 2)
            pool.affine_select(out=ident[:], in_=ident[:], compare_op=ALU.not_equal, fill=1.0, base=0,
                               pattern=[[-1, P]], channel_multiplier=1).then_inc(cut, 1)
            pool.wait_ge(cut, 1)


def norm_transpose(nc, name, x, sources, gain, u_hi, u_lo, ident, tiles):
    n = len(tiles)
    G = 2
    with Space(nc, name) as s:
        loaded = [s.sem(f"loaded{t}") for t in range(n)]
        gained = s.sem("gained")
        squared, rstd_in, rstd_done = s.sem("squared"), s.sem("rstd_in"), s.sem("rstd_done")
        normed, turned, scaled = s.sem("normed"), s.sem("turned"), s.sem("scaled")
        hi_done, lo_done, recip = s.sem("hi_done"), s.sem("lo_done"), s.sem("recip")
        junk = s.sb("junk", [D])
        xn = s.sb("xn", [2, D])
        uf = s.sb("uf", [2, KD, P])
        gcol = s.sb("gcol", [KD])
        ss = s.sb("ss", [n])
        ms = s.sb("ms", [n])
        rr = s.sb("rr", [n])
        rstd = s.sb("rstd", [n])
        pst = s.ps("pst", [2, KD, P])
        block = s.block()

        @block.sync
        def _(sp):
            sp.dma_start(gcol[:], gain.rearrange("(k p) -> p k", p=P), allow_slow_non_contiguous=True).then_inc(gained, 16)
            if sources is not None:
                for j, t in enumerate(tiles):
                    sp.dma_start(x[:, t, :], sources[j]).then_inc(loaded[j], 16)

        @block.scalar
        def _(act):
            for j0 in range(0, n, G):
                for j in range(j0, j0 + G):
                    if sources is not None:
                        act.wait_ge(loaded[j], 16)
                    if j:
                        act.wait_ge(squared, j)
                    act.activation(junk[:], x[:, tiles[j], :], ACT.Square, accum_out=ss[:, j:j + 1]).then_inc(squared, 1)
                act.wait_ge(recip, j0 // G + 1)
                act.activation(rstd[:, j0:j0 + G], rr[:, j0:j0 + G], ACT.Sqrt).then_inc(rstd_done, 1)
                for j in range(j0, j0 + G):
                    act.wait_ge(scaled, j + 1)
                    act.copy(u_hi[:, :, j * P:(j + 1) * P], uf[:, j % 2]).then_inc(hi_done, 1)

        @block.vector
        def _(dve):
            for j0 in range(0, n, G):
                dve.wait_ge(squared, j0 + G)
                dve.tensor_scalar(ms[:, j0:j0 + G], ss[:, j0:j0 + G], 1.0 / D, EPS, ALU.mult, ALU.add).then_inc(rstd_in, 1)
                dve.wait_ge(rstd_in, j0 // G + 1)
                dve.reciprocal(rr[:, j0:j0 + G], ms[:, j0:j0 + G]).then_inc(recip, 1)
                dve.wait_ge(rstd_done, j0 // G + 1)
                for j in range(j0, j0 + G):
                    if j >= 2:
                        dve.wait_ge(turned, j - 1)
                    dve.tensor_scalar(xn[:, j % 2], x[:, tiles[j], :], rstd[:, j:j + 1], None, ALU.mult).then_inc(normed, 1)
                for j in range(j0, j0 + G):
                    dve.wait_ge(turned, j + 1)
                    if j == 0:
                        dve.wait_ge(gained, 16)
                    if j >= 2:
                        dve.wait_ge(hi_done, j - 1)
                        dve.wait_ge(lo_done, j - 1)
                    dve.tensor_tensor(uf[:, j % 2], pst[:, j % 2], gcol[:].unsqueeze(2).to_broadcast([P, KD, P]),
                                      ALU.mult).then_inc(scaled, 1)

        @block.tensor
        def _(pe):
            for j in range(n):
                pe.wait_ge(normed, j + 1)
                if j >= 2:
                    pe.wait_ge(scaled, j - 1)
                for k in range(KD):
                    last = pe.transpose(pst[:, j % 2, k], xn[:, j % 2, k * P:(k + 1) * P], ident[:])
                last.then_inc(turned, 1)

        @block.gpsimd
        def _(pool):
            for j in range(n):
                pool.wait_ge(hi_done, j + 1)
                pool.tensor_tensor(u_lo[:, :, j * P:(j + 1) * P], uf[:, j % 2],
                                   u_hi[:, :, j * P:(j + 1) * P].bitcast(F32), ALU.subtract).then_inc(lo_done, 1)
            pool.wait_ge(lo_done, n)


def lagged(eng, n, unit, lag=None):
    unit(0, 0)
    pairs = (n - 1) // 2

    def both(u, b):
        unit(u, b)
        if lag is not None:
            lag(u - 1, 1 - b)
    if pairs:
        with eng.Fori(0, pairs) as i:
            both(i * 2 + 1, 1)
            both(i * 2 + 2, 0)
    if (n - 1) % 2:
        both(n - 1, (n - 1) % 2)
    if lag is not None:
        lag(n - 1, (n - 1) % 2)


def nth16(u, b, credit=0):
    return (u - b) * 8 + 16 + credit


def project(nc, name, u_hi, u_lo, w, col0, n, dst, tile0):
    with Space(nc, name) as s:
        w_raw = s.sb("w_raw", [2, KD, P])
        w_hi = s.sb("w_hi", [2, KD, P], F32R)
        w_lo = s.sb("w_lo", [2, KD, P], F32R)
        stage = s.sb("stage", [2, T])
        acc = s.ps("acc", [2, 4, TB])
        w_in = [s.sem(f"w_in{b}") for b in range(2)]
        stored = [s.sem(f"stored{b}") for b in range(2)]
        hi_done, lo_done = s.sem("hi_done"), s.sem("lo_done")
        mm_done, evicted = s.sem("mm_done"), s.sem("evicted")
        block = s.block()
        w_t = w.rearrange("(k p) n -> p k n", p=P)


        @block.sync
        def _(sp):
            for b in range(2):
                sp.sem_inc(stored[b], 16)

            def load(u, b):
                sp.wait_ge(hi_done, u + 1)
                sp.wait_ge(lo_done, u + 1)
                sp.dma_start(w_raw[:, b], w_t[:, :, bass.ds(u * P + col0, P)]).then_inc(w_in[b], 16)

            def store(u, b):
                sp.wait_ge(evicted, u + 3)
                sp.dma_start(dst[bass.ds(u + tile0, 1)].rearrange("a p n -> p (a n)"), stage[:, b]).then_inc(stored[b], 16)
            lagged(sp, n, load, store)
            for b in range(2):
                sp.wait_ge(stored[b], 16 + 16 * ((n - b + 1) // 2))

        @block.scalar
        def _(act):
            act.sem_inc(hi_done, 2)

            def unit(u, b):
                act.wait_ge(w_in[b], nth16(u, b))
                act.wait_ge(mm_done, u + 1)
                act.copy(w_hi[:, b], w_raw[:, b]).then_inc(hi_done, 1)
            lagged(act, n, unit)

        @block.gpsimd
        def _(pool):
            pool.sem_inc(lo_done, 2)

            def unit(u, b):
                pool.wait_ge(hi_done, u + 3)
                pool.tensor_tensor(w_lo[:, b], w_raw[:, b], w_hi[:, b].bitcast(F32), ALU.subtract).then_inc(lo_done, 1)
            lagged(pool, n, unit)

        @block.tensor
        def _(pe):
            pe.sem_inc(mm_done, 2)

            def unit(u, b):
                pe.wait_ge(lo_done, u + 3)
                pe.wait_ge(evicted, u + 1)
                for k in range(KD):
                    for tb in range(NTB):
                        sl = slice(tb * TB, (tb + 1) * TB)
                        last = mm3(pe, acc[:, b, tb], w_hi[:, b, k], w_lo[:, b, k], u_hi[:, k, sl], u_lo[:, k, sl],
                                   k == 0, k == KD - 1)
                last.then_inc(mm_done, 1)
            lagged(pe, n, unit)

        @block.vector
        def _(dve):
            dve.sem_inc(evicted, 2)

            def unit(u, b):
                dve.wait_ge(mm_done, u + 3)
                dve.wait_ge(stored[b], nth16(u, b))
                dve.tensor_copy(stage[:, b].rearrange("p (a n) -> p a n", a=NTB), acc[:, b, 0:NTB]).then_inc(evicted, 1)
            lagged(dve, n, unit)


class Chain:

    def __init__(self, eng, sem, i, per):
        self.eng, self.sem, self.i, self.per, self.n = eng, sem, i, per, 0

    def add(self, ins):
        ins.then_inc(self.sem, 1)
        self.n += 1
        return ins

    def link(self, ins):
        self.add(ins)
        self.wait()

    def wait(self):
        self.eng.wait_ge(self.sem, self.i * self.per + self.n)

    def end(self):
        assert self.n == self.per, self.n


def log1p_steps(dve, c, e, z, z2, acc):
    c.link(dve.tensor_scalar(z2, e, 2.0, None, ALU.add))
    c.link(dve.reciprocal(z, z2))
    c.link(dve.tensor_tensor(z, z, e, ALU.mult))
    c.link(dve.tensor_tensor(z2, z, z, ALU.mult))
    c.link(dve.tensor_scalar(acc, z2, 2.0 / 17, 2.0 / 15, ALU.mult, ALU.add))
    for n in (13, 11, 9, 7, 5, 3, 1):
        c.link(dve.tensor_tensor(acc, acc, z2, ALU.mult))
        c.link(dve.tensor_scalar(acc, acc, 2.0 / n, None, ALU.add))
    c.link(dve.tensor_tensor(acc, acc, z, ALU.mult))


LOG1P_STEPS = 20
PADW = T + 6


def conv_load(eng, xpad, src, sem):
    for o, (b, n) in zip((2, 1024 + 5), SEG):
        eng.dma_start(xpad[:, o:o + n], src[:, b:b + n]).then_inc(sem, 16)


def conv_zero(eng, xpad, sem):
    eng.memset(xpad[:, 0:2], 0.0).then_inc(sem, 1)
    eng.memset(xpad[:, 1026:1029], 0.0).then_inc(sem, 1)
    eng.memset(xpad[:, 1541:PADW], 0.0).then_inc(sem, 1)


def conv_steps(dve, c, out, xpad, cw, bias=None):
    for j in range(CW):
        for o, (b, n) in zip((0, 1024 + 3), SEG):
            dst, src = out[:, b:b + n], xpad[:, o + j:o + j + n]
            if j == 0 and bias is not None:
                c.add(dve.tensor_scalar(dst, src, cw[:, 0:1], bias, ALU.mult, ALU.add))
            elif j == 0:
                c.add(dve.tensor_scalar(dst, src, cw[:, 0:1], None, ALU.mult))
            else:
                c.add(dve.scalar_tensor_tensor(dst, src, cw[:, j:j + 1], dst, ALU.mult, ALU.add))
        c.wait()


def rglru(nc, proj, o_t, conv_w, conv_b, w_r, b_r, w_i, b_i, lam):
    with Space(nc, "lru") as s:
        loaded, gate_in, param_in = s.sem("loaded"), s.sem("gate_in"), s.sem("param_in")
        wbd_in, stored, zeroed = s.sem("wbd_in"), s.sem("stored"), s.sem("zeroed")
        chain, achain = s.sem("chain"), s.sem("achain")
        conv_done, gates_mm, params_done = s.sem("conv_done"), s.sem("gates_mm"), s.sem("params_done")
        exp_ready, exp_done = s.sem("exp_ready"), s.sem("exp_done")
        r_done, i_done, rt_done = s.sem("r_done"), s.sem("i_done"), s.sem("rt_done")
        v_done, a_done, a2_done, scan_done = s.sem("v_done"), s.sem("a_done"), s.sem("a2_done"), s.sem("scan_done")
        gelu_in, gelu_th, out_done, sum_done = s.sem("gelu_in"), s.sem("gelu_th"), s.sem("out_done"), s.sem("sum_done")
        free, m_done, b_done, gg_done = (s.sem(x) for x in ("free", "m_done", "b_done", "gg_done"))
        xpad, xc, gt = s.sb("xpad", [PADW]), s.sb("xc", [T]), s.sb("gt", [T])
        sg, ti, v, a = s.sb("sg", [T]), s.sb("ti", [T]), s.sb("v", [T]), s.sb("a", [T])
        rt, m, b = s.sb("rt", [T]), s.sb("m", [T]), s.sb("b", [T])
        h = s.sb("h", [2, T])
        gi, tg = s.sb("gi", [T]), s.sb("tg", [T])
        wbd = s.sb("wbd", [2, 2, P])
        cw = s.sb("cw", [CW])
        prm = s.sb("prm", [7])
        hb = s.sb("hb", [4])
        lt = s.sb("lt", [5, 2])
        sp2, sp4, nsp4 = s.sb("sp2", [2]), s.sb("sp4", [2]), s.sb("nsp4", [2])
        psr, psi = s.ps("psr", [4, TB]), s.ps("psi", [4, TB])
        block = s.block()
        CT = BW // P
        K_DVE = 3 + LOG1P_STEPS + 4 + 2 * CW

        @block.sync
        def _(sp):
            sp.wait_ge(zeroed, 4)
            with sp.Fori(0, CT) as i:
                sp.wait_ge(free, i + 1)
                conv_load(sp, xpad, proj[dsl(i + TILE_LRU)].rearrange("a p n -> p (a n)"), loaded)
                ch = bass.ds(i * P, P)
                sp.dma_start(cw[:], conv_w[:, ch].rearrange("j p -> p j"), allow_slow_non_contiguous=True).then_inc(param_in, 16)
                sp.dma_start(prm[:, 0:1], conv_b[ch].rearrange("(p a) -> p a", a=1)).then_inc(param_in, 16)
                for o, v in ((1, b_r), (3, b_i), (5, lam)):
                    sp.dma_start(prm[:, o:o + 2], v[:, ch].rearrange("d p -> p d"), allow_slow_non_contiguous=True).then_inc(param_in, 16)
                for g, v in enumerate((w_r, w_i)):
                    for half in range(2):
                        r = slice(64 * half, 64 * half + 64)
                        sp.dma_start(wbd[r, g, :, r], v[:, bass.ds(i * 2 + half, 1)].rearrange("d a c m -> c (d a) m")).then_inc(wbd_in, 16)
                sp.dma_start(gt[:], proj[dsl(i + (TILE_LRU + CT))].rearrange("a p n -> p (a n)")).then_inc(gate_in, 16)
                sp.wait_ge(out_done, i + 1)
                sp.dma_start(o_t[dsl(i + 2 * CT)].rearrange("a p n -> p (a n)"), gi[:]).then_inc(stored, 16)
                sp.wait_ge(stored, i * 16 + 16)
                sp.sem_inc(free, 1)

        @block.gpsimd
        def _(pool):
            conv_zero(pool, xpad, zeroed)
            pool.memset(wbd[:], 0.0).then_inc(zeroed, 1)
            pool.sem_inc(free, 1)
            with pool.Fori(0, CT) as i:
                pool.wait_ge(gelu_in, i * 3 + 2)
                pool.tensor_tensor(gi[:], tg[:], gt[:], ALU.mult).then_inc(gelu_in, 1)
                pool.wait_ge(scan_done, i * 2 + 2)
                pool.tensor_tensor(m[:], h[:, 0], h[:, 1], ALU.add).then_inc(sum_done, 1)

        @block.scalar
        def _(act):
            with act.Fori(0, CT) as i:
                act.wait_ge(exp_ready, i + 1)
                act.activation(lt[:, 2], lt[:, 1], ACT.Exp, scale=-1.0).then_inc(exp_done, 1)
                act.wait_ge(gate_in, i * 16 + 16)
                act.activation(gi[:], gt[:], ACT.Square).then_inc(gelu_in, 1)
                act.wait_ge(gelu_in, i * 3 + 1)
                act.activation(tg[:], gi[:], ACT.Copy, scale=0.044715, bias=1.0).then_inc(gelu_in, 1)
                act.wait_ge(gelu_in, i * 3 + 3)
                act.activation(tg[:], gi[:], ACT.Tanh, scale=float(np.sqrt(2 / np.pi))).then_inc(gelu_th, 1)
                act.wait_ge(params_done, i + 1)
                for d in range(2):
                    act.wait_ge(gates_mm, i * 4 + 2 * d + 1)
                    if d:
                        act.wait_ge(scan_done, i * 2 + 1)
                    act.activation(sg[:].rearrange("p (a n) -> p a n", a=NTB), psr[:, 0:NTB], ACT.Tanh, bias=hb[:, d:d + 1],
                                   scale=0.5).then_inc(achain, 1)
                    act.wait_ge(achain, i * 2 + d + 1)
                    act.activation(a[:], sg[:], ACT.Exp, bias=nsp4[:, d:d + 1], scale=nsp4[:, d:d + 1]).then_inc(a_done, 1)
                    act.wait_ge(a_done, i * 2 + d + 1)
                    act.activation(sg[:], sg[:], ACT.Tanh, bias=sp4[:, d:d + 1], scale=sp4[:, d:d + 1]).then_inc(r_done, 1)
                    act.activation(rt[:], a[:], ACT.Square).then_inc(a2_done, 1)
                    act.wait_ge(gates_mm, i * 4 + 2 * d + 2)
                    act.activation(ti[:].rearrange("p (a n) -> p a n", a=NTB), psi[:, 0:NTB], ACT.Tanh, bias=hb[:, 2 + d:3 + d],
                                   scale=0.5).then_inc(i_done, 1)
                    act.wait_ge(v_done, i * 2 + d + 1)
                    act.activation(rt[:], v[:], ACT.Sqrt).then_inc(rt_done, 1)

        @block.tensor
        def _(pe):
            with pe.Fori(0, CT) as i:
                pe.wait_ge(conv_done, i + 1)
                pe.wait_ge(wbd_in, i * 64 + 64)
                for d in range(2):
                    for g, ps in enumerate((psr, psi)):
                        if d:
                            pe.wait_ge((r_done, i_done)[g], i * 2 + 1)
                        for tb in range(NTB):
                            last = pe.matmul(ps[:, tb], wbd[:, g, d], xc[:, tb * TB:(tb + 1) * TB], start=True, stop=True)
                        last.then_inc(gates_mm, 1)

        @block.vector
        def _(dve):
            with dve.Fori(0, CT) as i:
                c = Chain(dve, chain, i, K_DVE)
                dve.wait_ge(param_in, i * 80 + 80)
                c.add(dve.tensor_scalar(hb[:], prm[:, 1:5], 0.5, None, ALU.mult))
                c.link(dve.tensor_scalar(lt[:, 0], prm[:, 5:7], -1.0, None, ALU.mult))
                c.link(dve.tensor_tensor(lt[:, 1], lt[:, 0], prm[:, 5:7], ALU.max))
                dve.sem_inc(exp_ready, 1)
                dve.wait_ge(exp_done, i + 1)
                log1p_steps(dve, c, lt[:, 2], lt[:, 3], lt[:, 4], sp2[:])
                c.link(dve.tensor_scalar(lt[:, 0], lt[:, 0], 0.0, None, ALU.max))
                c.link(dve.tensor_tensor(sp2[:], sp2[:], lt[:, 0], ALU.add))
                c.add(dve.tensor_scalar(sp4[:], sp2[:], 4.0, None, ALU.mult))
                c.add(dve.tensor_scalar(nsp4[:], sp2[:], -4.0, None, ALU.mult))
                c.wait()
                dve.sem_inc(params_done, 1)
                dve.wait_ge(loaded, i * 32 + 32)
                conv_steps(dve, c, xc, xpad, cw, prm[:, 0:1])
                dve.sem_inc(conv_done, 1)
                for d in range(2):
                    dve.wait_ge(r_done, i * 2 + d + 1)
                    dve.wait_ge(a2_done, i * 2 + d + 1)
                    dve.scalar_tensor_tensor(v[:], rt[:], 1.0, sg[:], ALU.add, ALU.mult).then_inc(v_done, 1)
                    dve.wait_ge(i_done, i * 2 + d + 1)
                    if d:
                        dve.wait_ge(scan_done, i * 2 + 1)
                    dve.scalar_tensor_tensor(m[:], ti[:], 1.0, xc[:], ALU.add, ALU.mult).then_inc(m_done, 1)
                    dve.wait_ge(rt_done, i * 2 + d + 1)
                    dve.wait_ge(m_done, i * 2 + d + 1)
                    dve.tensor_tensor(b[:], rt[:], m[:], ALU.mult).then_inc(b_done, 1)
                    dve.wait_ge(b_done, i * 2 + d + 1)
                    for b0, n in SEG:
                        sl = slice(b0, b0 + n) if d == 0 else slice(b0 + n - 1, b0 - 1 if b0 else None, -1)
                        last = dve.tensor_tensor_scan(h[:, d, sl], a[:, sl], b[:, sl], 0.0, ALU.mult, ALU.add)
                    last.then_inc(scan_done, 1)
                dve.wait_ge(gelu_th, i + 1)
                dve.wait_ge(scan_done, i * 2 + 2)
                dve.scalar_tensor_tensor(b[:], tg[:], 1.0, gt[:], ALU.add, ALU.mult).then_inc(gg_done, 1)
                dve.wait_ge(gg_done, i + 1)
                dve.wait_ge(sum_done, i + 1)
                dve.scalar_tensor_tensor(gi[:], m[:], 0.25, b[:], ALU.mult, ALU.mult).then_inc(out_done, 1)
                c.end()


NA_ROWS = [(b, r, n // GRID) for b, n in SEG for r in range(n // GRID)]
NA_TILES = [e for e in range(T // GRID) if e not in (SEG[0][1] // GRID - 1, T // GRID - 1)]
KEYS = NA_KH * GRID
NH_PAIR = BW // P


def na_bias(nc, rpb, pad, bias_d):
    with Space(nc, "nb") as s:
        table_in, padded, skewed = s.sem("table_in"), s.sem("padded"), s.sem("skewed")
        zeroed, io, chain, stored = s.sem("zeroed"), s.sem("io"), s.sem("chain"), s.sem("stored")
        copied = s.sem("copied")
        ready, flip_made, flipped = s.sem("ready"), s.sem("flip_made"), s.sem("flipped")
        rev = s.sb("rev", [NH_PAIR, NDR * GRID])
        flip = s.sb("flip", [P])
        ps = s.ps("ps", [NH_PAIR * 2, TB])
        rows = s.sb("rows", [P])
        raw = s.sb("raw", [NH_PAIR, NDR, GRID])
        qc, kc, w0, mask, neg = (s.sb(x, [GRID]) for x in ("qc", "kc", "w0", "mask", "neg"))
        block = s.block()
        nrow = 8 * NDR
        first = GRID - 1 - (NA_KW - 1)

        @block.gpsimd
        def _(pool):
            pool.memset(rows[:], 0.0).then_inc(zeroed, 1)
            pool.memset(flip[:], 0.0).then_inc(flip_made, 1)
            pool.wait_ge(flip_made, 1)
            for half in range(2):
                r = slice(64 * half, 64 * half + 64)
                pool.affine_select(out=flip[r, r], in_=flip[r, r], compare_op=ALU.not_equal, fill=1.0, base=1 - GRID,
                                   pattern=[[1, GRID]], channel_multiplier=1).then_inc(flip_made, 1)
            pool.wait_ge(zeroed, 1)
            for half in range(2):
                pool.iota(qc[64 * half:64 * half + 64, :], pattern=[[0, GRID]], base=0, channel_multiplier=1,
                          allow_small_or_imprecise_dtypes=True).then_inc(io, 1)
            pool.wait_ge(io, 2)
            pool.iota(kc[:], pattern=[[1, GRID]], base=0, channel_multiplier=0, allow_small_or_imprecise_dtypes=True).then_inc(io, 1)

        @block.sync
        def _(sp):
            sp.wait_ge(zeroed, 1)
            sp.dma_start(rows[0:nrow, first:first + NDC], rpb.rearrange("h r c -> (h r) c")).then_inc(table_in, 16)
            sp.wait_ge(table_in, 16)
            sp.dma_start(pad, rows[0:nrow, :]).then_inc(padded, 16)
            sp.wait_ge(padded, 16)
            for h in range(8):
                src = bass.AP(tensor=pad.tensor, offset=h * NDR * P, ap=[[1, GRID], [P, NDR], [1, GRID]])
                sp.dma_start(rev[64 * (h % 2):64 * (h % 2) + 64, h // 2], src).then_inc(skewed, 16)
            sp.wait_ge(ready, NH_PAIR)
            sp.dma_start(bias_d.rearrange("a p r c -> p a r c"), raw[:]).then_inc(stored, 16)
            sp.wait_ge(stored, 16)

        @block.tensor
        def _(pe):
            pe.wait_ge(flip_made, 3)
            pe.wait_ge(skewed, 8 * 16)
            half = NDR * GRID // 2
            for a in range(NH_PAIR):
                for z in range(2):
                    pe.matmul(ps[:, 2 * a + z, 0:half], flip[:], rev[:, a, z * half:(z + 1) * half], start=True,
                              stop=True).then_inc(flipped, 1)

        @block.scalar
        def _(act):
            half = NDR * GRID // 2
            for a in range(NH_PAIR):
                act.wait_ge(flipped, 2 * a + 2)
                act.copy(raw[:, a].rearrange("p r c -> p (r c)").rearrange("p (z n) -> p z n", z=2),
                         ps[:, 2 * a:2 * a + 2, 0:half]).then_inc(copied, 1)

        @block.vector
        def _(dve):
            c = Chain(dve, chain, 0, 6)
            dve.wait_ge(io, 3)
            c.link(dve.tensor_scalar(w0[:], qc[:], float(-(NA_KW // 2)), 0.0, ALU.add, ALU.max))
            c.link(dve.tensor_scalar(w0[:], w0[:], float(GRID - NA_KW), None, ALU.min))
            c.link(dve.tensor_tensor(w0[:], kc[:], w0[:], ALU.subtract))
            c.link(dve.tensor_scalar(mask[:], w0[:], 0.0, None, ALU.is_ge))
            c.link(dve.scalar_tensor_tensor(mask[:], w0[:], float(NA_KW), mask[:], ALU.is_lt, ALU.mult))
            c.link(dve.tensor_scalar(neg[:], mask[:], -1.0, -NEG, ALU.add, ALU.mult))
            for a in range(NH_PAIR):
                dve.wait_ge(copied, a + 1)
                wide = [P, NDR, GRID]
                dve.tensor_tensor(raw[:, a], raw[:, a], mask[:].unsqueeze(1).to_broadcast(wide), ALU.mult).then_inc(chain, 1)
                dve.wait_ge(chain, 6 + a + 1)
                dve.tensor_tensor(raw[:, a], raw[:, a], neg[:].unsqueeze(1).to_broadcast(wide), ALU.add).then_inc(ready, 1)
            c.end()


def attention(nc, proj, bias_d, o_t, ident):
    NR = len(NA_ROWS)
    NS = 3
    with Space(nc, "na") as s:
        q_in, k_in, v_in, b_in = (s.sem(x) for x in ("q_in", "k_in", "v_in", "b_in"))
        seen = s.sem("seen")
        free, q_done, v_turned, v_done = (s.sem(x) for x in ("free", "q_done", "v_turned", "v_done"))
        scored, biased, exped, recip = (s.sem(x) for x in ("scored", "biased", "exped", "recip"))
        normed, turned, copied, mixed, out_done, stored, zeroed = (
            s.sem(x) for x in ("normed", "turned", "copied", "mixed", "out_done", "stored", "zeroed"))
        qt, kt, vt = s.sb("qt", [T]), s.sb("kt", [T]), s.sb("vt", [T])
        bias = s.sb("bias", [NDR * GRID])
        qbd = s.sb("qbd", [NR, P])
        vtm = s.sb("vtm", [T // GRID, P])
        sc, pr, pn, pt = s.sb("sc", [NS, KEYS]), s.sb("pr", [NS, KEYS]), s.sb("pn", [NS, KEYS]), s.sb("pt", [NS, KEYS])
        nmax, rsum, rinv = s.sb("nmax", [NR]), s.sb("rsum", [NR]), s.sb("rinv", [NR])
        ot = s.sb("ot", [T])
        ps_s = s.ps("ps_s", [3, KEYS])
        ps_t = s.ps("ps_t", [3, KEYS])
        ps_o = s.ps("ps_o", [2, 4, P])
        NVG = (len(NA_TILES) + 3) // 4
        block = s.block()

        @block.sync
        def _(sp):
            with sp.Fori(0, NH_PAIR) as i:
                sp.wait_ge(free, i + 1)
                for buf, sem, t0 in ((qt, q_in, 0), (kt, k_in, NH_PAIR), (vt, v_in, 2 * NH_PAIR)):
                    sp.dma_start(buf[:], proj[dsl(i + t0)].rearrange("a p n -> p (a n)")).then_inc(sem, 16)
                sp.dma_start(bias[:], bias_d[dsl(i)].rearrange("a p r c -> p (a r c)")).then_inc(b_in, 16)
                sp.wait_ge(out_done, i * 12 + 12)
                sp.dma_start(o_t[dsl(i)].rearrange("a p n -> p (a n)"), ot[:]).then_inc(stored, 16)
                sp.wait_ge(stored, i * 16 + 16)
                sp.sem_inc(free, 1)

        @block.gpsimd
        def _(pool):
            pool.memset(qbd[:], 0.0).then_inc(zeroed, 1)
            pool.sem_inc(free, 1)

        @block.tensor
        def _(pe):
            with pe.Fori(0, NH_PAIR) as i:
                pe.wait_ge(v_in, i * 16 + 16)
                for g in range(NVG):
                    if g >= 3:
                        pe.wait_ge(v_done, i * NVG + g - 2)
                    for j, e in enumerate(NA_TILES[4 * g:4 * g + 4]):
                        last = pe.transpose(ps_t[:, g % 3, j * P:(j + 1) * P], vt[:, e * GRID:e * GRID + P], ident[:])
                    last.then_inc(v_turned, 1)
                pe.wait_ge(q_done, i * 2 + 2)
                pe.wait_ge(k_in, i * 16 + 16)
                for n in range(NR + 3):
                    if n < NR:
                        if n >= 3:
                            pe.wait_ge(biased, i * NR + n - 2)
                        b, r, rows = NA_ROWS[n]
                        k0 = b + min(max(r - NA_KH // 2, 0), rows - NA_KH) * GRID
                        pe.matmul(ps_s[:, n % 3], qbd[:, n], kt[:, k0:k0 + KEYS], start=True, stop=True).then_inc(scored, 1)
                    if 2 <= n < NR + 2:
                        m = n - 2
                        pe.wait_ge(normed, i * NR + m + 1)
                        if m >= 3:
                            pe.wait_ge(copied, i * NR + m - 2)
                        else:
                            pe.wait_ge(v_done, i * NVG + NVG)
                        for j in range(4):
                            last = pe.transpose(ps_t[:, m % 3, j * P:(j + 1) * P], pn[:, m % NS, j * P:(j + 1) * P], ident[:])
                        last.then_inc(turned, 1)
                    if n >= 3:
                        m = n - 3
                        pe.wait_ge(copied, i * NR + m + 1)
                        if m % 4 == 0 and m >= 8:
                            pe.wait_ge(out_done, i * 12 + (m // 4 - 2) * 2 + 2)
                        b, r, rows = NA_ROWS[m]
                        e0 = b // GRID + min(max(r - NA_KH // 2, 0), rows - NA_KH)
                        for j in range(4):
                            last = pe.matmul(ps_o[:, m // 4 % 2, m % 4], vtm[:, e0 + 2 * j], pt[:, m % NS, j * P:(j + 1) * P],
                                             start=(j == 0), stop=(j == 3))
                        last.then_inc(mixed, 1)

        @block.vector
        def _(dve):
            dve.wait_ge(zeroed, 1)
            with dve.Fori(0, NH_PAIR) as i:
                dve.wait_ge(q_in, i * 16 + 16)
                for h in range(2):
                    r = slice(64 * h, 64 * h + 64)
                    dve.tensor_scalar(qbd[r, :, r], qt[r, :].rearrange("p (n c) -> p n c", c=GRID), NA_HD ** -0.5, None,
                                      ALU.mult).then_inc(q_done, 1)
                dve.wait_ge(b_in, i * 16 + 16)
                for n in range(NR + 3):
                    if n < NR:
                        dve.wait_ge(scored, i * NR + n + 1)
                        if n >= NS:
                            dve.wait_ge(exped, i * NR + n - NS + 1)
                        b, r, rows = NA_ROWS[n]
                        o = min(max(r - NA_KH // 2, 0), rows - NA_KH) - r + NA_KH - 1
                        dve.sem_inc(seen, 1)
                        dve.tensor_tensor_reduce(sc[:, n % NS], ps_s[:, n % 3], bias[:, o * GRID:o * GRID + KEYS], -1.0, 1e38,
                                                 ALU.add, ALU.min, nmax[:, n:n + 1]).then_inc(biased, 1)
                    if 1 <= n < NR + 1:
                        m = n - 1
                        dve.wait_ge(exped, i * NR + m + 1)
                        dve.reciprocal(rinv[:, m:m + 1], rsum[:, m:m + 1]).then_inc(recip, 1)
                        dve.wait_ge(recip, i * NR + m + 1)
                        if m >= NS:
                            dve.wait_ge(turned, i * NR + m - NS + 1)
                        dve.tensor_scalar(pn[:, m % NS], pr[:, m % NS], rinv[:, m:m + 1], None, ALU.mult).then_inc(normed, 1)
                    if n >= 3 and (n - 3) % 4 == 3:
                        g = (n - 3) // 4
                        dve.wait_ge(mixed, i * NR + 4 * g + 4)
                        for h in range(2):
                            r = slice(64 * h, 64 * h + 64)
                            dve.tensor_copy(ot[r, 4 * g * GRID:4 * (g + 1) * GRID].rearrange("p (a c) -> p a c", c=GRID),
                                            ps_o[r, g % 2, :, r]).then_inc(out_done, 1)

        @block.scalar
        def _(act):
            with act.Fori(0, NH_PAIR) as i:
                for g in range(NVG):
                    es = NA_TILES[4 * g:4 * g + 4]
                    act.wait_ge(v_turned, i * NVG + g + 1)
                    runs = [(0, len(es))] if es[-1] - es[0] == len(es) - 1 else None
                    if runs is None:
                        cut = next(j for j in range(1, len(es)) if es[j] != es[j - 1] + 1)
                        runs = [(0, cut), (cut, len(es))]
                    for a, z in runs:
                        last = act.copy(vtm[:, es[a]:es[z - 1] + 1], ps_t[:, g % 3, a * P:z * P].rearrange("p (a n) -> p a n", n=P))
                    last.then_inc(v_done, 1)
                for n in range(NR + 3):
                    if n < NR:
                        act.wait_ge(biased, i * NR + n + 1)
                        if n >= NS:
                            act.wait_ge(normed, i * NR + n - NS + 1)
                        act.activation(pr[:, n % NS], sc[:, n % NS], ACT.Exp, bias=nmax[:, n:n + 1], scale=-1.0,
                                       accum_out=rsum[:, n:n + 1]).then_inc(exped, 1)
                    if n >= 3:
                        m = n - 3
                        act.wait_ge(turned, i * NR + m + 1)
                        if m >= NS:
                            act.wait_ge(mixed, i * NR + m - NS + 1)
                        act.copy(pt[:, m % NS], ps_t[:, m % 3]).then_inc(copied, 1)


def delta_prep(nc, proj, g_rows, cols, a_log, dt_bias, ident):
    R = 2 * HEADS
    with Space(nc, "dp") as s:
        b_in, a_in, prm_in, stored = (s.sem(x) for x in ("b_in", "a_in", "prm_in", "stored"))
        chain, achain, turned, done = (s.sem(x) for x in ("chain", "achain", "turned", "done"))
        br, ar, e, t1, z, z2 = (s.sb(x, [T]) for x in ("br", "ar", "e", "t1", "z", "z2"))
        gf, gb, keep = s.sb("gf", [T]), s.sb("gb", [T]), s.sb("keep", [T])
        al, dt, ea = s.sb("al", [1]), s.sb("dt", [1]), s.sb("ea", [1])
        ps = s.ps("ps", [3, NT, R])
        block = s.block()
        abs_in, exp_done, beta_in, sums = (s.sem(x) for x in ("abs_in", "exp_done", "beta_in", "sums"))

        @block.sync
        def _(sp):
            sp.dma_start(al[0:R, :], a_log.rearrange("d (h a) -> (d h) a", a=1)).then_inc(prm_in, 16)
            sp.dma_start(dt[0:R, :], dt_bias.rearrange("d (h a) -> (d h) a", a=1)).then_inc(prm_in, 16)
            sp.dma_start(ar[0:R, :], proj[TILE_BA, R:2 * R, :]).then_inc(a_in, 16)
            sp.dma_start(br[0:R, :], proj[TILE_BA, 0:R, :]).then_inc(b_in, 16)
            sp.wait_ge(sums, 2)
            sp.dma_start(g_rows[0:R, :], gf[0:R, :]).then_inc(stored, 16)
            sp.dma_start(g_rows[R:2 * R, :], gb[0:R, :]).then_inc(stored, 16)
            sp.wait_ge(stored, 32)

        @block.scalar
        def _(act):
            act.wait_ge(prm_in, 32)
            act.activation(ea[0:R, :], al[0:R, :], ACT.Exp).then_inc(achain, 1)
            act.wait_ge(b_in, 16)
            act.activation(br[0:R, :], br[0:R, :], ACT.Tanh, scale=0.5).then_inc(beta_in, 1)
            act.wait_ge(abs_in, 1)
            act.activation(e[0:R, :], t1[0:R, :], ACT.Exp, scale=-1.0).then_inc(exp_done, 1)

        @block.vector
        def _(dve):
            c = Chain(dve, chain, 0, 10 + LOG1P_STEPS)
            r = slice(0, R)
            c.add(dve.memset(keep[r, :], 1.0))
            dve.wait_ge(prm_in, 32)
            dve.wait_ge(a_in, 16)
            c.link(dve.tensor_scalar(ar[r, :], ar[r, :], dt[r, :], None, ALU.add))
            c.add(dve.memset(keep[r, :].rearrange("p (t n) -> p t n", n=P)[:, :, 0:1], 0.0))
            c.link(dve.scalar_tensor_tensor(t1[r, :], ar[r, :], -1.0, ar[r, :], ALU.mult, ALU.max))
            dve.sem_inc(abs_in, 1)
            dve.wait_ge(exp_done, 1)
            log1p_steps(dve, c, e[r, :], z[r, :], z2[r, :], t1[r, :])
            c.link(dve.scalar_tensor_tensor(t1[r, :], ar[r, :], 0.0, t1[r, :], ALU.max, ALU.add))
            dve.wait_ge(achain, 1)
            c.link(dve.tensor_scalar(t1[r, :], t1[r, :], ea[r, :], -1.0, ALU.mult, ALU.mult))
            c.add(dve.tensor_tensor_scan(gf[r, :], keep[r, :], t1[r, :], 0.0, ALU.mult, ALU.add))
            c.add(dve.tensor_tensor_scan(gb[r, ::-1], keep[r, :], t1[r, ::-1], 0.0, ALU.mult, ALU.add))
            dve.wait_ge(beta_in, 1)
            c.link(dve.tensor_scalar(br[r, :], br[r, :], 1.0, 0.5, ALU.add, ALU.mult))
            dve.sem_inc(sums, 2)
            dve.wait_ge(turned, 1)
            for kind, (src, o) in enumerate(((0, 0), (1, HEADS), (2, 0), (2, HEADS))):
                c2 = dve.tensor_copy(cols[:, :, kind, :], ps[:, src, :, o:o + HEADS].rearrange("p t h -> p h t"))
            c.link(c2)
            c.end()

        @block.tensor
        def _(pe):
            pe.wait_ge(sums, 2)
            for n, src in enumerate((gf, gb, br)):
                for t in range(NT):
                    last = pe.transpose(ps[:, n, t], src[0:R, t * P:(t + 1) * P], ident[0:R, 0:R])
            last.then_inc(turned, 1)




def delta_masks(nc, neg_strict, incl, join):
    with Space(nc, "dm") as s:
        io, conv, chain, step = s.sem("io"), s.sem("conv"), s.sem("chain"), s.sem("step")
        I32 = mybir.dt.int32
        pi, fi = s.sb("pi", [P], I32), s.sb("fi", [P], I32)
        pf, ff, pb, fb, a, b = (s.sb(x, [P]) for x in ("pf", "ff", "pb", "fb", "a", "b"))
        pm, fm = s.sb("pm", [P], I32), s.sb("fm", [P], I32)
        block = s.block()

        @block.gpsimd
        def _(pool):
            pool.iota(pi[:], pattern=[[0, P]], base=0, channel_multiplier=1).then_inc(io, 1)
            pool.iota(fi[:], pattern=[[1, P]], base=0, channel_multiplier=0).then_inc(io, 1)

        @block.vector
        def _(dve):
            dve.wait_ge(io, 2)
            c = Chain(dve, chain, 0, 0)
            c.per = 10 ** 6
            c.link(dve.tensor_copy(pf[:], pi[:]))
            c.link(dve.tensor_copy(ff[:], fi[:]))
            c.add(dve.tensor_tensor(a[:], pf[:], ff[:], ALU.is_gt))
            c.link(dve.tensor_tensor(b[:], pf[:], ff[:], ALU.is_lt))
            c.add(dve.tensor_scalar(neg_strict[:, 0], a[:], -1.0, None, ALU.mult))
            c.add(dve.tensor_scalar(neg_strict[:, 1], b[:], -1.0, None, ALU.mult))
            c.add(dve.tensor_tensor(incl[:, 0], ff[:], pf[:], ALU.is_ge))
            c.add(dve.tensor_tensor(incl[:, 1], pf[:], ff[:], ALU.is_ge))
            for v in range(LEVELS):
                for d, (odd, even) in enumerate(((fi, pi), (pi, fi))):
                    c.link(dve.tensor_scalar(pm[:], pi[:], v + 1, None, ALU.arith_shift_right))
                    c.link(dve.tensor_scalar(fm[:], fi[:], v + 1, None, ALU.arith_shift_right))
                    c.link(dve.tensor_copy(pb[:], pm[:]))
                    c.link(dve.tensor_copy(fb[:], fm[:]))
                    c.link(dve.tensor_tensor(a[:], pb[:], fb[:], ALU.is_equal))
                    c.link(dve.tensor_scalar(pm[:], odd[:], v, 1, ALU.arith_shift_right, ALU.bitwise_and))
                    c.link(dve.tensor_scalar(fm[:], even[:], v, 1, ALU.arith_shift_right, ALU.bitwise_and))
                    c.link(dve.tensor_copy(pb[:], pm[:]))
                    c.link(dve.tensor_copy(fb[:], fm[:]))
                    c.link(dve.tensor_tensor(b[:], pb[:], fb[:], ALU.is_gt))
                    c.link(dve.tensor_tensor(join[:, v, d], a[:], b[:], ALU.mult))


DCHAINS = [(d, g) for g in range(len(SEG)) for d in range(2)]


def deltanet(nc, proj, g_rows, cols, masks, o_t, conv_w, norm_w, ident, ones):
    neg_strict, incl, join = masks
    UN = [(tg, d) for tg in range(NTB) for d in range(2)]
    with Space(nc, "dn") as s:
        names = ("qkv_in", "z_in", "g_in", "prm_in", "free", "stored", "out_done", "zeroed", "chain", "achain",
                 "conv", "tanh", "silu", "sq", "ssum", "rooted", "rs", "unit", "kt_mm", "kt_ev", "cols_in", "cexp",
                 "cols_out", "eg", "qd", "gram", "ediff", "dexp", "dmask", "amat", "u0", "s_mm", "s_ev", "u_mm", "u_ev",
                 "ks", "r", "new_mm", "new_ev", "o_mm", "o_ev", "st_mm", "st_ev", "osum", "osq", "oss", "orr", "oroot",
                 "zt", "kd", "bv", "at_ev", "s0", "seen")
        S = {x: s.sem(x) for x in names}
        qkv = s.sb("qkv", [3, PADW])
        y = s.sb("y", [3, T])
        th = s.sb("th", [T])
        gbc = s.sb("gbc", [2, T])
        qd = s.sb("qd", [2, T])
        kd = s.sb("kd", [2, NT, P])
        bv = s.sb("bv", [2, NT, P])
        am = s.sb("am", [2 * NTB, 4, P])
        at = s.sb("at", [2 * NTB, 4, P])
        un = s.sb("un", [2 * NTB, 4, P])
        tn = s.sb("tn", [2 * NTB, 4, P])
        qk = s.sb("qk", [2 * NTB, 4, P])
        dd = s.sb("dd", [4, 4, P])
        cw = s.sb("cw", [3, CW])
        nw = s.sb("nw", [1])
        col = s.sb("col", [4, NT])
        cx = s.sb("cx", [6, NT])
        st = s.sb("st", [4, P])
        rb, nb = s.sb("rb", [4, P]), s.sb("nb", [4, P])
        ps = s.ps("ps", [8, 4, P])
        flat = lambda a: a.rearrange("p a n -> p (a n)")
        three = lambda a: a.rearrange("p (a n) -> p a n", a=NTB)
        four = lambda a: a.rearrange("p (a n) -> p a n", n=P)
        oc = [qkv[:, 0, 0:T], qkv[:, 1, 0:T]]
        zt = qkv[:, 2, 0:T]
        ss_r = th
        sbuf_s = [dd[:, j] for j in range(4)]
        block = s.block()
        EGL = {0: 4, 1: 5}

        def glast(d):
            g4 = gbc[:, d].rearrange("p (t n) -> p t n", n=P)
            return g4[:, :, P - 1] if d == 0 else g4[:, :, 0]

        @block.sync
        def _(sp):
            sp.wait_ge(S["zeroed"], 9)
            sp.dma_start(nw[:], norm_w.rearrange("(p a) -> p a", a=1)).then_inc(S["prm_in"], 16)
            sp.wait_ge(S["prm_in"], 16)
            with sp.Fori(0, HEADS) as i:
                sp.wait_ge(S["free"], i + 1)
                for n in range(3):
                    conv_load(sp, qkv[:, n], flat(proj[dsl(i + (TILE_DN + n * HEADS))].rearrange("a p n -> p a n")), S["qkv_in"])
                    sp.dma_start(cw[:, n], conv_w[:, bass.ds(i * P + n * BW, P)].rearrange("j p -> p j"),
                                 allow_slow_non_contiguous=True).then_inc(S["qkv_in"], 16)
                for d in range(2):
                    row = g_rows[bass.ds(i + d * (2 * HEADS + HEADS), 1), :]
                    sp.dma_start(gbc[:, d], row.to_broadcast([P, T])).then_inc(S["g_in"], 16)
                sp.wait_ge(S["conv"], i * 3 + 3)
                sp.dma_start(zt, flat(proj[dsl(i + TILE_Z)].rearrange("a p n -> p a n"))).then_inc(S["z_in"], 16)
                sp.wait_ge(S["out_done"], i + 1)
                sp.dma_start(flat(o_t[dsl(i + HEADS)].rearrange("a p n -> p a n")), oc[0]).then_inc(S["stored"], 16)
                sp.wait_ge(S["stored"], i * 16 + 16)
                sp.sem_inc(S["free"], 1)

        @block.gpsimd
        def _(pool):
            for n in range(3):
                conv_zero(pool, qkv[:, n], S["zeroed"])
            pool.sem_inc(S["free"], 1)
            with pool.Fori(0, HEADS) as i:
                for n, (tg, d) in enumerate(UN):
                    pool.wait_ge(S["dexp"], i * 12 + 2 * n + 2)
                    b = n % 2
                    pool.tensor_tensor(dd[:, 2 * b], dd[:, 2 * b], neg_strict[:, d].unsqueeze(1).to_broadcast([P, 4, P]),
                                       ALU.mult).then_inc(S["dmask"], 1)
                    pool.tensor_tensor(dd[:, 2 * b + 1], dd[:, 2 * b + 1], incl[:, d].unsqueeze(1).to_broadcast([P, 4, P]),
                                       ALU.mult).then_inc(S["dmask"], 1)
                    pool.tensor_copy(un[:, n], ident[:].unsqueeze(1).to_broadcast([P, 4, P])).then_inc(S["u0"], 1)
                    pool.tensor_copy(tn[:, n], ident[:].unsqueeze(1).to_broadcast([P, 4, P])).then_inc(S["u0"], 1)

        @block.scalar
        def _(act):
            with act.Fori(0, HEADS) as i:
                for n in range(3):
                    act.wait_ge(S["conv"], i * 3 + n + 1)
                    if n:
                        act.wait_ge(S["silu"], i * 3 + n)
                    act.activation(th[:], y[:, n], ACT.Tanh, scale=0.5).then_inc(S["tanh"], 1)
                for n in range(2):
                    if n == 0:
                        act.wait_ge(S["silu"], i * 3 + 3)
                    else:
                        act.wait_ge(S["unit"], i * 2 + 1)
                    act.activation(th[:], y[:, n], ACT.Square, scale=0.5).then_inc(S["sq"], 1)
                    act.wait_ge(S["rs"], i * 2 + n + 1)
                    act.activation(qd[:, 0], qd[:, 1], ACT.Sqrt).then_inc(S["rooted"], 1)
                act.wait_ge(S["cols_in"], i + 1)
                act.activation(cx[:].rearrange("p a t -> p (a t)"), cx[:].rearrange("p a t -> p (a t)"), ACT.Exp).then_inc(S["cexp"], 1)
                for d in range(2):
                    act.wait_ge(S["unit"], i * 2 + 2)
                    act.activation(qd[:, d], gbc[:, d], ACT.Exp).then_inc(S["eg"], 1)
                for n in range(2 * NTB):
                    act.wait_ge(S["ediff"], i * 12 + 2 * n + 2)
                    b = n % 2
                    act.activation(flat(dd[:, 2 * b]), flat(dd[:, 2 * b]), ACT.Exp, scale=-1.0).then_inc(S["dexp"], 1)
                    act.activation(flat(dd[:, 2 * b + 1]), flat(dd[:, 2 * b + 1]), ACT.Exp).then_inc(S["dexp"], 1)
                for n in range(2 * NTB):
                    act.wait_ge(S["u_mm"], i * LEVELS * 6 + n + 1)
                    act.copy(at[:, n], ps[:, 4 + 2 * (n % 2)]).then_inc(S["at_ev"], 1)
                for v in range(LEVELS - 1):
                    for n in range(2 * NTB):
                        k = v * 2 * NTB + n
                        act.wait_ge(S["s_mm"], i * (LEVELS - 1) * 6 + k + 1)
                        if k == 0:
                            act.wait_ge(S["amat"], i * 12 + 12)
                        if k >= 4:
                            act.wait_ge(S["u_mm"], i * LEVELS * 6 + 6 + k - 3)
                        act.copy(sbuf_s[k % 4], ps[:, k % 4]).then_inc(S["s_ev"], 1)
                k = 0
                for step in range(8):
                    for j, (d, g) in enumerate(DCHAINS):
                        nt = SEG[g][1] // P
                        if step < nt:
                            act.wait_ge(S["new_mm"], i * 24 + k + 1)
                            if step:
                                act.wait_ge(S["st_mm"], i * 24 + K_OF[(step - 1, j)] + 1)
                            act.copy(nb[:, j], ps[:, 4 + j, 0]).then_inc(S["new_ev"], 1)
                            k += 1
                    for j, (d, g) in enumerate(DCHAINS):
                        nt = SEG[g][1] // P
                        if step < nt:
                            t = SEG[g][0] // P + (step if d == 0 else nt - 1 - step)
                            act.wait_ge(S["o_mm"], i * 24 + K_OF[(step, j)] + 1)
                            act.copy(oc[d][:, t * P:(t + 1) * P], ps[:, 4 + j, 1]).then_inc(S["o_ev"], 1)
                act.wait_ge(S["osum"], i + 1)
                act.activation(th[:], oc[0], ACT.Square).then_inc(S["osq"], 1)
                act.wait_ge(S["orr"], i + 1)
                act.activation(y[:, 1], y[:, 0], ACT.Sqrt).then_inc(S["oroot"], 1)
                act.wait_ge(S["z_in"], i * 16 + 16)
                act.activation(y[:, 2], zt, ACT.Tanh, scale=0.5).then_inc(S["zt"], 1)

        @block.tensor
        def _(pe):
            with pe.Fori(0, HEADS) as i:
                for n in range(2):
                    pe.wait_ge(S["sq"], i * 2 + n + 1)
                    for tb in range(NTB):
                        last = pe.matmul(flat(ps[:, tb]), ones[:], th[:, tb * TB:(tb + 1) * TB], start=True, stop=True)
                    last.then_inc(S["ssum"], 1)
                pe.wait_ge(S["unit"], i * 2 + 2)
                for n in range(2 * NTB):
                    if n >= 4:
                        pe.wait_ge(S["kt_ev"], i * 12 + 2 * (n - 4) + 2)
                    for j in range(4):
                        t = 4 * (n // 2) + j
                        last = pe.transpose(ps[:, 4 + n % 4, j], y[:, 1 + n % 2, t * P:(t + 1) * P], ident[:])
                    last.then_inc(S["kt_mm"], 1)
                for tg in range(NTB):
                    if tg:
                        pe.wait_ge(S["amat"], i * 12 + 4 * tg)
                    for n, mov in enumerate((1, 0)):
                        for j in range(4):
                            sl = slice((4 * tg + j) * P, (4 * tg + j + 1) * P)
                            last = pe.matmul(ps[:, n, j], y[:, 1, sl], y[:, mov, sl], start=True, stop=True)
                    last.then_inc(S["gram"], 1)
                for n in range(2 * NTB):
                    pe.wait_ge(S["amat"], i * 12 + 12)
                    pe.wait_ge(S["kt_ev"], i * 12 + 12)
                    if n >= 2:
                        pe.wait_ge(S["u_ev"], i * LEVELS * 6 + n - 1)
                        pe.wait_ge(S["at_ev"], i * 6 + n - 1)
                    for j in range(4):
                        last = pe.transpose(ps[:, 4 + 2 * (n % 2), j], am[:, n, j], ident[:])
                    last.then_inc(S["u_mm"], 1)
                pe.wait_ge(S["at_ev"], i * 6 + 6)
                for v in range(1, LEVELS):
                    for n in range(2 * NTB + 1):
                        if n < 2 * NTB:
                            k = (v - 1) * 6 + n
                            pe.wait_ge(S["u_ev"], i * LEVELS * 6 + k + 1)
                            if k >= 4:
                                pe.wait_ge(S["s_ev"], i * (LEVELS - 1) * 6 + k - 3)
                            for j in range(4):
                                last = pe.matmul(ps[:, k % 4, j], at[:, n, j], tn[:, n, j], start=True, stop=True)
                            last.then_inc(S["s_mm"], 1)
                        if n:
                            m = n - 1
                            k = (v - 1) * 6 + m
                            pe.wait_ge(S["s_ev"], i * (LEVELS - 1) * 6 + k + 1)
                            pe.wait_ge(S["u_ev"], i * LEVELS * 6 + 6 + k - 1)
                            for j in range(4):
                                if v < LEVELS - 1:
                                    pe.matmul(ps[:, 4 + 2 * (m % 2), j], un[:, m, j], sbuf_s[k % 4][:, j], start=True, stop=True)
                                last = pe.matmul(ps[:, 5 + 2 * (m % 2), j], sbuf_s[k % 4][:, j], un[:, m, j], start=True, stop=True)
                            last.then_inc(S["u_mm"], 1)
                pe.wait_ge(S["u_ev"], i * LEVELS * 6 + LEVELS * 6)
                pe.wait_ge(S["s_ev"], i * (LEVELS - 1) * 6 + (LEVELS - 1) * 6)
                pe.wait_ge(S["s0"], i + 1)
                pe.wait_ge(S["qd"], i * 2 + 2)
                for step in range(8):
                    live = [(j, d, SEG[g][0] // P + (step if d == 0 else SEG[g][1] // P - 1 - step))
                            for j, (d, g) in enumerate(DCHAINS) if step < SEG[g][1] // P]
                    for j, d, t in live:
                        if step:
                            pe.wait_ge(S["st_ev"], i * 24 + K_OF[(step - 1, j)] + 1)
                        pe.matmul(ps[:, j, 0], y[:, 1, t * P:(t + 1) * P], st[:, j], start=True, stop=True).then_inc(S["ks"], 1)
                    for j, d, t in live:
                        pe.wait_ge(S["r"], i * 24 + K_OF[(step, j)] + 1)
                        if step:
                            pe.wait_ge(S["o_ev"], i * 24 + K_OF[(step - 1, j)] + 1)
                        pe.matmul(ps[:, 4 + j, 0], un[:, 2 * (t // 4) + d, t % 4], rb[:, j], start=True, stop=True).then_inc(S["new_mm"], 1)
                    for j, d, t in live:
                        pe.wait_ge(S["new_ev"], i * 24 + K_OF[(step, j)] + 1)
                        pe.matmul(ps[:, j, 1], kd[:, d, t], nb[:, j], start=True, stop=True).then_inc(S["st_mm"], 1)
                        pe.matmul(ps[:, 4 + j, 1], st[:, j], qd[:, d, t * P:(t + 1) * P], start=True, stop=False)
                        pe.matmul(ps[:, 4 + j, 1], nb[:, j], qk[:, 2 * (t // 4) + d, t % 4], start=False, stop=True).then_inc(S["o_mm"], 1)
                pe.wait_ge(S["osq"], i + 1)
                for tb in range(NTB):
                    last = pe.matmul(flat(ps[:, tb]), ones[:], th[:, tb * TB:(tb + 1) * TB], start=True, stop=True)
                last.then_inc(S["oss"], 1)

        @block.vector
        def _(dve):
            with dve.Fori(0, HEADS) as i:
                c = Chain(dve, S["chain"], i, K_DN)
                dve.wait_ge(S["qkv_in"], i * 144 + 144)
                for n in range(3):
                    for a, z in ((0, 2), (1026, 1029), (1541, PADW)):
                        c.add(dve.memset(qkv[:, n, a:z], 0.0))
                    c.wait()
                    conv_steps(dve, c, y[:, n], qkv[:, n], cw[:, n])
                    dve.sem_inc(S["conv"], 1)
                for n in range(3):
                    dve.wait_ge(S["tanh"], i * 3 + n + 1)
                    c.link(dve.scalar_tensor_tensor(y[:, n], th[:], 1.0, y[:, n], ALU.add, ALU.mult))
                    if n == 2:
                        c.link(dve.tensor_scalar(y[:, n], y[:, n], 0.5, None, ALU.mult))
                    dve.sem_inc(S["silu"], 1)
                for n in range(2):
                    dve.wait_ge(S["ssum"], i * 2 + n + 1)
                    c.link(dve.tensor_scalar(three(th[:]), ps[:, 0:NTB].rearrange("p a b n -> p a (b n)"), EPS, None, ALU.add))
                    dve.reciprocal(qd[:, 1], th[:]).then_inc(S["rs"], 1)
                    dve.wait_ge(S["rooted"], i * 2 + n + 1)
                    dve.scalar_tensor_tensor(y[:, n], y[:, n], (0.5 * P ** -0.5) if n == 0 else 0.5, qd[:, 0], ALU.mult,
                                             ALU.mult).then_inc(S["unit"], 1)
                c.link(dve.tensor_copy(col[:], cols[:, bass.ds(i, 1)].rearrange("p a k t -> p (a k) t")))
                dve.wait_ge(S["g_in"], i * 32 + 32)
                for d in range(2):
                    c.add(dve.tensor_copy(cx[:, d], col[:, d]))
                    c.add(dve.tensor_tensor(cx[:, 2 + d], glast(d), col[:, d], ALU.subtract))
                    c.add(dve.tensor_copy(cx[:, 4 + d], glast(d)))
                c.wait()
                dve.sem_inc(S["cols_in"], 1)
                dve.wait_ge(S["cexp"], i + 1)
                c.link(dve.scalar_tensor_tensor(cx[:, 0:2], col[:, 2:4], -1.0, cx[:, 0:2], ALU.mult, ALU.mult))
                for n in range(2 * NTB):
                    dve.wait_ge(S["kt_mm"], i * 6 + n + 1)
                    tg = n // 2
                    for d in range(2):
                        fac = cx[:, 2 + d, 4 * tg:4 * tg + 4] if n % 2 == 0 else col[:, 2 + d, 4 * tg:4 * tg + 4]
                        dst = (kd, bv)[n % 2]
                        dve.tensor_tensor(dst[:, d, 4 * tg:4 * tg + 4], ps[:, 4 + n % 4], fac.unsqueeze(2).to_broadcast([P, 4, P]),
                                          ALU.mult).then_inc(S["kt_ev"], 1)
                for d in range(2):
                    dve.wait_ge(S["eg"], i * 2 + d + 1)
                    dve.tensor_tensor(qd[:, d], qd[:, d], y[:, 0], ALU.mult).then_inc(S["qd"], 1)

                def ediff(n):
                    tg, d = UN[n]
                    b = n % 2
                    if n >= 2:
                        dve.wait_ge(S["amat"], i * 12 + 2 * (n - 2) + 2)
                    e = dd[:, 2 * b]
                    c.link(dve.tensor_tensor(e, four(gbc[:, d, tg * TB:(tg + 1) * TB]),
                                             col[:, d, 4 * tg:4 * tg + 4].unsqueeze(2).to_broadcast([P, 4, P]), ALU.subtract))
                    dve.tensor_scalar(dd[:, 2 * b + 1], e, 0.0, None, ALU.min).then_inc(S["ediff"], 1)
                    dve.wait_ge(S["ediff"], i * 12 + 2 * n + 1)
                    dve.tensor_scalar(e, e, 0.0, None, ALU.max).then_inc(S["ediff"], 1)

                def amat(n):
                    tg, d = UN[n]
                    b = n % 2
                    dve.wait_ge(S["dmask"], i * 12 + 2 * n + 2)
                    dve.wait_ge(S["gram"], i * NTB + tg + 1)
                    c.link(dve.tensor_tensor(am[:, n], ps[:, 0], dd[:, 2 * b], ALU.mult))
                    dve.tensor_tensor(am[:, n], am[:, n], col[:, 2 + d, 4 * tg:4 * tg + 4].unsqueeze(2).to_broadcast([P, 4, P]),
                                      ALU.mult).then_inc(S["amat"], 1)
                    dve.tensor_tensor(qk[:, n], ps[:, 1], dd[:, 2 * b + 1], ALU.mult).then_inc(S["amat"], 1)

                ediff(0)
                for n in range(2 * NTB):
                    if n + 1 < 2 * NTB:
                        ediff(n + 1)
                    amat(n)
                dve.wait_ge(S["u0"], i * 12 + 12)
                for v in range(LEVELS):
                    for n in range(2 * NTB):
                        if v == 0:
                            dve.wait_ge(S["at_ev"], i * 6 + n + 1)
                        else:
                            dve.wait_ge(S["u_mm"], i * LEVELS * 6 + v * 6 + n + 1)
                        dve.sem_inc(S["seen"], 1)
                        d, bank = UN[n][1], 4 + 2 * (n % 2)
                        wide = [P, 4, P]
                        if v < LEVELS - 1:
                            dve.copy_predicated(tn[:, n], join[:, v, 1 - d].unsqueeze(1).to_broadcast(wide),
                                                am[:, n] if v == 0 else ps[:, bank])
                        dve.copy_predicated(un[:, n], join[:, v, d].unsqueeze(1).to_broadcast(wide),
                                            at[:, n] if v == 0 else ps[:, bank + 1]).then_inc(S["u_ev"], 1)
                dve.memset(st[:], 0.0).then_inc(S["s0"], 1)
                dve.wait_ge(S["s0"], i + 1)
                for step in range(8):
                    live = [(j, d, SEG[g][0] // P + (step if d == 0 else SEG[g][1] // P - 1 - step))
                            for j, (d, g) in enumerate(DCHAINS) if step < SEG[g][1] // P]
                    for j, d, t in live:
                        dve.wait_ge(S["ks"], i * 24 + K_OF[(step, j)] + 1)
                        if step:
                            dve.wait_ge(S["new_mm"], i * 24 + K_OF[(step - 1, j)] + 1)
                        dve.scalar_tensor_tensor(rb[:, j], ps[:, j, 0], cx[:, d, t:t + 1], bv[:, d, t], ALU.mult, ALU.add).then_inc(S["r"], 1)
                    for j, d, t in live:
                        dve.wait_ge(S["st_mm"], i * 24 + K_OF[(step, j)] + 1)
                        dve.wait_ge(S["o_mm"], i * 24 + K_OF[(step, j)] + 1)
                        dve.scalar_tensor_tensor(st[:, j], st[:, j], cx[:, EGL[d], t:t + 1], ps[:, j, 1], ALU.mult, ALU.add).then_inc(S["st_ev"], 1)
                dve.wait_ge(S["o_ev"], i * 24 + 24)
                dve.tensor_tensor(oc[0], oc[0], oc[1], ALU.add).then_inc(S["osum"], 1)
                dve.wait_ge(S["oss"], i + 1)
                c.link(dve.tensor_scalar(three(th[:]), ps[:, 0:NTB].rearrange("p a b n -> p a (b n)"), 1.0 / P, EPS, ALU.mult, ALU.add))
                dve.reciprocal(y[:, 0], th[:]).then_inc(S["orr"], 1)
                dve.wait_ge(S["oroot"], i + 1)
                c.link(dve.scalar_tensor_tensor(oc[0], oc[0], nw[:], y[:, 1], ALU.mult, ALU.mult))
                dve.wait_ge(S["zt"], i + 1)
                c.link(dve.scalar_tensor_tensor(y[:, 2], y[:, 2], 1.0, zt, ALU.add, ALU.mult))
                dve.scalar_tensor_tensor(oc[0], oc[0], 0.5, y[:, 2], ALU.mult, ALU.mult).then_inc(S["out_done"], 1)
                c.end()


K_OF = {}
for _step in range(8):
    for _j, (_d, _g) in enumerate(DCHAINS):
        if _step < SEG[_g][1] // P:
            K_OF[(_step, _j)] = len(K_OF)
K_DN = 3 * (3 + 2 * CW) + 4 + 2 + 1 + 6 + 1 + 2 * 6 + 3


def merge(nc, proj, o_t, merged, w_br):
    NB = 3
    KB = BW // P
    NU = NB * KD
    with Space(nc, "mg") as s:
        o_hi, o_lo = s.sb("o_hi", [NB * KB, T], F32R), s.sb("o_lo", [NB * KB, T], F32R)
        stage = s.sb("stage", [2, T])
        w_raw = s.sb("w_raw", [2, KB, P])
        w_hi, w_lo = s.sb("w_hi", [2, KB, P], F32R), s.sb("w_lo", [2, KB, P], F32R)
        gate, total = s.sb("gate", [2, T]), s.sb("total", [2, T])
        acc = s.ps("acc", [2, 4, TB])
        o_in = [s.sem(f"o_in{b}") for b in range(2)]
        w_in = [s.sem(f"w_in{b}") for b in range(2)]
        g_in = [s.sem(f"g_in{b}") for b in range(2)]
        stored = [s.sem(f"stored{b}") for b in range(2)]
        (o_hi_done, o_lo_done, hi_done, lo_done, mm_done, th_done, gated, summed) = (
            s.sem(x) for x in ("o_hi_done", "o_lo_done", "hi_done", "lo_done", "mm_done", "th_done", "gated", "summed"))
        g_prod = s.sem("g_prod")
        block = s.block()
        w_t = w_br.rearrange("b (k p) n -> p b k n", p=P)


        def columns(i, n):
            return bass.ds(i * (2 * P) + (n // NB) * P, P)

        def half(i, n):
            return i * 48 + (n // 2) * 16 + 16

        @block.sync
        def _(sp):
            for t in range(NB * KB):
                if t >= 2:
                    sp.wait_ge(o_hi_done, t - 1)
                    sp.wait_ge(o_lo_done, t - 1)
                sp.dma_start(stage[:, t % 2], o_t[t]).then_inc(o_in[t % 2], 16)
            with sp.Fori(0, KD // 2) as i:
                for n in range(2 * NB):
                    sp.wait_ge(hi_done, i * 6 + n + 1)
                    sp.wait_ge(lo_done, i * 6 + n + 1)
                    sp.dma_start(w_raw[:, n % 2], w_t[:, n % NB, :, columns(i, n)]).then_inc(w_in[n % 2], 16)
                    sp.wait_ge(gated, i * 6 + n + 1)
                    sp.dma_start(gate[:, n % 2], proj[bass.ds(i * 2 + (N_MIX + (n % NB) * KD + n // NB), 1)]
                                 .rearrange("a p n -> p (a n)")).then_inc(g_in[n % 2], 16)

        @block.scalar
        def _(act):
            for t in range(NB * KB):
                act.wait_ge(o_in[t % 2], t // 2 * 16 + 16)
                act.copy(o_hi[:, t], stage[:, t % 2]).then_inc(o_hi_done, 1)
            act.sem_inc(hi_done, 2)
            with act.Fori(0, KD // 2) as i:
                for n in range(2 * NB):
                    b = n % 2
                    act.wait_ge(w_in[b], half(i, n))
                    act.wait_ge(mm_done, i * 6 + n + 1)
                    act.copy(w_hi[:, b], w_raw[:, b]).then_inc(hi_done, 1)
                    act.wait_ge(g_in[b], half(i, n))
                    act.activation(gate[:, b], gate[:, b], ACT.Tanh, scale=0.5).then_inc(th_done, 1)
                    if n % NB == NB - 1:
                        act.wait_ge(summed, i * 6 + n + 1)
                        act.dma_start(merged[bass.ds(i * 2 + n // NB, 1)].rearrange("a p n -> p (a n)"), total[:, n // NB])\
                            .then_inc(stored[n // NB], 16)
            for b in range(2):
                act.wait_ge(stored[b], 16 + KD // 2 * 16)

        @block.gpsimd
        def _(pool):
            for t in range(NB * KB):
                pool.wait_ge(o_hi_done, t + 1)
                pool.tensor_tensor(o_lo[:, t], stage[:, t % 2], o_hi[:, t].bitcast(F32), ALU.subtract).then_inc(o_lo_done, 1)
            pool.sem_inc(lo_done, 2)
            with pool.Fori(0, KD // 2) as i:
                for n in range(2 * NB):
                    b = n % 2
                    pool.wait_ge(hi_done, i * 6 + n + 3)
                    pool.tensor_tensor(w_lo[:, b], w_raw[:, b], w_hi[:, b].bitcast(F32), ALU.subtract).then_inc(lo_done, 1)

        @block.tensor
        def _(pe):
            pe.sem_inc(mm_done, 2)
            pe.wait_ge(o_lo_done, NB * KB)
            with pe.Fori(0, KD // 2) as i:
                for n in range(2 * NB):
                    b = n % 2
                    pe.wait_ge(lo_done, i * 6 + n + 3)
                    pe.wait_ge(gated, i * 6 + n + 1)
                    for k in range(KB):
                        for tb in range(NTB):
                            sl = slice(tb * TB, (tb + 1) * TB)
                            o = (n % NB) * KB + k
                            last = mm3(pe, acc[:, b, tb], w_hi[:, b, k], w_lo[:, b, k], o_hi[:, o, sl], o_lo[:, o, sl],
                                       k == 0, k == KB - 1)
                    last.then_inc(mm_done, 1)

        @block.vector
        def _(dve):
            dve.sem_inc(gated, 2)
            for b in range(2):
                dve.sem_inc(stored[b], 16)
            three = lambda a: a.rearrange("p (a n) -> p a n", a=NTB)
            with dve.Fori(0, KD // 2) as i:
                for n in range(2 * NB):
                    b, row, first = n % 2, n // NB, n % NB == 0
                    dve.wait_ge(th_done, i * 6 + n + 1)
                    dve.wait_ge(mm_done, i * 6 + n + 3)
                    if first:
                        dve.wait_ge(stored[row], i * 16 + 16)
                        dve.scalar_tensor_tensor(three(total[:, row]), three(gate[:, b]), 1.0, acc[:, b, 0:NTB], ALU.add,
                                                 ALU.mult).then_inc(gated, 1)
                        dve.sem_inc(summed, 1)
                    else:
                        dve.scalar_tensor_tensor(three(gate[:, b]), three(gate[:, b]), 1.0, acc[:, b, 0:NTB], ALU.add,
                                                 ALU.mult).then_inc(g_prod, 1)
                        dve.wait_ge(g_prod, i * 4 + [0, 1, 2, 2, 3, 4][n])
                        dve.tensor_tensor(total[:, row], total[:, row], gate[:, b], ALU.add).then_inc(gated, 1)
                        dve.wait_ge(gated, i * 6 + n + 3)
                        dve.sem_inc(summed, 1)


def out_project(nc, merged, w_out, x_tm, rows):
    NH = D // TB
    with Space(nc, "wo") as s:
        w_hi, w_lo = s.sb("w_hi", [KD, D], F32R), s.sb("w_lo", [KD, D], F32R)
        w_raw = s.sb("w_raw", [2, D])
        m_raw = s.sb("m_raw", [2, KD, P])
        m_hi, m_lo = s.sb("m_hi", [2, KD, P], F32R), s.sb("m_lo", [2, KD, P], F32R)
        acc = s.ps("acc", [2, NH, TB])
        w_in = [s.sem(f"w_in{b}") for b in range(2)]
        m_in = [s.sem(f"m_in{b}") for b in range(2)]
        x_in = [s.sem(f"x_in{t}") for t in range(NT)]
        w_hi_done, w_lo_done, hi_done, lo_done, halved, mm_done, added = (
            s.sem(x) for x in ("w_hi_done", "w_lo_done", "hi_done", "lo_done", "halved", "mm_done", "added"))
        block = s.block()
        m_t = merged.rearrange("k p n -> p k n")

        @block.sync
        def _(sp):
            for t in range(NT):
                sp.dma_start(x_tm[:, t], rows[t]).then_inc(x_in[t], 16)
                if t < KD:
                    if t >= 2:
                        sp.wait_ge(w_hi_done, t - 1)
                        sp.wait_ge(w_lo_done, t - 1)
                    sp.dma_start(w_raw[:, t % 2], w_out[t * P:(t + 1) * P, :]).then_inc(w_in[t % 2], 16)
            for t in range(NT):
                if t >= 2:
                    sp.wait_ge(lo_done, t - 1)
                sp.dma_start(m_raw[:, t % 2], m_t[:, :, t * P:(t + 1) * P]).then_inc(m_in[t % 2], 16)

        @block.scalar
        def _(act):
            for k in range(KD):
                act.wait_ge(w_in[k % 2], k // 2 * 16 + 16)
                act.copy(w_hi[:, k], w_raw[:, k % 2]).then_inc(w_hi_done, 1)
            for t in range(NT):
                act.wait_ge(halved, t + 1)
                if t >= 2:
                    act.wait_ge(mm_done, t - 1)
                act.copy(m_hi[:, t % 2], m_raw[:, t % 2]).then_inc(hi_done, 1)

        @block.gpsimd
        def _(pool):
            for k in range(KD):
                pool.wait_ge(w_hi_done, k + 1)
                pool.tensor_tensor(w_lo[:, k], w_raw[:, k % 2], w_hi[:, k].bitcast(F32), ALU.subtract).then_inc(w_lo_done, 1)
            for t in range(NT):
                pool.wait_ge(hi_done, t + 1)
                pool.tensor_tensor(m_lo[:, t % 2], m_raw[:, t % 2], m_hi[:, t % 2].bitcast(F32), ALU.subtract).then_inc(lo_done, 1)

        @block.tensor
        def _(pe):
            pe.wait_ge(w_lo_done, KD)
            for t in range(NT):
                b = t % 2
                pe.wait_ge(lo_done, t + 1)
                if t >= 2:
                    pe.wait_ge(added, t - 1)
                for k in range(KD):
                    for n in range(NH):
                        sl = slice(n * TB, (n + 1) * TB)
                        last = mm3(pe, acc[:, b, n], m_hi[:, b, k], m_lo[:, b, k], w_hi[:, k, sl], w_lo[:, k, sl],
                                   k == 0, k == KD - 1)
                last.then_inc(mm_done, 1)

        @block.vector
        def _(dve):
            def halve(t):
                dve.wait_ge(m_in[t % 2], t // 2 * 16 + 16)
                dve.tensor_scalar(m_raw[:, t % 2], m_raw[:, t % 2], 0.5, None, ALU.mult).then_inc(halved, 1)
            halve(0)
            for t in range(NT):
                if t + 1 < NT:
                    halve(t + 1)
                dve.wait_ge(mm_done, t + 1)
                dve.wait_ge(x_in[t], 16)
                xt = x_tm[:, t].rearrange("p (a n) -> p a n", a=NH)
                dve.tensor_tensor(xt, acc[:, t % 2], xt, ALU.add).then_inc(added, 1)


def mlp(nc, name, w1, w2, x_tm, u_hi, u_lo, tiles):
    TOK = len(tiles) * P
    HT = TOK // 2
    NG = FF // (2 * P)
    NP = len(tiles) * 2
    with Space(nc, name) as s:
        w1_raw = s.sb("w1_raw", [2, KD, P])
        w1_hi, w1_lo = s.sb("w1_hi", [2, KD, P], F32R), s.sb("w1_lo", [2, KD, P], F32R)
        w2_raw = s.sb("w2_raw", [2, D])
        w2_hi, w2_lo = s.sb("w2_hi", [4, D], F32R), s.sb("w2_lo", [4, D], F32R)
        rel = s.sb("rel", [2, TOK])
        h_hi, h_lo = s.sb("h_hi", [4, TOK], F32R), s.sb("h_lo", [4, TOK], F32R)
        ps1 = s.ps("ps1", [2, 2, TB])
        ps2 = s.ps("ps2", [4, TB])
        w1_in = [s.sem(f"w1_in{b}") for b in range(2)]
        w2_in = [s.sem(f"w2_in{b}") for b in range(2)]
        (w1_hi_done, w1_lo_done, w2_hi_done, w2_lo_done, up_done, relu_done, sq_done, hh_done, hl_done, part_done,
         added) = (s.sem(x) for x in ("w1_hi_done", "w1_lo_done", "w2_hi_done", "w2_lo_done", "up_done", "relu_done",
                                      "sq_done", "hh_done", "hl_done", "part_done", "added"))
        block = s.block()
        w1_t = w1.rearrange("(k p) n -> p k n", p=P)
        two = lambda a: a.rearrange("p (a n) -> p a n", a=2)


        def groups(eng, up, down, late=lambda g, par: None):
            def ahead(g, par):
                up(g + 1, 1 - par)
                down(g, par)
                late(g + 1, 1 - par)
            up(0, 0)
            late(0, 0)
            with eng.Fori(0, NG // 2 - 1) as i:
                ahead(i * 2, 0)
                ahead(i * 2 + 1, 1)
            ahead(NG - 2, 0)
            down(NG - 1, 1)

        @block.sync
        def _(sp):
            def load_w1(g, par):
                for j in range(2):
                    sp.wait_ge(w1_lo_done, g * 2 + j + 1)
                    sp.dma_start(w1_raw[:, j], w1_t[:, :, bass.ds(g * (2 * P) + j * P, P)]).then_inc(w1_in[j], 16)

            def load_w2(g, par):
                for j in range(2):
                    sp.wait_ge(w2_lo_done, g * 2 + j + 1)
                    sp.dma_start(w2_raw[:, j], w2[bass.ds(g * (2 * P) + j * P, P), :]).then_inc(w2_in[j], 16)
            groups(sp, load_w1, load_w2)

        @block.scalar
        def _(act):
            act.sem_inc(relu_done, 2)

            def up(g, par):
                for j in range(2):
                    m = g * 2 + j
                    act.wait_ge(w1_in[j], g * 16 + 16)
                    act.wait_ge(up_done, m + 1)
                    act.copy(w1_hi[:, j], w1_raw[:, j]).then_inc(w1_hi_done, 1)

            def square(g, par):
                for j in range(2):
                    m = g * 2 + j
                    act.wait_ge(up_done, m + 3)
                    act.wait_ge(hl_done, m + 1)
                    act.activation(two(rel[:, j]), ps1[:, j, :, 0:HT], ACT.Relu).then_inc(relu_done, 1)
                    act.wait_ge(sq_done, m + 1)
                    act.copy(h_hi[:, 2 * par + j], rel[:, j]).then_inc(hh_done, 1)

            def down(g, par):
                for j in range(2):
                    act.wait_ge(w2_in[j], g * 16 + 16)
                    act.wait_ge(part_done, g * NP + NP)
                    act.copy(w2_hi[:, 2 * par + j], w2_raw[:, j]).then_inc(w2_hi_done, 1)
            groups(act, up, down, square)

        @block.gpsimd
        def _(pool):
            pool.sem_inc(w1_lo_done, 2)
            pool.sem_inc(w2_lo_done, 2)
            pool.sem_inc(hl_done, 2)

            def up(g, par):
                for j in range(2):
                    m = g * 2 + j
                    pool.wait_ge(w1_hi_done, m + 1)
                    pool.tensor_tensor(w1_lo[:, j], w1_raw[:, j], w1_hi[:, j].bitcast(F32), ALU.subtract).then_inc(w1_lo_done, 1)

            def square(g, par):
                for j in range(2):
                    m = g * 2 + j
                    pool.wait_ge(relu_done, m + 3)
                    pool.wait_ge(part_done, g * NP + NP)
                    pool.tensor_tensor(rel[:, j], rel[:, j], rel[:, j], ALU.mult).then_inc(sq_done, 1)
                    pool.wait_ge(hh_done, m + 1)
                    pool.tensor_tensor(h_lo[:, 2 * par + j], rel[:, j], h_hi[:, 2 * par + j].bitcast(F32), ALU.subtract)\
                        .then_inc(hl_done, 1)

            def down(g, par):
                for j in range(2):
                    pool.wait_ge(w2_hi_done, g * 2 + j + 1)
                    pool.tensor_tensor(w2_lo[:, 2 * par + j], w2_raw[:, j], w2_hi[:, 2 * par + j].bitcast(F32), ALU.subtract)\
                        .then_inc(w2_lo_done, 1)
            groups(pool, up, down, square)

        @block.tensor
        def _(pe):
            pe.sem_inc(up_done, 2)
            pe.sem_inc(part_done, 2 * NP)

            def up(g, par):
                for j in range(2):
                    m = g * 2 + j
                    pe.wait_ge(w1_lo_done, m + 3)
                    pe.wait_ge(relu_done, m + 1)
                    for k in range(KD):
                        for t in range(2):
                            sl = slice(t * HT, (t + 1) * HT)
                            last = mm3(pe, ps1[:, j, t, 0:HT], w1_hi[:, j, k], w1_lo[:, j, k], u_hi[:, k, sl], u_lo[:, k, sl],
                                       k == 0, k == KD - 1)
                    last.then_inc(up_done, 1)

            def down(g, par):
                pe.wait_ge(hl_done, g * 2 + 4)
                pe.wait_ge(w2_lo_done, g * 2 + 4)
                for t in range(len(tiles)):
                    for n in range(2):
                        q = 2 * t + n
                        pe.wait_ge(added, g * NP + q + 1)
                        for j in range(2):
                            a = 2 * par + j
                            last = mm3(pe, ps2[:, q % 4], h_hi[:, a, t * P:(t + 1) * P], h_lo[:, a, t * P:(t + 1) * P],
                                       w2_hi[:, a, n * TB:(n + 1) * TB], w2_lo[:, a, n * TB:(n + 1) * TB], j == 0, j == 1)
                        last.then_inc(part_done, 1)
            groups(pe, up, down)

        @block.vector
        def _(dve):
            dve.sem_inc(added, 4)

            def down(g, par):
                for t in range(len(tiles)):
                    for n in range(2):
                        q = 2 * t + n
                        dve.wait_ge(part_done, g * NP + (2 * NP + q + 1))
                        xt = x_tm[:, tiles[t], n * TB:(n + 1) * TB]
                        dve.tensor_tensor(xt, ps2[:, q % 4], xt, ALU.add).then_inc(added, 1)
            groups(dve, lambda g, par: None, down)


def final_norm(nc, x_tm, gain, outs):
    with Space(nc, "fn") as s:
        junk, ss, ms, rr, rstd, g = s.sb("junk", [D]), s.sb("ss", [NT]), s.sb("ms", [NT]), s.sb("rr", [NT]), s.sb("rstd", [NT]), s.sb("g", [D])
        g_in, squared, mean, recip, rooted, normed, stored = (
            s.sem(x) for x in ("g_in", "squared", "mean", "recip", "rooted", "normed", "stored"))
        block = s.block()

        @block.sync
        def _(sp):
            sp.dma_start(g[:], gain.rearrange("(a n) -> a n", a=1).to_broadcast([P, D])).then_inc(g_in, 16)
            for t in range(NT):
                sp.wait_ge(normed, t + 1)
                sp.dma_start(outs[t], x_tm[:, t]).then_inc(stored, 16)
            sp.wait_ge(stored, NT * 16)

        @block.scalar
        def _(act):
            for t in range(NT):
                if t:
                    act.wait_ge(squared, t)
                act.activation(junk[:], x_tm[:, t], ACT.Square, accum_out=ss[:, t:t + 1]).then_inc(squared, 1)
                if t % 4 == 3:
                    act.wait_ge(recip, t // 4 + 1)
                    act.activation(rstd[:, t - 3:t + 1], rr[:, t - 3:t + 1], ACT.Sqrt).then_inc(rooted, 1)

        @block.vector
        def _(dve):
            dve.wait_ge(g_in, 16)
            for a in range(0, NT, 4):
                sl = slice(a, a + 4)
                dve.wait_ge(squared, a + 4)
                dve.tensor_scalar(ms[:, sl], ss[:, sl], 1.0 / D, EPS, ALU.mult, ALU.add).then_inc(mean, 1)
                dve.wait_ge(mean, a // 4 + 1)
                dve.reciprocal(rr[:, sl], ms[:, sl]).then_inc(recip, 1)
                dve.wait_ge(rooted, a // 4 + 1)
                for t in range(a, a + 4):
                    dve.scalar_tensor_tensor(x_tm[:, t], x_tm[:, t], rstd[:, t:t + 1], g[:], ALU.mult, ALU.mult).then_inc(normed, 1)


def trunk(nc, outs, x_prompt, x_sample, norm1, w_in, na_rpb, dn_conv_w, dn_a_log, dn_dt_bias, dn_norm, lru_conv_w,
          lru_conv_b, lru_w_r, lru_b_r, lru_w_i, lru_b_i, lru_lam, w_br, w_out, norm2, w_mlp1, w_mlp2, norm_f):
    with ExitStack() as whole:
        def scratch(name, shape):
            return nc.dram_tensor(name, shape, F32, kind="Internal").ap()

        proj = scratch("proj", (N_MIX + N_GATE, P, T))
        o_t = scratch("o_t", (3 * BW // P, P, T))
        merged = scratch("merged", (KD, P, T))
        pad = scratch("rpb_pad", (8 * NDR, P))
        bias_d = scratch("bias_table", (NH_PAIR, P, NDR, GRID))
        g_rows = scratch("g_rows", (4 * HEADS, T))
        ident = whole.enter_context(nc.sbuf_tensor("ident", [P, P], F32))
        ones = whole.enter_context(nc.sbuf_tensor("ones", [P, P], F32))
        constants(nc, ident, ones)
        rows = [x_prompt[0, t * P:(t + 1) * P, :] for t in range(8)] + [x_sample[0, t * P:(t + 1) * P, :] for t in range(4)]
        with ExitStack() as held:
            u_hi = held.enter_context(nc.sbuf_tensor("u_hi", [P, KD, T], F32R))
            u_lo = held.enter_context(nc.sbuf_tensor("u_lo", [P, KD, T], F32R))
            with nc.sbuf_tensor("x_in", [P, NT, D], F32) as x_in:
                norm_transpose(nc, "n1", x_in, rows, norm1[0], u_hi, u_lo, ident, list(range(NT)))
            project(nc, "pm", u_hi, u_lo, w_in[0], 0, TILE_LRU, proj, 0)
            project(nc, "pg", u_hi, u_lo, w_in[0], COL_LRU, N_MIX - TILE_LRU + N_GATE, proj, TILE_LRU)
        rglru(nc, proj, o_t, lru_conv_w[0], lru_conv_b[0], lru_w_r[0], lru_b_r[0], lru_w_i[0], lru_b_i[0], lru_lam[0])
        na_bias(nc, na_rpb[0], pad, bias_d)
        attention(nc, proj, bias_d, o_t, ident)
        with ExitStack() as held:
            cols = held.enter_context(nc.sbuf_tensor("cols", [P, HEADS, 4, NT], F32))
            neg_strict = held.enter_context(nc.sbuf_tensor("neg_strict", [P, 2, P], F32))
            incl = held.enter_context(nc.sbuf_tensor("incl", [P, 2, P], F32))
            join = held.enter_context(nc.sbuf_tensor("join", [P, LEVELS, 2, P], U8))
            delta_masks(nc, neg_strict, incl, join)
            delta_prep(nc, proj, g_rows, cols, dn_a_log[0], dn_dt_bias[0], ident)
            deltanet(nc, proj, g_rows, cols, (neg_strict, incl, join), o_t, dn_conv_w[0], dn_norm[0], ident, ones)
        merge(nc, proj, o_t, merged, w_br[0])
        with nc.sbuf_tensor("x_tm", [P, NT, D], F32) as x_tm:
            out_project(nc, merged, w_out[0], x_tm, rows)
            half = NT // 2
            with ExitStack() as held:
                u_hi = held.enter_context(nc.sbuf_tensor("v_hi", [P, KD, half * P], F32R))
                u_lo = held.enter_context(nc.sbuf_tensor("v_lo", [P, KD, half * P], F32R))
                for n in range(2):
                    tiles = list(range(n * half, (n + 1) * half))
                    norm_transpose(nc, f"n2{n}", x_tm, None, norm2[0], u_hi, u_lo, ident, tiles)
                    mlp(nc, f"m{n}", w_mlp1[0], w_mlp2[0], x_tm, u_hi, u_lo, tiles)
            dst = [outs[0][0, t * P:(t + 1) * P, :] for t in range(8)] + [outs[1][0, t * P:(t + 1) * P, :] for t in range(4)]
            final_norm(nc, x_tm, norm_f, dst)


_INS = ['x_prompt', 'x_sample', 'norm1', 'w_in', 'na_rpb', 'dn_conv_w', 'dn_a_log', 'dn_dt_bias', 'dn_norm', 'lru_conv_w',
        'lru_conv_b', 'lru_w_r', 'lru_b_r', 'lru_w_i', 'lru_b_i', 'lru_lam', 'w_br', 'w_out', 'norm2', 'w_mlp1',
        'w_mlp2', 'norm_f']
_OUTS = [(1, 1024, 1024), (1, 512, 1024)]


def kernel(**inputs):
    import numpy as _np
    import concourse.bacc as _bacc
    from concourse import mybir as _mybir
    from concourse.bass_utils import run_bass_kernel_spmd as _run

    nc = _bacc.Bacc("TRN2", target_bir_lowering=False, num_devices=1)
    arrays, aps = {}, {}
    for name in _INS:
        a = _np.ascontiguousarray(inputs[name])
        arrays[f"in_{name}_dram"] = a
        aps[name] = nc.dram_tensor(f"in_{name}_dram", a.shape, _mybir.dt.from_np(a.dtype), kind="ExternalInput").ap()
    outs = [nc.dram_tensor(f"out_{i}_dram", shape, _mybir.dt.float32, kind="ExternalOutput").ap()
            for i, shape in enumerate(_OUTS)]
    trunk(nc, outs=outs, **aps)
    r = _run(nc, [arrays], core_ids=[0])
    return tuple(r.results[0][f"out_{i}_dram"] for i in range(len(_OUTS)))
```

```python
from contextlib import ExitStack

import concourse.bass as bass
import numpy as np
from concourse import mybir

F32 = mybir.dt.float32
F32R = mybir.dt.float32r
U8 = mybir.dt.uint8
ACT = mybir.ActivationFunctionType
ALU = mybir.AluOpType
AX = mybir.AxisListType

P = 128
D = 1024
KD = D // P
SEG = [(0, 1024), (1024, 512)]
T = 1536
NT = T // P
TB = 512
NTB = T // TB
EPS = 1e-6
BW = 512
CW = 4

GRID = 64
NA_HD = 64
NA_KH = 8
NA_KW = 16
NDR = 2 * NA_KH - 1
NDC = 2 * NA_KW - 1
NEG = -1e30

HEADS = 4
LEVELS = 7
FF = 4096

COL_BA = 3584
COL_LRU = 3600
COL_GATE = 4624
TILE_DN = 12
TILE_Z = 24
TILE_BA = 28
TILE_LRU = 29
N_MIX = 37
N_GATE = 24


def dsl(i, n=1):
    return bass.ds(i * n, n)


class Space:

    def __init__(self, nc, name):
        self.nc, self.name, self.ctx, self.sems = nc, name, ExitStack(), []

    def __enter__(self):
        return self

    def __exit__(self, *e):
        self.ctx.__exit__(*e)
        if e[0] is None:
            self.nc.clear_and_free_semaphores(self.sems)
            self.nc.all_engine_barrier()

    def sb(self, name, shape, dt=F32):
        return self.ctx.enter_context(self.nc.sbuf_tensor(f"{self.name}_{name}", [P] + list(shape), dt))

    def ps(self, name, shape):
        return self.ctx.enter_context(self.nc.psum_tensor(f"{self.name}_{name}", [P] + list(shape), F32))

    def sem(self, name):
        self.sems.append(self.nc.alloc_semaphore(name=f"{self.name}_{name}"))
        return self.sems[-1]

    def block(self):
        return self.ctx.enter_context(self.nc.Block())


def mm3(pe, out, w_hi, w_lo, x_hi, x_lo, first, last):
    pe.matmul(out, w_hi, x_hi, start=first, stop=False)
    pe.matmul(out, w_hi, x_lo, start=False, stop=False)
    return pe.matmul(out, w_lo, x_hi, start=False, stop=last)


def constants(nc, ident, ones):
    with Space(nc, "c") as s:
        made, cut = s.sem("made"), s.sem("cut")
        block = s.block()

        @block.gpsimd
        def _(pool):
            pool.memset(ones[:], 1.0).then_inc(made, 1)
            pool.memset(ident[:], 0.0).then_inc(made, 1)
            pool.wait_ge(made, 2)
            pool.affine_select(out=ident[:], in_=ident[:], compare_op=ALU.not_equal, fill=1.0, base=0,
                               pattern=[[-1, P]], channel_multiplier=1).then_inc(cut, 1)
            pool.wait_ge(cut, 1)


def norm_transpose(nc, name, x, sources, gain, u_hi, u_lo, ident, tiles):
    n = len(tiles)
    G = 4 if sources is not None else n
    with Space(nc, name) as s:
        loaded = [s.sem(f"loaded{t}") for t in range(n)]
        gained = s.sem("gained")
        squared, rstd_in, rstd_done = s.sem("squared"), s.sem("rstd_in"), s.sem("rstd_done")
        normed, turned, scaled = s.sem("normed"), s.sem("turned"), s.sem("scaled")
        hi_done, lo_done, recip = s.sem("hi_done"), s.sem("lo_done"), s.sem("recip")
        junk = s.sb("junk", [D])
        xn = s.sb("xn", [2, D])
        uf = s.sb("uf", [2, KD, P])
        gcol = s.sb("gcol", [KD])
        ss = s.sb("ss", [n])
        ms = s.sb("ms", [n])
        rr = s.sb("rr", [n])
        rstd = s.sb("rstd", [n])
        pst = s.ps("pst", [2, KD, P])
        block = s.block()

        @block.sync
        def _(sp):
            sp.dma_start(gcol[:], gain.rearrange("(k p) -> p k", p=P), allow_slow_non_contiguous=True).then_inc(gained, 16)
            if sources is not None:
                for j, t in enumerate(tiles):
                    sp.dma_start(x[:, t, :], sources[j]).then_inc(loaded[j], 16)

        @block.scalar
        def _(act):
            def square(j):
                if sources is not None:
                    act.wait_ge(loaded[j], 16)
                if j:
                    act.wait_ge(squared, j)
                act.activation(junk[:], x[:, tiles[j], :], ACT.Square, accum_out=ss[:, j:j + 1]).then_inc(squared, 1)

            for j in range(G):
                square(j)
            for j0 in range(0, n, G):
                act.wait_ge(recip, j0 // G + 1)
                act.activation(rstd[:, j0:j0 + G], rr[:, j0:j0 + G], ACT.Sqrt).then_inc(rstd_done, 1)
                for j in range(j0, j0 + G):
                    if j + G < n:
                        square(j + G)
                    act.wait_ge(scaled, j + 1)
                    act.copy(u_hi[:, :, j * P:(j + 1) * P], uf[:, j % 2]).then_inc(hi_done, 1)

        @block.vector
        def _(dve):
            def mean(j0):
                dve.wait_ge(squared, j0 + G)
                dve.tensor_scalar(ms[:, j0:j0 + G], ss[:, j0:j0 + G], 1.0 / D, EPS, ALU.mult, ALU.add).then_inc(rstd_in, 1)
                dve.wait_ge(rstd_in, j0 // G + 1)
                dve.reciprocal(rr[:, j0:j0 + G], ms[:, j0:j0 + G]).then_inc(recip, 1)
                dve.wait_ge(rstd_done, j0 // G + 1)

            def gain_tile(j):
                dve.wait_ge(turned, j + 1)
                if j == 0:
                    dve.wait_ge(gained, 16)
                if j >= 2:
                    dve.wait_ge(hi_done, j - 1)
                    dve.wait_ge(lo_done, j - 1)
                dve.tensor_tensor(uf[:, j % 2], pst[:, j % 2], gcol[:].unsqueeze(2).to_broadcast([P, KD, P]),
                                  ALU.mult).then_inc(scaled, 1)

            for j in range(n):
                if j and j % G == 0:
                    gain_tile(j - 1)
                if j % G == 0:
                    mean(j)
                if j >= 2:
                    dve.wait_ge(turned, j - 1)
                dve.tensor_scalar(xn[:, j % 2], x[:, tiles[j], :], rstd[:, j:j + 1], None, ALU.mult).then_inc(normed, 1)
                if j % G:
                    gain_tile(j - 1)
            gain_tile(n - 1)

        @block.tensor
        def _(pe):
            for j in range(n):
                pe.wait_ge(normed, j + 1)
                if j >= 2:
                    pe.wait_ge(scaled, j - 1)
                for k in range(KD):
                    last = pe.transpose(pst[:, j % 2, k], xn[:, j % 2, k * P:(k + 1) * P], ident[:])
                last.then_inc(turned, 1)

        @block.gpsimd
        def _(pool):
            for j in range(n):
                pool.wait_ge(hi_done, j + 1)
                pool.tensor_tensor(u_lo[:, :, j * P:(j + 1) * P], uf[:, j % 2],
                                   u_hi[:, :, j * P:(j + 1) * P].bitcast(F32), ALU.subtract).then_inc(lo_done, 1)
            pool.wait_ge(lo_done, n)


def lagged(eng, n, unit, lag=None):
    unit(0, 0)
    pairs = (n - 1) // 2

    def both(u, b):
        unit(u, b)
        if lag is not None:
            lag(u - 1, 1 - b)
    if pairs:
        with eng.Fori(0, pairs) as i:
            both(i * 2 + 1, 1)
            both(i * 2 + 2, 0)
    if (n - 1) % 2:
        both(n - 1, (n - 1) % 2)
    if lag is not None:
        lag(n - 1, (n - 1) % 2)


def nth16(u, b, credit=0):
    return (u - b) * 8 + 16 + credit


def project(nc, name, u_hi, u_lo, w, col0, n, dst, tile0):
    with Space(nc, name) as s:
        w_raw = s.sb("w_raw", [2, KD, P])
        w_hi = s.sb("w_hi", [2, KD, P], F32R)
        w_lo = s.sb("w_lo", [2, KD, P], F32R)
        stage = s.sb("stage", [2, T])
        acc = s.ps("acc", [2, 4, TB])
        w_in = [s.sem(f"w_in{b}") for b in range(2)]
        stored = [s.sem(f"stored{b}") for b in range(2)]
        hi_done, lo_done = s.sem("hi_done"), s.sem("lo_done")
        mm_done, evicted = s.sem("mm_done"), s.sem("evicted")
        block = s.block()
        w_t = w.rearrange("(k p) n -> p k n", p=P)


        @block.sync
        def _(sp):
            for b in range(2):
                sp.sem_inc(stored[b], 16)

            def load(u, b):
                sp.wait_ge(hi_done, u + 1)
                sp.wait_ge(lo_done, u + 1)
                sp.dma_start(w_raw[:, b], w_t[:, :, bass.ds(u * P + col0, P)]).then_inc(w_in[b], 16)

            def store(u, b):
                sp.wait_ge(evicted, u + 3)
                sp.dma_start(dst[bass.ds(u + tile0, 1)].rearrange("a p n -> p (a n)"), stage[:, b]).then_inc(stored[b], 16)
            lagged(sp, n, load, store)
            for b in range(2):
                sp.wait_ge(stored[b], 16 + 16 * ((n - b + 1) // 2))

        @block.scalar
        def _(act):
            act.sem_inc(hi_done, 2)

            def unit(u, b):
                act.wait_ge(w_in[b], nth16(u, b))
                act.wait_ge(mm_done, u + 1)
                act.copy(w_hi[:, b], w_raw[:, b]).then_inc(hi_done, 1)
            lagged(act, n, unit)

        @block.gpsimd
        def _(pool):
            pool.sem_inc(lo_done, 2)

            def unit(u, b):
                pool.wait_ge(hi_done, u + 3)
                pool.tensor_tensor(w_lo[:, b], w_raw[:, b], w_hi[:, b].bitcast(F32), ALU.subtract).then_inc(lo_done, 1)
            lagged(pool, n, unit)

        @block.tensor
        def _(pe):
            pe.sem_inc(mm_done, 2)

            def unit(u, b):
                pe.wait_ge(lo_done, u + 3)
                pe.wait_ge(evicted, u + 1)
                for k in range(KD):
                    for tb in range(NTB):
                        sl = slice(tb * TB, (tb + 1) * TB)
                        last = mm3(pe, acc[:, b, tb], w_hi[:, b, k], w_lo[:, b, k], u_hi[:, k, sl], u_lo[:, k, sl],
                                   k == 0, k == KD - 1)
                last.then_inc(mm_done, 1)
            lagged(pe, n, unit)

        @block.vector
        def _(dve):
            dve.sem_inc(evicted, 2)

            def unit(u, b):
                dve.wait_ge(mm_done, u + 3)
                dve.wait_ge(stored[b], nth16(u, b))
                dve.tensor_copy(stage[:, b].rearrange("p (a n) -> p a n", a=NTB), acc[:, b, 0:NTB]).then_inc(evicted, 1)
            lagged(dve, n, unit)


class Chain:

    def __init__(self, eng, sem, i, per):
        self.eng, self.sem, self.i, self.per, self.n = eng, sem, i, per, 0

    def add(self, ins):
        ins.then_inc(self.sem, 1)
        self.n += 1
        return ins

    def link(self, ins):
        self.add(ins)
        self.wait()

    def wait(self):
        self.eng.wait_ge(self.sem, self.i * self.per + self.n)

    def end(self):
        assert self.n == self.per, self.n


def log1p_steps(dve, c, e, z, z2, acc):
    c.link(dve.tensor_scalar(z2, e, 2.0, None, ALU.add))
    c.link(dve.reciprocal(z, z2))
    c.link(dve.tensor_tensor(z, z, e, ALU.mult))
    c.link(dve.tensor_tensor(z2, z, z, ALU.mult))
    c.link(dve.tensor_scalar(acc, z2, 2.0 / 17, 2.0 / 15, ALU.mult, ALU.add))
    for n in (13, 11, 9, 7, 5, 3, 1):
        c.link(dve.tensor_tensor(acc, acc, z2, ALU.mult))
        c.link(dve.tensor_scalar(acc, acc, 2.0 / n, None, ALU.add))
    c.link(dve.tensor_tensor(acc, acc, z, ALU.mult))


LOG1P_STEPS = 20
PADW = T + 6


def conv_load(eng, xpad, src, sem):
    for o, (b, n) in zip((2, 1024 + 5), SEG):
        eng.dma_start(xpad[:, o:o + n], src[:, b:b + n]).then_inc(sem, 16)


def conv_zero(eng, xpad, sem):
    eng.memset(xpad[:, 0:2], 0.0).then_inc(sem, 1)
    eng.memset(xpad[:, 1026:1029], 0.0).then_inc(sem, 1)
    eng.memset(xpad[:, 1541:PADW], 0.0).then_inc(sem, 1)


def conv_steps(dve, c, out, xpad, cw, bias=None):
    for j in range(CW):
        for o, (b, n) in zip((0, 1024 + 3), SEG):
            dst, src = out[:, b:b + n], xpad[:, o + j:o + j + n]
            if j == 0 and bias is not None:
                c.add(dve.tensor_scalar(dst, src, cw[:, 0:1], bias, ALU.mult, ALU.add))
            elif j == 0:
                c.add(dve.tensor_scalar(dst, src, cw[:, 0:1], None, ALU.mult))
            else:
                c.add(dve.scalar_tensor_tensor(dst, src, cw[:, j:j + 1], dst, ALU.mult, ALU.add))
        c.wait()


def project_rglru(nc, u_hi, u_lo, w, proj, o_t, conv_w, conv_b, w_r, b_r, w_i, b_i, lam):
    CT = BW // P
    HALF = TILE_Z // CT
    N = 2 * HALF
    assert HALF * CT == N_GATE and N % 2 == 0
    with Space(nc, "pl") as s:
        w_in = [s.sem(f"w_in{b}") for b in range(2)]
        w_stored = [s.sem(f"w_stored{b}") for b in range(2)]
        hi_done, lo_done = s.sem("hi_done"), s.sem("lo_done")
        mm_done, evicted = s.sem("mm_done"), s.sem("evicted")
        loaded, gate_in, param_in = s.sem("loaded"), s.sem("gate_in"), s.sem("param_in")
        wbd_in, stored, zeroed = s.sem("wbd_in"), s.sem("stored"), s.sem("zeroed")
        chain, achain = s.sem("chain"), s.sem("achain")
        conv_done, gates_mm, params_done = s.sem("conv_done"), s.sem("gates_mm"), s.sem("params_done")
        exp_ready, exp_done = s.sem("exp_ready"), s.sem("exp_done")
        r_done, i_done, rt_done = s.sem("r_done"), s.sem("i_done"), s.sem("rt_done")
        v_done, a_done, a2_done, scan_done = s.sem("v_done"), s.sem("a_done"), s.sem("a2_done"), s.sem("scan_done")
        gelu_in, gelu_th, out_done, sum_done = s.sem("gelu_in"), s.sem("gelu_th"), s.sem("out_done"), s.sem("sum_done")
        m_done, b_done, gg_done = (s.sem(x) for x in ("m_done", "b_done", "gg_done"))
        w_raw = s.sb("w_raw", [2, KD, P])
        w_hi = s.sb("w_hi", [2, KD, P], F32R)
        w_lo = s.sb("w_lo", [2, KD, P], F32R)
        stage = s.sb("stage", [2, T])
        acc = s.ps("acc", [2 * NTB, TB])
        xpad, xc, gt = s.sb("xpad", [PADW]), s.sb("xc", [T]), s.sb("gt", [T])
        sg, ti, a = s.sb("sg", [T]), s.sb("ti", [T]), s.sb("a", [T])
        rt, m = s.sb("rt", [T]), s.sb("m", [T])
        h = s.sb("h", [2, T])
        tg = s.sb("tg", [T])
        wbd = s.sb("wbd", [2, 2, P])
        cw = s.sb("cw", [CW])
        prm = s.sb("prm", [7])
        hb = s.sb("hb", [4])
        lt = s.sb("lt", [5, 2])
        sp2, sp4, nsp4 = s.sb("sp2", [2]), s.sb("sp4", [2]), s.sb("nsp4", [2])
        psg = s.ps("psg", [2, TB])
        block = s.block()
        K_DVE = 3 + LOG1P_STEPS + 4 + 2 * CW
        w_t = w.rearrange("(k p) n -> p k n", p=P)
        PE_GATES = (3, 6)

        def tile_of(i, n):
            if n < HALF:
                return i * HALF + n, i * (HALF * P) + n * P
            return i * HALF + (N_MIX + n - HALF), i * (HALF * P) + ((n - HALF) * P + COL_GATE)


        @block.sync
        def _(sp):
            for b in range(2):
                sp.sem_inc(w_stored[b], 16)
            sp.sem_inc(stored, 16)
            sp.wait_ge(zeroed, 4)

            def load(i, n):
                sp.wait_ge(hi_done, i * N + n + 1)
                sp.wait_ge(lo_done, i * N + n + 1)
                sp.dma_start(w_raw[:, n % 2], w_t[:, :, bass.ds(tile_of(i, n)[1], P)]).then_inc(w_in[n % 2], 16)

            def store(i, n):
                sp.wait_ge(evicted, i * N + n + 3)
                sp.dma_start(proj[bass.ds(tile_of(i, n)[0], 1)].rearrange("a p n -> p (a n)"),
                             stage[:, n % 2]).then_inc(w_stored[n % 2], 16)

            def lru_loads(i):
                sp.wait_ge(stored, i * 16 + 16)
                conv_load(sp, xpad, proj[dsl(i + TILE_LRU)].rearrange("a p n -> p (a n)"), loaded)
                ch = bass.ds(i * P, P)
                sp.dma_start(cw[:], conv_w[:, ch].rearrange("j p -> p j"), allow_slow_non_contiguous=True).then_inc(param_in, 16)
                sp.dma_start(prm[:, 0:1], conv_b[ch].rearrange("(p a) -> p a", a=1)).then_inc(param_in, 16)
                for o, v in ((1, b_r), (3, b_i), (5, lam)):
                    sp.dma_start(prm[:, o:o + 2], v[:, ch].rearrange("d p -> p d"), allow_slow_non_contiguous=True).then_inc(param_in, 16)
                for g, v in enumerate((w_r, w_i)):
                    for half in range(2):
                        r = slice(64 * half, 64 * half + 64)
                        sp.dma_start(wbd[r, g, :, r], v[:, bass.ds(i * 2 + half, 1)].rearrange("d a c m -> c (d a) m")).then_inc(wbd_in, 16)
                sp.dma_start(gt[:], proj[dsl(i + (TILE_LRU + CT))].rearrange("a p n -> p (a n)")).then_inc(gate_in, 16)

            def body(i, last):
                lru_loads(i)
                for n in range(N):
                    if n + 1 < N:
                        load(i, n + 1)
                    elif not last:
                        load(i + 1, 0)
                    store(i, n)
                    if n == N - 2:
                        sp.wait_ge(out_done, i + 1)
                        sp.dma_start(o_t[dsl(i + 2 * CT)].rearrange("a p n -> p (a n)"), m[:]).then_inc(stored, 16)
            load(0, 0)
            with sp.Fori(0, CT - 1) as i:
                body(i, False)
            body(CT - 1, True)
            sp.wait_ge(stored, 16 + 16 * CT)
            for b in range(2):
                sp.wait_ge(w_stored[b], 16 + 16 * (CT * N // 2))

        @block.gpsimd
        def _(pool):
            conv_zero(pool, xpad, zeroed)
            pool.memset(wbd[:], 0.0).then_inc(zeroed, 1)
            pool.sem_inc(lo_done, 2)
            with pool.Fori(0, CT) as i:
                for n in range(N):
                    b = n % 2
                    pool.wait_ge(hi_done, i * N + n + 3)
                    pool.tensor_tensor(w_lo[:, b], w_raw[:, b], w_hi[:, b].bitcast(F32), ALU.subtract).then_inc(lo_done, 1)
                    if n == 2:
                        pool.wait_ge(gelu_in, i * 3 + 2)
                        pool.tensor_tensor(ti[:], tg[:], gt[:], ALU.mult).then_inc(gelu_in, 1)
                    if n == 8:
                        pool.wait_ge(scan_done, i * 2 + 2)
                        pool.tensor_tensor(m[:], h[:, 0], h[:, 1], ALU.add).then_inc(sum_done, 1)

        @block.scalar
        def _(act):
            act.sem_inc(hi_done, 2)
            with act.Fori(0, CT) as i:
                for n in range(N):
                    b = n % 2
                    act.wait_ge(w_in[b], i * (N * 8) + nth16(n, b))
                    act.wait_ge(mm_done, i * N + n + 1)
                    act.copy(w_hi[:, b], w_raw[:, b]).then_inc(hi_done, 1)
                    if n == 1:
                        act.wait_ge(exp_ready, i + 1)
                        act.activation(lt[:, 2], lt[:, 1], ACT.Exp, scale=-1.0).then_inc(exp_done, 1)
                    if n == 2:
                        act.wait_ge(gate_in, i * 16 + 16)
                        act.activation(ti[:], gt[:], ACT.Square).then_inc(gelu_in, 1)
                        act.wait_ge(gelu_in, i * 3 + 1)
                        act.activation(tg[:], ti[:], ACT.Copy, scale=0.044715, bias=1.0).then_inc(gelu_in, 1)
                    if n == 3:
                        act.wait_ge(gelu_in, i * 3 + 3)
                        act.activation(tg[:], ti[:], ACT.Tanh, scale=float(np.sqrt(2 / np.pi))).then_inc(gelu_th, 1)
                        act.wait_ge(params_done, i + 1)
                    if n - 1 not in PE_GATES:
                        continue
                    d = PE_GATES.index(n - 1)
                    if d:
                        act.wait_ge(scan_done, i * 2 + 1)
                    else:
                        act.wait_ge(gelu_th, i + 1)
                    for tb in range(NTB):
                        sl = slice(tb * TB, (tb + 1) * TB)
                        act.wait_ge(gates_mm, i * 12 + 6 * d + 2 * tb + 2)
                        act.activation(sg[:, sl], psg[:, 0], ACT.Tanh, bias=hb[:, d:d + 1], scale=0.5).then_inc(achain, 1)
                        act.activation(ti[:, sl], psg[:, 1], ACT.Tanh, bias=hb[:, 2 + d:3 + d], scale=0.5).then_inc(i_done, 1)
                    act.wait_ge(achain, i * 6 + 3 * d + 3)
                    act.activation(a[:], sg[:], ACT.Exp, bias=nsp4[:, d:d + 1], scale=nsp4[:, d:d + 1]).then_inc(a_done, 1)
                    act.wait_ge(a_done, i * 2 + d + 1)
                    act.activation(sg[:], sg[:], ACT.Tanh, bias=sp4[:, d:d + 1], scale=sp4[:, d:d + 1]).then_inc(r_done, 1)
                    act.activation(rt[:], a[:], ACT.Square).then_inc(a2_done, 1)
                    act.wait_ge(v_done, i * 2 + d + 1)
                    act.activation(rt[:], rt[:], ACT.Sqrt).then_inc(rt_done, 1)

        @block.tensor
        def _(pe):
            pe.sem_inc(mm_done, 2)
            with pe.Fori(0, CT) as i:
                for n in range(N):
                    b = n % 2
                    pe.wait_ge(lo_done, i * N + n + 3)
                    pe.wait_ge(evicted, i * N + n + 1)
                    for k in range(KD):
                        for tb in range(NTB):
                            sl = slice(tb * TB, (tb + 1) * TB)
                            last = mm3(pe, acc[:, b * NTB + tb], w_hi[:, b, k], w_lo[:, b, k], u_hi[:, k, sl], u_lo[:, k, sl],
                                       k == 0, k == KD - 1)
                        if n in PE_GATES and k % 2 == 0 and k // 2 < NTB:
                            d, tb = PE_GATES.index(n), k // 2
                            if d == 0 and tb == 0:
                                pe.wait_ge(conv_done, i + 1)
                                pe.wait_ge(wbd_in, i * 64 + 64)
                            if d or tb:
                                pe.wait_ge(achain, i * 6 + 3 * d + tb)
                                pe.wait_ge(i_done, i * 6 + 3 * d + tb)
                            for g in range(2):
                                pe.matmul(psg[:, g], wbd[:, g, d], xc[:, tb * TB:(tb + 1) * TB], start=True,
                                          stop=True).then_inc(gates_mm, 1)
                    last.then_inc(mm_done, 1)

        @block.vector
        def _(dve):
            dve.sem_inc(evicted, 2)

            def params(i, c):
                dve.wait_ge(param_in, i * 80 + 80)
                c.add(dve.tensor_scalar(hb[:], prm[:, 1:5], 0.5, None, ALU.mult))
                c.link(dve.tensor_scalar(lt[:, 0], prm[:, 5:7], -1.0, None, ALU.mult))
                c.link(dve.tensor_tensor(lt[:, 1], lt[:, 0], prm[:, 5:7], ALU.max))
                dve.sem_inc(exp_ready, 1)
                dve.wait_ge(exp_done, i + 1)
                log1p_steps(dve, c, lt[:, 2], lt[:, 3], lt[:, 4], sp2[:])
                c.link(dve.tensor_scalar(lt[:, 0], lt[:, 0], 0.0, None, ALU.max))
                c.link(dve.tensor_tensor(sp2[:], sp2[:], lt[:, 0], ALU.add))
                c.add(dve.tensor_scalar(sp4[:], sp2[:], 4.0, None, ALU.mult))
                c.add(dve.tensor_scalar(nsp4[:], sp2[:], -4.0, None, ALU.mult))
                c.wait()
                dve.sem_inc(params_done, 1)

            def direction(i, d):
                dve.wait_ge(r_done, i * 2 + d + 1)
                dve.wait_ge(a2_done, i * 2 + d + 1)
                dve.scalar_tensor_tensor(rt[:], rt[:], 1.0, sg[:], ALU.add, ALU.mult).then_inc(v_done, 1)
                dve.wait_ge(i_done, i * 6 + 3 * d + 3)
                dve.scalar_tensor_tensor(m[:], ti[:], 1.0, xc[:], ALU.add, ALU.mult).then_inc(m_done, 1)
                dve.wait_ge(rt_done, i * 2 + d + 1)
                dve.wait_ge(m_done, i * 2 + d + 1)
                dve.tensor_tensor(rt[:], rt[:], m[:], ALU.mult).then_inc(b_done, 1)
                dve.wait_ge(b_done, i * 2 + d + 1)
                for b0, n in SEG:
                    sl = slice(b0, b0 + n) if d == 0 else slice(b0 + n - 1, b0 - 1 if b0 else None, -1)
                    last = dve.tensor_tensor_scan(h[:, d, sl], a[:, sl], rt[:, sl], 0.0, ALU.mult, ALU.add)
                last.then_inc(scan_done, 1)

            with dve.Fori(0, CT) as i:
                c = Chain(dve, chain, i, K_DVE)
                for n in range(N):
                    b = n % 2
                    dve.wait_ge(mm_done, i * N + n + 3)
                    dve.wait_ge(w_stored[b], i * (N * 8) + nth16(n, b))
                    dve.tensor_copy(stage[:, b].rearrange("p (a n) -> p a n", a=NTB),
                                    acc[:, b * NTB:(b + 1) * NTB]).then_inc(evicted, 1)
                    if n == 0:
                        params(i, c)
                    if n == 1:
                        dve.wait_ge(loaded, i * 32 + 32)
                        conv_steps(dve, c, xc, xpad, cw, prm[:, 0:1])
                        dve.sem_inc(conv_done, 1)
                    if n in PE_GATES:
                        direction(i, PE_GATES.index(n))
                    if n == 8:
                        dve.wait_ge(gelu_th, i + 1)
                        dve.scalar_tensor_tensor(tg[:], tg[:], 1.0, gt[:], ALU.add, ALU.mult).then_inc(gg_done, 1)
                        dve.wait_ge(gg_done, i + 1)
                        dve.wait_ge(sum_done, i + 1)
                        dve.scalar_tensor_tensor(m[:], m[:], 0.25, tg[:], ALU.mult, ALU.mult).then_inc(out_done, 1)
                c.end()


NA_ROWS = [(b, r, n // GRID) for b, n in SEG for r in range(n // GRID)]
NA_TILES = [e for e in range(T // GRID) if e not in (SEG[0][1] // GRID - 1, T // GRID - 1)]
KEYS = NA_KH * GRID
NH_PAIR = BW // P


def na_bias(nc, rpb, pad, bias_d):
    with Space(nc, "nb") as s:
        table_in, padded, skewed = s.sem("table_in"), s.sem("padded"), s.sem("skewed")
        zeroed, io, chain, stored = s.sem("zeroed"), s.sem("io"), s.sem("chain"), s.sem("stored")
        copied = s.sem("copied")
        ready, flip_made, flipped = s.sem("ready"), s.sem("flip_made"), s.sem("flipped")
        rev = s.sb("rev", [NH_PAIR, NDR * GRID])
        flip = s.sb("flip", [P])
        ps = s.ps("ps", [NH_PAIR * 2, TB])
        rows = s.sb("rows", [P])
        raw = s.sb("raw", [NH_PAIR, NDR, GRID])
        qc, kc, w0, mask, neg = (s.sb(x, [GRID]) for x in ("qc", "kc", "w0", "mask", "neg"))
        block = s.block()
        nrow = 8 * NDR
        first = GRID - 1 - (NA_KW - 1)

        @block.gpsimd
        def _(pool):
            pool.memset(rows[:], 0.0).then_inc(zeroed, 1)
            pool.memset(flip[:], 0.0).then_inc(flip_made, 1)
            pool.wait_ge(flip_made, 1)
            for half in range(2):
                r = slice(64 * half, 64 * half + 64)
                pool.affine_select(out=flip[r, r], in_=flip[r, r], compare_op=ALU.not_equal, fill=1.0, base=1 - GRID,
                                   pattern=[[1, GRID]], channel_multiplier=1).then_inc(flip_made, 1)
            pool.wait_ge(zeroed, 1)
            for half in range(2):
                pool.iota(qc[64 * half:64 * half + 64, :], pattern=[[0, GRID]], base=0, channel_multiplier=1,
                          allow_small_or_imprecise_dtypes=True).then_inc(io, 1)
            pool.wait_ge(io, 2)
            pool.iota(kc[:], pattern=[[1, GRID]], base=0, channel_multiplier=0, allow_small_or_imprecise_dtypes=True).then_inc(io, 1)

        @block.sync
        def _(sp):
            sp.wait_ge(zeroed, 1)
            sp.dma_start(rows[0:nrow, first:first + NDC], rpb.rearrange("h r c -> (h r) c")).then_inc(table_in, 16)
            sp.wait_ge(table_in, 16)
            sp.dma_start(pad, rows[0:nrow, :]).then_inc(padded, 16)
            sp.wait_ge(padded, 16)
            for h in range(8):
                src = bass.AP(tensor=pad.tensor, offset=h * NDR * P, ap=[[1, GRID], [P, NDR], [1, GRID]])
                sp.dma_start(rev[64 * (h % 2):64 * (h % 2) + 64, h // 2], src).then_inc(skewed, 16)
            sp.wait_ge(ready, NH_PAIR)
            sp.dma_start(bias_d.rearrange("a p r c -> p a r c"), raw[:]).then_inc(stored, 16)
            sp.wait_ge(stored, 16)

        @block.tensor
        def _(pe):
            pe.wait_ge(flip_made, 3)
            pe.wait_ge(skewed, 8 * 16)
            half = NDR * GRID // 2
            for a in range(NH_PAIR):
                for z in range(2):
                    pe.matmul(ps[:, 2 * a + z, 0:half], flip[:], rev[:, a, z * half:(z + 1) * half], start=True,
                              stop=True).then_inc(flipped, 1)

        @block.scalar
        def _(act):
            half = NDR * GRID // 2
            for a in range(NH_PAIR):
                act.wait_ge(flipped, 2 * a + 2)
                act.copy(raw[:, a].rearrange("p r c -> p (r c)").rearrange("p (z n) -> p z n", z=2),
                         ps[:, 2 * a:2 * a + 2, 0:half]).then_inc(copied, 1)

        @block.vector
        def _(dve):
            c = Chain(dve, chain, 0, 6)
            dve.wait_ge(io, 3)
            c.link(dve.tensor_scalar(w0[:], qc[:], float(-(NA_KW // 2)), 0.0, ALU.add, ALU.max))
            c.link(dve.tensor_scalar(w0[:], w0[:], float(GRID - NA_KW), None, ALU.min))
            c.link(dve.tensor_tensor(w0[:], kc[:], w0[:], ALU.subtract))
            c.link(dve.tensor_scalar(mask[:], w0[:], 0.0, None, ALU.is_ge))
            c.link(dve.scalar_tensor_tensor(mask[:], w0[:], float(NA_KW), mask[:], ALU.is_lt, ALU.mult))
            c.link(dve.tensor_scalar(neg[:], mask[:], -1.0, -NEG, ALU.add, ALU.mult))
            for a in range(NH_PAIR):
                dve.wait_ge(copied, a + 1)
                wide = [P, NDR, GRID]
                dve.tensor_tensor(raw[:, a], raw[:, a], mask[:].unsqueeze(1).to_broadcast(wide), ALU.mult).then_inc(chain, 1)
                dve.wait_ge(chain, 6 + a + 1)
                dve.tensor_tensor(raw[:, a], raw[:, a], neg[:].unsqueeze(1).to_broadcast(wide), ALU.add).then_inc(ready, 1)
            c.end()


def attention(nc, proj, bias_d, o_t, ident, masks):
    NR = len(NA_ROWS)
    NS = 3
    with Space(nc, "na") as s:
        q_in, k_in, v_in, b_in = (s.sem(x) for x in ("q_in", "k_in", "v_in", "b_in"))
        seen = s.sem("seen")
        free, q_done, v_turned, v_done = (s.sem(x) for x in ("free", "q_done", "v_turned", "v_done"))
        scored, biased, exped, recip = (s.sem(x) for x in ("scored", "biased", "exped", "recip"))
        normed, turned, copied, mixed, out_done, stored, zeroed = (
            s.sem(x) for x in ("normed", "turned", "copied", "mixed", "out_done", "stored", "zeroed"))
        qt, kt, vt = s.sb("qt", [T]), s.sb("kt", [T]), s.sb("vt", [T])
        bias = s.sb("bias", [NDR * GRID])
        qbd = s.sb("qbd", [NR, P])
        vtm = s.sb("vtm", [T // GRID, P])
        sc, pr, pn, pt = s.sb("sc", [NS, KEYS]), s.sb("pr", [NS, KEYS]), s.sb("pn", [NS, KEYS]), s.sb("pt", [NS, KEYS])
        nmax, rsum, rinv = s.sb("nmax", [NR]), s.sb("rsum", [NR]), s.sb("rinv", [NR])
        ot = s.sb("ot", [T])
        ps_s = s.ps("ps_s", [3, KEYS])
        ps_t = s.ps("ps_t", [3, KEYS])
        ps_o = s.ps("ps_o", [2, 4, P])
        NVG = (len(NA_TILES) + 3) // 4
        mask_chain, mask_work = s.sem("mask_chain"), s.sb("mask_work", [P])
        block = s.block()

        @block.sync
        def _(sp):
            with sp.Fori(0, NH_PAIR) as i:
                sp.wait_ge(free, i + 1)
                for buf, sem, t0 in ((qt, q_in, 0), (kt, k_in, NH_PAIR), (vt, v_in, 2 * NH_PAIR)):
                    sp.dma_start(buf[:], proj[dsl(i + t0)].rearrange("a p n -> p (a n)")).then_inc(sem, 16)
                sp.dma_start(bias[:], bias_d[dsl(i)].rearrange("a p r c -> p (a r c)")).then_inc(b_in, 16)
                sp.wait_ge(out_done, i * 12 + 12)
                sp.dma_start(o_t[dsl(i)].rearrange("a p n -> p (a n)"), ot[:]).then_inc(stored, 16)
                sp.wait_ge(stored, i * 16 + 16)
                sp.sem_inc(free, 1)

        @block.gpsimd
        def _(pool):
            pool.memset(qbd[:], 0.0).then_inc(zeroed, 1)
            pool.sem_inc(free, 1)
            delta_masks(pool, mask_chain, mask_work, *masks)

        @block.tensor
        def _(pe):
            with pe.Fori(0, NH_PAIR) as i:
                pe.wait_ge(v_in, i * 16 + 16)
                for g in range(NVG):
                    if g >= 3:
                        pe.wait_ge(v_done, i * NVG + g - 2)
                    for j, e in enumerate(NA_TILES[4 * g:4 * g + 4]):
                        last = pe.transpose(ps_t[:, g % 3, j * P:(j + 1) * P], vt[:, e * GRID:e * GRID + P], ident[:])
                    last.then_inc(v_turned, 1)
                pe.wait_ge(q_done, i * 2 + 2)
                pe.wait_ge(k_in, i * 16 + 16)
                for n in range(NR + 3):
                    if n < NR:
                        if n >= 3:
                            pe.wait_ge(biased, i * NR + n - 2)
                        b, r, rows = NA_ROWS[n]
                        k0 = b + min(max(r - NA_KH // 2, 0), rows - NA_KH) * GRID
                        pe.matmul(ps_s[:, n % 3], qbd[:, n], kt[:, k0:k0 + KEYS], start=True, stop=True).then_inc(scored, 1)
                    if 2 <= n < NR + 2:
                        m = n - 2
                        pe.wait_ge(normed, i * NR + m + 1)
                        if m >= 3:
                            pe.wait_ge(copied, i * NR + m - 2)
                        else:
                            pe.wait_ge(v_done, i * NVG + NVG)
                        for j in range(4):
                            last = pe.transpose(ps_t[:, m % 3, j * P:(j + 1) * P], pn[:, m % NS, j * P:(j + 1) * P], ident[:])
                        last.then_inc(turned, 1)
                    if n >= 3:
                        m = n - 3
                        pe.wait_ge(copied, i * NR + m + 1)
                        if m % 4 == 0 and m >= 8:
                            pe.wait_ge(out_done, i * 12 + (m // 4 - 2) * 2 + 2)
                        b, r, rows = NA_ROWS[m]
                        e0 = b // GRID + min(max(r - NA_KH // 2, 0), rows - NA_KH)
                        for j in range(4):
                            last = pe.matmul(ps_o[:, m // 4 % 2, m % 4], vtm[:, e0 + 2 * j], pt[:, m % NS, j * P:(j + 1) * P],
                                             start=(j == 0), stop=(j == 3))
                        last.then_inc(mixed, 1)

        @block.vector
        def _(dve):
            dve.wait_ge(zeroed, 1)
            with dve.Fori(0, NH_PAIR) as i:
                dve.wait_ge(q_in, i * 16 + 16)
                for h in range(2):
                    r = slice(64 * h, 64 * h + 64)
                    dve.tensor_scalar(qbd[r, :, r], qt[r, :].rearrange("p (n c) -> p n c", c=GRID), NA_HD ** -0.5, None,
                                      ALU.mult).then_inc(q_done, 1)
                dve.wait_ge(b_in, i * 16 + 16)
                for n in range(NR + 3):
                    if n < NR:
                        dve.wait_ge(scored, i * NR + n + 1)
                        if n >= NS:
                            dve.wait_ge(exped, i * NR + n - NS + 1)
                        b, r, rows = NA_ROWS[n]
                        o = min(max(r - NA_KH // 2, 0), rows - NA_KH) - r + NA_KH - 1
                        dve.sem_inc(seen, 1)
                        dve.tensor_tensor_reduce(sc[:, n % NS], ps_s[:, n % 3], bias[:, o * GRID:o * GRID + KEYS], -1.0, 1e38,
                                                 ALU.add, ALU.min, nmax[:, n:n + 1]).then_inc(biased, 1)
                    if 1 <= n < NR + 1:
                        m = n - 1
                        dve.wait_ge(exped, i * NR + m + 1)
                        dve.reciprocal(rinv[:, m:m + 1], rsum[:, m:m + 1]).then_inc(recip, 1)
                        dve.wait_ge(recip, i * NR + m + 1)
                        if m >= NS:
                            dve.wait_ge(turned, i * NR + m - NS + 1)
                        dve.tensor_scalar(pn[:, m % NS], pr[:, m % NS], rinv[:, m:m + 1], None, ALU.mult).then_inc(normed, 1)
                    if n >= 3 and (n - 3) % 4 == 3:
                        g = (n - 3) // 4
                        dve.wait_ge(mixed, i * NR + 4 * g + 4)
                        for h in range(2):
                            r = slice(64 * h, 64 * h + 64)
                            dve.tensor_copy(ot[r, 4 * g * GRID:4 * (g + 1) * GRID].rearrange("p (a c) -> p a c", c=GRID),
                                            ps_o[r, g % 2, :, r]).then_inc(out_done, 1)

        @block.scalar
        def _(act):
            with act.Fori(0, NH_PAIR) as i:
                for g in range(NVG):
                    es = NA_TILES[4 * g:4 * g + 4]
                    act.wait_ge(v_turned, i * NVG + g + 1)
                    runs = [(0, len(es))] if es[-1] - es[0] == len(es) - 1 else None
                    if runs is None:
                        cut = next(j for j in range(1, len(es)) if es[j] != es[j - 1] + 1)
                        runs = [(0, cut), (cut, len(es))]
                    for a, z in runs:
                        last = act.copy(vtm[:, es[a]:es[z - 1] + 1], ps_t[:, g % 3, a * P:z * P].rearrange("p (a n) -> p a n", n=P))
                    last.then_inc(v_done, 1)
                for n in range(NR + 3):
                    if n >= 3:
                        m = n - 3
                        act.wait_ge(turned, i * NR + m + 1)
                        if m >= NS:
                            act.wait_ge(mixed, i * NR + m - NS + 1)
                        act.copy(pt[:, m % NS], ps_t[:, m % 3]).then_inc(copied, 1)
                    if n < NR:
                        act.wait_ge(biased, i * NR + n + 1)
                        if n >= NS:
                            act.wait_ge(normed, i * NR + n - NS + 1)
                        act.activation(pr[:, n % NS], sc[:, n % NS], ACT.Exp, bias=nmax[:, n:n + 1], scale=-1.0,
                                       accum_out=rsum[:, n:n + 1]).then_inc(exped, 1)


def delta_prep(nc, proj, g_rows, cols, a_log, dt_bias, ident):
    R = 2 * HEADS
    with Space(nc, "dp") as s:
        b_in, a_in, prm_in, stored = (s.sem(x) for x in ("b_in", "a_in", "prm_in", "stored"))
        chain, achain, turned, done = (s.sem(x) for x in ("chain", "achain", "turned", "done"))
        br, ar, e, t1, z, z2 = (s.sb(x, [T]) for x in ("br", "ar", "e", "t1", "z", "z2"))
        gf, gb, keep = s.sb("gf", [T]), s.sb("gb", [T]), s.sb("keep", [T])
        al, dt, ea = s.sb("al", [1]), s.sb("dt", [1]), s.sb("ea", [1])
        ps = s.ps("ps", [3, NT, R])
        block = s.block()
        abs_in, exp_done, beta_in, sums = (s.sem(x) for x in ("abs_in", "exp_done", "beta_in", "sums"))

        @block.sync
        def _(sp):
            sp.dma_start(al[0:R, :], a_log.rearrange("d (h a) -> (d h) a", a=1)).then_inc(prm_in, 16)
            sp.dma_start(dt[0:R, :], dt_bias.rearrange("d (h a) -> (d h) a", a=1)).then_inc(prm_in, 16)
            sp.dma_start(ar[0:R, :], proj[TILE_BA, R:2 * R, :]).then_inc(a_in, 16)
            sp.dma_start(br[0:R, :], proj[TILE_BA, 0:R, :]).then_inc(b_in, 16)
            sp.wait_ge(sums, 2)
            sp.dma_start(g_rows[0:R, :], gf[0:R, :]).then_inc(stored, 16)
            sp.dma_start(g_rows[R:2 * R, :], gb[0:R, :]).then_inc(stored, 16)
            sp.wait_ge(stored, 32)

        @block.scalar
        def _(act):
            act.wait_ge(prm_in, 32)
            act.activation(ea[0:R, :], al[0:R, :], ACT.Exp).then_inc(achain, 1)
            act.wait_ge(b_in, 16)
            act.activation(br[0:R, :], br[0:R, :], ACT.Tanh, scale=0.5).then_inc(beta_in, 1)
            act.wait_ge(abs_in, 1)
            act.activation(e[0:R, :], t1[0:R, :], ACT.Exp, scale=-1.0).then_inc(exp_done, 1)

        @block.vector
        def _(dve):
            c = Chain(dve, chain, 0, 10 + LOG1P_STEPS)
            r = slice(0, R)
            c.add(dve.memset(keep[r, :], 1.0))
            dve.wait_ge(prm_in, 32)
            dve.wait_ge(a_in, 16)
            c.link(dve.tensor_scalar(ar[r, :], ar[r, :], dt[r, :], None, ALU.add))
            c.add(dve.memset(keep[r, :].rearrange("p (t n) -> p t n", n=P)[:, :, 0:1], 0.0))
            c.link(dve.scalar_tensor_tensor(t1[r, :], ar[r, :], -1.0, ar[r, :], ALU.mult, ALU.max))
            dve.sem_inc(abs_in, 1)
            dve.wait_ge(exp_done, 1)
            log1p_steps(dve, c, e[r, :], z[r, :], z2[r, :], t1[r, :])
            c.link(dve.scalar_tensor_tensor(t1[r, :], ar[r, :], 0.0, t1[r, :], ALU.max, ALU.add))
            dve.wait_ge(achain, 1)
            c.link(dve.tensor_scalar(t1[r, :], t1[r, :], ea[r, :], -1.0, ALU.mult, ALU.mult))
            c.add(dve.tensor_tensor_scan(gf[r, :], keep[r, :], t1[r, :], 0.0, ALU.mult, ALU.add))
            c.add(dve.tensor_tensor_scan(gb[r, ::-1], keep[r, :], t1[r, ::-1], 0.0, ALU.mult, ALU.add))
            dve.wait_ge(beta_in, 1)
            c.link(dve.tensor_scalar(br[r, :], br[r, :], 1.0, 0.5, ALU.add, ALU.mult))
            dve.sem_inc(sums, 2)
            dve.wait_ge(turned, 1)
            for kind, (src, o) in enumerate(((0, 0), (1, HEADS), (2, 0), (2, HEADS))):
                c2 = dve.tensor_copy(cols[:, :, kind, :], ps[:, src, :, o:o + HEADS].rearrange("p t h -> p h t"))
            c.link(c2)
            c.end()

        @block.tensor
        def _(pe):
            pe.wait_ge(sums, 2)
            for n, src in enumerate((gf, gb, br)):
                for t in range(NT):
                    last = pe.transpose(ps[:, n, t], src[0:R, t * P:(t + 1) * P], ident[0:R, 0:R])
            last.then_inc(turned, 1)


def delta_masks(pool, chain, work, neg_strict, incl, join):

    def keep(n, tile, pattern, base, step):
        pool.wait_ge(chain, n)
        pool.affine_select(out=tile, in_=tile, compare_op=ALU.is_ge, fill=0.0, base=base, pattern=pattern,
                           channel_multiplier=step).then_inc(chain, 1)

    n = 0
    for tile, value, col, row, base in ((neg_strict[:, 0], -1.0, -1, 1, -1), (neg_strict[:, 1], -1.0, 1, -1, -1),
                                        (incl[:, 0], 1.0, 1, -1, 0), (incl[:, 1], 1.0, -1, 1, 0)):
        pool.memset(tile, value).then_inc(chain, 1)
        keep(n + 1, tile, [[col, P]], base, row)
        n += 2
    for v in range(LEVELS):
        m = 2 ** v
        for d in range(2):
            blocks = work[:].rearrange("p (c two m) -> p c two m", two=2, m=m)[:, :, 1 - d]
            pool.wait_ge(chain, n)
            pool.memset(work[:], 0.0).then_inc(chain, 1)
            pool.wait_ge(chain, n + 1)
            pool.memset(blocks, 1.0).then_inc(chain, 1)
            keep(n + 2, blocks, [[-2 * m, P // (2 * m)], [0, m]], -d * m, 1)
            keep(n + 3, blocks, [[2 * m, P // (2 * m)], [0, m]], m - 1 + d * m, -1)
            pool.wait_ge(chain, n + 4)
            pool.tensor_copy(join[:, v, d], work[:]).then_inc(chain, 1)
            n += 5
    pool.wait_ge(chain, n)


DCHAINS = [(d, g) for g in range(len(SEG)) for d in range(2)]
CONV_AT = {s + g: (n, tap, g) for s, n, tap in ((0, 0, 0), (2, 0, 1), (4, 0, 2), (6, 0, 3), (8, 1, 0), (10, 1, 1),
                                                (13, 1, 2), (15, 1, 3), (17, 2, 0), (19, 2, 1), (22, 2, 2), (24, 2, 3))
           for g in range(len(SEG))}
SILU_AT = {12: 0, 21: 1, 29: 2}
RS_AT, HALF_AT, GATE_AT = 28, 30, 35
SCALE_AT = {s: m for m, s in enumerate((33, 34, 37, 38, 40, 41))}
TANH_AT = {10: 0, 19: 1, 27: 2}
SQUARE_AT = {15: 0, 24: 1}
ROOT_AT, ZTANH_AT = 29, 31
SSUM_AT = {18: 0, 26: 1}
SPREAD_AT = {s: m for m, s in enumerate((31, 32, 35, 36, 38, 39))}
UNITS = LEVELS * 2 * NTB


def deltanet(nc, proj, g_rows, cols, masks, o_t, conv_w, norm_w, ident, ones):
    neg_strict, incl, join = masks
    UN = [(tg, d) for tg in range(NTB) for d in range(2)]
    with Space(nc, "dn") as s:
        names = ("x_in0", "x_in1", "z_in", "g_in", "prm_in", "stored", "out_done", "zeroed", "chain", "fchain",
                 "conv", "tanh", "silu", "sq", "ssum", "rs_in", "rooted", "diag", "bc", "scaled", "vhalf", "kc",
                 "kt_mm", "kt_ev", "cols_in", "cexp", "eg", "qd", "gram", "ediff", "dexp", "dmask", "amat", "u0",
                 "s_mm", "s_ev", "u_mm", "u_ev", "ks", "r", "new_mm", "new_ev", "o_mm", "o_ev", "st_mm", "st_ev",
                 "osum", "osq", "oss", "orr", "oroot", "odiag", "obc", "onormed", "zt", "gated", "at_ev", "s0", "seen", "pool_seen")
        S = {x: s.sem(x) for x in names}
        x = s.sb("x", [2, PADW])
        yn = s.sb("yn", [3, T])
        kf = s.sb("kf", [T])
        th = s.sb("th", [2, T])
        oz = s.sb("oz", [3, T])
        gbc = s.sb("gbc", [2, T])
        qd = s.sb("qd", [2, T])
        kd = s.sb("kd", [2, NT, P])
        bv = s.sb("bv", [2, NT, P])
        am = s.sb("am", [2 * NTB, 4, P])
        at = s.sb("at", [2 * NTB, 4, P])
        un = s.sb("un", [2 * NTB, 4, P])
        tn = s.sb("tn", [2 * NTB, 4, P])
        qk = s.sb("qk", [2 * NTB, 4, P])
        dd = s.sb("dd", [4, 4, P])
        cw = s.sb("cw", [3, CW])
        nw = s.sb("nw", [1])
        col = s.sb("col", [4, NT])
        cx = s.sb("cx", [6, NT])
        ms, rr, rs = (s.sb(v, [2, NT]) for v in ("ms", "rr", "rs"))
        oms, orr, ors = (s.sb(v, [NT]) for v in ("oms", "orr", "ors"))
        st = s.sb("st", [4, P])
        rb, nb = s.sb("rb", [4, P]), s.sb("nb", [4, P])
        ps = s.ps("ps", [8, 4, P])
        flat = lambda a: a.rearrange("p a n -> p (a n)")
        three = lambda a: a.rearrange("p (a n) -> p a n", a=NTB)
        four = lambda a: a.rearrange("p (a n) -> p a n", n=P)
        oc = [oz[:, 0], oz[:, 1]]
        zt = oz[:, 2]
        diag = [am[:, NTB * n:NTB * (n + 1)].rearrange("p a b n -> p (a b) n") for n in range(2)]
        sbuf_s = [dd[:, j] for j in range(4)]
        block = s.block()
        EGL = {0: 4, 1: 5}
        VT = LEVELS * 2 * NTB

        def glast(d):
            g4 = gbc[:, d].rearrange("p (t n) -> p t n", n=P)
            return g4[:, :, P - 1] if d == 0 else g4[:, :, 0]

        def live_chains(step):
            return [(j, d, SEG[g][0] // P + (step if d == 0 else SEG[g][1] // P - 1 - step))
                    for j, (d, g) in enumerate(DCHAINS) if step < SEG[g][1] // P]


        @block.sync
        def _(sp):
            sp.sem_inc(S["conv"], 1)
            sp.sem_inc(S["stored"], 16)
            sp.wait_ge(S["zeroed"], 6)
            sp.dma_start(nw[:], norm_w.rearrange("(p a) -> p a", a=1)).then_inc(S["prm_in"], 16)

            def load_x(h, n):
                sem = S[f"x_in{n % 2}"]
                conv_load(sp, x[:, n % 2], flat(proj[dsl(h + (TILE_DN + n * HEADS))].rearrange("a p n -> p a n")), sem)
                sp.dma_start(cw[:, n], conv_w[:, bass.ds(h * P + n * BW, P)].rearrange("j p -> p j"),
                             allow_slow_non_contiguous=True).then_inc(sem, 16)

            def load_qk(h):
                sp.wait_ge(S["conv"], h * 3 + 1)
                load_x(h, 0)
                load_x(h, 1)

            def load_v(h):
                sp.wait_ge(S["conv"], h * 3 + 2)
                load_x(h, 2)

            def load_g(h):
                for d in range(2):
                    row = g_rows[bass.ds(h + d * (2 * HEADS + HEADS), 1), :]
                    sp.dma_start(gbc[:, d], row.to_broadcast([P, T])).then_inc(S["g_in"], 16)

            def load_z(h):
                sp.dma_start(zt, flat(proj[dsl(h + TILE_Z)].rearrange("a p n -> p a n"))).then_inc(S["z_in"], 16)

            def store(i):
                sp.wait_ge(S["out_done"], i + 1)
                sp.dma_start(flat(o_t[dsl(i + HEADS)].rearrange("a p n -> p a n")), oc[0]).then_inc(S["stored"], 16)
            load_qk(0)
            load_g(0)
            load_z(0)
            load_v(0)
            with sp.Fori(0, HEADS - 1) as i:
                load_qk(i + 1)
                sp.wait_ge(S["amat"], i * 12 + 12)
                sp.wait_ge(S["eg"], i * 2 + 2)
                load_g(i + 1)
                load_v(i + 1)
                store(i)
                load_z(i + 1)
            store(HEADS - 1)
            sp.wait_ge(S["prm_in"], 16)
            sp.wait_ge(S["stored"], 16 + 16 * HEADS)

        @block.gpsimd
        def _(pool):
            for n in range(2):
                conv_zero(pool, x[:, n], S["zeroed"])

            def reset(buf, n):
                pool.tensor_copy(buf[:, n], ident[:].unsqueeze(1).to_broadcast([P, 4, P])).then_inc(S["u0"], 1)

            def lengths(h):
                for n in range(2):
                    pool.wait_ge(S["rooted"], h + 1)
                    pool.tensor_tensor(diag[n], ident[:].unsqueeze(1).to_broadcast([P, NT, P]),
                                       rs[:, n].unsqueeze(2).to_broadcast([P, NT, P]), ALU.mult).then_inc(S["diag"], 1)

            def decays(i):
                for n, (tg, d) in enumerate(UN):
                    pool.wait_ge(S["dexp"], i * 12 + 2 * n + 2)
                    b = n % 2
                    for a, mask in ((2 * b, neg_strict), (2 * b + 1, incl)):
                        pool.tensor_tensor(dd[:, a], dd[:, a], mask[:, d].unsqueeze(1).to_broadcast([P, 4, P]),
                                           ALU.mult).then_inc(S["dmask"], 1)
            for n in range(2 * NTB):
                reset(un, n)
                reset(tn, n)
            lengths(0)
            with pool.Fori(0, HEADS - 1) as i:
                decays(i)
                lengths(i + 1)
                pool.wait_ge(S["u_mm"], i * VT + VT)
                pool.wait_ge(S["u_ev"], i * VT + VT)
                pool.sem_inc(S["pool_seen"], 1)
                for n in range(2 * NTB):
                    reset(tn, n)
                pool.wait_ge(S["new_mm"], i * 24 + 24)
                pool.sem_inc(S["pool_seen"], 1)
                for n in range(2 * NTB):
                    reset(un, n)
            decays(HEADS - 1)

        @block.scalar
        def _(act):
            def front(h, u):
                if u in TANH_AT:
                    n = TANH_AT[u]
                    act.wait_ge(S["conv"], h * 3 + n + 2)
                    if n:
                        act.wait_ge(S["silu"], h * 3 + n)
                    act.activation(th[:, 0], yn[:, n], ACT.Tanh, scale=0.5).then_inc(S["tanh"], 1)
                if u in SQUARE_AT:
                    n = SQUARE_AT[u]
                    act.wait_ge(S["silu"], h * 3 + n + 1)
                    if n:
                        act.wait_ge(S["ssum"], h * 2 + n)
                    act.activation(th[:, 1], yn[:, n], ACT.Square, scale=0.5).then_inc(S["sq"], 1)
                if u == ROOT_AT:
                    act.wait_ge(S["rs_in"], h + 1)
                    act.activation(flat(rs[:]), flat(rr[:]), ACT.Sqrt).then_inc(S["rooted"], 1)

            def main(i, more):
                act.wait_ge(S["cols_in"], i + 1)
                act.activation(flat(cx[:]), flat(cx[:]), ACT.Exp).then_inc(S["cexp"], 1)
                act.wait_ge(S["g_in"], i * 32 + 32)
                for d in range(2):
                    act.activation(qd[:, d], gbc[:, d], ACT.Exp).then_inc(S["eg"], 1)
                for n in range(2 * NTB):
                    act.wait_ge(S["ediff"], i * 12 + 2 * n + 2)
                    b = n % 2
                    act.activation(flat(dd[:, 2 * b]), flat(dd[:, 2 * b]), ACT.Exp, scale=-1.0).then_inc(S["dexp"], 1)
                    act.activation(flat(dd[:, 2 * b + 1]), flat(dd[:, 2 * b + 1]), ACT.Exp).then_inc(S["dexp"], 1)
                act.wait_ge(S["scaled"], i * 6 + 6)
                act.copy(kf[:], yn[:, 1]).then_inc(S["kc"], 1)
                for n in range(2 * NTB):
                    act.wait_ge(S["u_mm"], i * VT + n + 1)
                    act.copy(at[:, n], ps[:, 4 + 2 * (n % 2)]).then_inc(S["at_ev"], 1)
                for k in range(UNITS - 2 * NTB):
                    act.wait_ge(S["s_mm"], i * (UNITS - 6) + k + 1)
                    if k == 0:
                        act.wait_ge(S["amat"], i * 12 + 12)
                    if k >= 4:
                        act.wait_ge(S["u_mm"], i * VT + 6 + k - 3)
                    act.copy(sbuf_s[k % 4], ps[:, k % 2]).then_inc(S["s_ev"], 1)
                    u = k + 2 * NTB
                    if more:
                        front(i + 1, u)
                    if u == ZTANH_AT:
                        act.wait_ge(S["z_in"], i * 16 + 16)
                        act.activation(th[:, 1], zt, ACT.Tanh, scale=0.5).then_inc(S["zt"], 1)
                act.wait_ge(S["stored"], i * 16 + 16)
                for step in range(8):
                    for j, d, t in live_chains(step):
                        act.wait_ge(S["new_mm"], i * 24 + K_OF[(step, j)] + 1)
                        if step:
                            act.wait_ge(S["st_mm"], i * 24 + K_OF[(step - 1, j)] + 1)
                        act.copy(nb[:, j], ps[:, 4 + j, 0]).then_inc(S["new_ev"], 1)
                    for j, d, t in live_chains(step):
                        act.wait_ge(S["o_mm"], i * 24 + K_OF[(step, j)] + 1)
                        act.copy(oc[d][:, t * P:(t + 1) * P], ps[:, 4 + j, 1]).then_inc(S["o_ev"], 1)
                act.wait_ge(S["osum"], i + 1)
                act.activation(th[:, 0], oc[0], ACT.Square).then_inc(S["osq"], 1)
                act.wait_ge(S["orr"], i + 1)
                act.activation(ors[:], orr[:], ACT.Sqrt).then_inc(S["oroot"], 1)
            for u in range(UNITS):
                front(0, u)
            with act.Fori(0, HEADS - 1) as i:
                main(i, True)
            main(HEADS - 1, False)

        @block.tensor
        def _(pe):
            def lengths(bank, col0, squares):
                for t in range(NT):
                    last = pe.matmul(ps[:, bank, 0, col0 + t:col0 + t + 1], squares[:, t * P:(t + 1) * P], ones[:, 0:1],
                                     start=True, stop=True)
                return last

            def front(h, u):
                if u in SSUM_AT:
                    n = SSUM_AT[u]
                    pe.wait_ge(S["sq"], h * 2 + n + 1)
                    lengths(2, n * NT, th[:, 1]).then_inc(S["ssum"], 1)
                if u in SPREAD_AT:
                    m = SPREAD_AT[u]
                    pe.wait_ge(S["diag"], h * 2 + m // NTB + 1)
                    if m >= 2:
                        pe.wait_ge(S["scaled"], h * 6 + m - 1)
                    pe.matmul(flat(ps[:, 2 + m % 2]), ones[:], flat(am[:, m]), start=True, stop=True).then_inc(S["bc"], 1)

            def main(i, more):
                pe.wait_ge(S["scaled"], i * 6 + 6)
                pe.wait_ge(S["vhalf"], i + 1)

                def token_major(n):
                    if n >= 4:
                        pe.wait_ge(S["kt_ev"], i * 12 + 2 * (n - 4) + 2)
                    for j in range(4):
                        t = 4 * (n // 2) + j
                        last = pe.transpose(ps[:, 4 + n % 4, j], yn[:, 1 + n % 2, t * P:(t + 1) * P], ident[:])
                    last.then_inc(S["kt_mm"], 1)

                for n in range(4):
                    token_major(n)
                pe.wait_ge(S["onormed"], i + 1)
                for tg in range(NTB):
                    if tg:
                        pe.wait_ge(S["amat"], i * 12 + 4 * tg)
                    for n, mov in enumerate((1, 0)):
                        for j in range(4):
                            sl = slice((4 * tg + j) * P, (4 * tg + j + 1) * P)
                            last = pe.matmul(ps[:, n, j], yn[:, 1, sl], yn[:, mov, sl], start=True, stop=True)
                    last.then_inc(S["gram"], 1)
                    if tg == 0:
                        for n in range(4, 2 * NTB):
                            token_major(n)
                for n in range(2 * NTB):
                    pe.wait_ge(S["amat"], i * 12 + 12)
                    pe.wait_ge(S["kt_ev"], i * 12 + 12)
                    if n >= 2:
                        pe.wait_ge(S["u_ev"], i * VT + n - 1)
                        pe.wait_ge(S["at_ev"], i * 6 + n - 1)
                    for j in range(4):
                        last = pe.transpose(ps[:, 4 + 2 * (n % 2), j], am[:, n, j], ident[:])
                    last.then_inc(S["u_mm"], 1)
                pe.wait_ge(S["at_ev"], i * 6 + 6)
                for v in range(1, LEVELS):
                    for n in range(2 * NTB + 1):
                        if n < 2 * NTB:
                            k = (v - 1) * 6 + n
                            pe.wait_ge(S["u_ev"], i * VT + k + 1)
                            if k >= 2:
                                pe.wait_ge(S["s_ev"], i * (UNITS - 6) + k - 1)
                            for j in range(4):
                                last = pe.matmul(ps[:, k % 2, j], at[:, n, j], tn[:, n, j], start=True, stop=True)
                            last.then_inc(S["s_mm"], 1)
                        if n:
                            m = n - 1
                            k = (v - 1) * 6 + m
                            pe.wait_ge(S["s_ev"], i * (UNITS - 6) + k + 1)
                            pe.wait_ge(S["u_ev"], i * VT + 6 + k - 1)
                            for j in range(4):
                                if v < LEVELS - 1:
                                    pe.matmul(ps[:, 4 + 2 * (m % 2), j], un[:, m, j], sbuf_s[k % 4][:, j], start=True, stop=True)
                                last = pe.matmul(ps[:, 5 + 2 * (m % 2), j], sbuf_s[k % 4][:, j], un[:, m, j], start=True, stop=True)
                            last.then_inc(S["u_mm"], 1)
                            if more:
                                front(i + 1, v * 6 + m)
                pe.wait_ge(S["u_ev"], i * VT + VT)
                pe.wait_ge(S["s_ev"], i * (UNITS - 6) + UNITS - 6)
                if more:
                    pe.wait_ge(S["scaled"], i * 6 + 12)
                pe.wait_ge(S["s0"], i + 1)
                pe.wait_ge(S["kc"], i + 1)
                pe.wait_ge(S["qd"], i * 2 + 2)
                for step in range(8):
                    live = live_chains(step)
                    for j, d, t in live:
                        if step:
                            pe.wait_ge(S["st_ev"], i * 24 + K_OF[(step - 1, j)] + 1)
                        pe.matmul(ps[:, j, 0], kf[:, t * P:(t + 1) * P], st[:, j], start=True, stop=True).then_inc(S["ks"], 1)
                    for j, d, t in live:
                        pe.wait_ge(S["r"], i * 24 + K_OF[(step, j)] + 1)
                        if step:
                            pe.wait_ge(S["o_ev"], i * 24 + K_OF[(step - 1, j)] + 1)
                        pe.matmul(ps[:, 4 + j, 0], un[:, 2 * (t // 4) + d, t % 4], rb[:, j], start=True, stop=True).then_inc(S["new_mm"], 1)
                    for j, d, t in live:
                        pe.wait_ge(S["new_ev"], i * 24 + K_OF[(step, j)] + 1)
                        pe.matmul(ps[:, j, 1], kd[:, d, t], nb[:, j], start=True, stop=True).then_inc(S["st_mm"], 1)
                        pe.matmul(ps[:, 4 + j, 1], st[:, j], qd[:, d, t * P:(t + 1) * P], start=True, stop=False)
                        pe.matmul(ps[:, 4 + j, 1], nb[:, j], qk[:, 2 * (t // 4) + d, t % 4], start=False, stop=True).then_inc(S["o_mm"], 1)
                pe.wait_ge(S["osq"], i + 1)
                lengths(0, 0, th[:, 0]).then_inc(S["oss"], 1)
                pe.wait_ge(S["odiag"], i + 1)
                for tb in range(NTB):
                    last = pe.matmul(flat(ps[:, 1 + tb]), ones[:], flat(am[:, tb]), start=True, stop=True)
                last.then_inc(S["obc"], 1)
            for u in range(UNITS):
                front(0, u)
            with pe.Fori(0, HEADS - 1) as i:
                main(i, True)
            main(HEADS - 1, False)

        @block.vector
        def _(dve):
            def front(h, u, c, later):
                if u in CONV_AT:
                    n, tap, g = CONV_AT[u]
                    if tap == 0 and g == 0:
                        dve.wait_ge(S[f"x_in{n % 2}"], h * (48, 96)[n % 2 == 0] + (48, 48, 96)[n])
                        if n == 1 and later:
                            dve.wait_ge(S["kc"], h)
                    if later or c.n:
                        c.wait()
                    o, (b, length) = (0, 1024 + 3)[g], SEG[g]
                    dst, src = yn[:, n, b:b + length], x[:, n % 2, o + tap:o + tap + length]
                    if tap == 0:
                        c.add(dve.tensor_scalar(dst, src, cw[:, n, 0:1], None, ALU.mult))
                    else:
                        c.add(dve.scalar_tensor_tensor(dst, src, cw[:, n, tap:tap + 1], dst, ALU.mult, ALU.add))
                    if tap == CW - 1 and g == 1:
                        c.wait()
                        dve.sem_inc(S["conv"], 1)
                if u in SILU_AT:
                    n = SILU_AT[u]
                    dve.wait_ge(S["tanh"], h * 3 + n + 1)
                    dve.scalar_tensor_tensor(yn[:, n], th[:, 0], 1.0, yn[:, n], ALU.add, ALU.mult).then_inc(S["silu"], 1)
                if u == RS_AT:
                    dve.wait_ge(S["ssum"], h * 2 + 2)
                    c.link(dve.tensor_scalar(flat(ms[:]), ps[:, 2, 0, 0:2 * NT], EPS, None, ALU.add))
                    dve.reciprocal(flat(rr[:]), flat(ms[:])).then_inc(S["rs_in"], 1)
                if u == HALF_AT:
                    dve.wait_ge(S["silu"], h * 3 + 3)
                    dve.tensor_scalar(yn[:, 2], yn[:, 2], 0.5, None, ALU.mult).then_inc(S["vhalf"], 1)
                if u in SCALE_AT:
                    m = SCALE_AT[u]
                    n, sl = m // NTB, slice(m % NTB * TB, (m % NTB + 1) * TB)
                    dve.wait_ge(S["bc"], h * 6 + m + 1)
                    dve.scalar_tensor_tensor(yn[:, n, sl], yn[:, n, sl], (0.5 * P ** -0.5) if n == 0 else 0.5,
                                             flat(ps[:, 2 + m % 2]), ALU.mult, ALU.mult).then_inc(S["scaled"], 1)

            def main(i, more):
                c = Chain(dve, S["chain"], i, K_DN)
                fc = Chain(dve, S["fchain"], i + 1, K_FRONT)
                c.link(dve.tensor_copy(col[:], cols[:, bass.ds(i, 1)].rearrange("p a k t -> p (a k) t")))
                dve.wait_ge(S["g_in"], i * 32 + 32)
                for d in range(2):
                    c.add(dve.tensor_copy(cx[:, d], col[:, d]))
                    c.add(dve.tensor_tensor(cx[:, 2 + d], glast(d), col[:, d], ALU.subtract))
                    c.add(dve.tensor_copy(cx[:, 4 + d], glast(d)))
                c.wait()
                dve.sem_inc(S["cols_in"], 1)

                def ediff(n):
                    tg, d = UN[n]
                    b = n % 2
                    if n >= 2:
                        dve.wait_ge(S["amat"], i * 12 + 2 * (n - 2) + 2)
                    e = dd[:, 2 * b]
                    c.link(dve.tensor_tensor(e, four(gbc[:, d, tg * TB:(tg + 1) * TB]),
                                             col[:, d, 4 * tg:4 * tg + 4].unsqueeze(2).to_broadcast([P, 4, P]), ALU.subtract))
                    dve.tensor_scalar(dd[:, 2 * b + 1], e, 0.0, None, ALU.min).then_inc(S["ediff"], 1)
                    dve.wait_ge(S["ediff"], i * 12 + 2 * n + 1)
                    dve.tensor_scalar(e, e, 0.0, None, ALU.max).then_inc(S["ediff"], 1)

                def amat(n):
                    tg, d = UN[n]
                    b = n % 2
                    dve.wait_ge(S["dmask"], i * 12 + 2 * n + 2)
                    dve.wait_ge(S["gram"], i * NTB + tg + 1)
                    c.link(dve.tensor_tensor(am[:, n], ps[:, 0], dd[:, 2 * b], ALU.mult))
                    dve.tensor_tensor(am[:, n], am[:, n], col[:, 2 + d, 4 * tg:4 * tg + 4].unsqueeze(2).to_broadcast([P, 4, P]),
                                      ALU.mult).then_inc(S["amat"], 1)
                    dve.tensor_tensor(qk[:, n], ps[:, 1], dd[:, 2 * b + 1], ALU.mult).then_inc(S["amat"], 1)

                def token_major(n):
                    dve.wait_ge(S["kt_mm"], i * 6 + n + 1)
                    tg = n // 2
                    for d in range(2):
                        fac = cx[:, 2 + d, 4 * tg:4 * tg + 4] if n % 2 == 0 else col[:, 2 + d, 4 * tg:4 * tg + 4]
                        dst = (kd, bv)[n % 2]
                        dve.tensor_tensor(dst[:, d, 4 * tg:4 * tg + 4], ps[:, 4 + n % 4], fac.unsqueeze(2).to_broadcast([P, 4, P]),
                                          ALU.mult).then_inc(S["kt_ev"], 1)

                ediff(0)
                dve.wait_ge(S["cexp"], i + 1)
                c.link(dve.scalar_tensor_tensor(cx[:, 0:2], col[:, 2:4], -1.0, cx[:, 0:2], ALU.mult, ALU.mult))
                dve.wait_ge(S["scaled"], i * 6 + 6)
                for n in range(2 * NTB):
                    if n + 1 < 2 * NTB:
                        ediff(n + 1)
                    token_major(n)
                    if n % 3 == 1:
                        d = n // 3
                        dve.wait_ge(S["eg"], i * 2 + d + 1)
                        dve.tensor_tensor(qd[:, d], qd[:, d], yn[:, 0], ALU.mult).then_inc(S["qd"], 1)
                    amat(n)
                dve.memset(st[:], 0.0).then_inc(S["s0"], 1)
                dve.wait_ge(S["u0"], i * 12 + 12)
                for v in range(LEVELS):
                    for n in range(2 * NTB):
                        if v == 0:
                            dve.wait_ge(S["at_ev"], i * 6 + n + 1)
                        else:
                            dve.wait_ge(S["u_mm"], i * VT + v * 6 + n + 1)
                        dve.sem_inc(S["seen"], 1)
                        d, bank = UN[n][1], 4 + 2 * (n % 2)
                        wide = [P, 4, P]
                        if v < LEVELS - 1:
                            dve.copy_predicated(tn[:, n], join[:, v, 1 - d].unsqueeze(1).to_broadcast(wide),
                                                am[:, n] if v == 0 else ps[:, bank])
                        dve.copy_predicated(un[:, n], join[:, v, d].unsqueeze(1).to_broadcast(wide),
                                            at[:, n] if v == 0 else ps[:, bank + 1]).then_inc(S["u_ev"], 1)
                        u = v * 2 * NTB + n
                        if more:
                            front(i + 1, u, fc, True)
                        if u == GATE_AT:
                            dve.wait_ge(S["zt"], i + 1)
                            dve.scalar_tensor_tensor(zt, th[:, 1], 1.0, zt, ALU.add, ALU.mult).then_inc(S["gated"], 1)
                if more:
                    fc.end()
                dve.wait_ge(S["s0"], i + 1)
                for step in range(8):
                    live = live_chains(step)
                    for j, d, t in live:
                        dve.wait_ge(S["ks"], i * 24 + K_OF[(step, j)] + 1)
                        if step:
                            dve.wait_ge(S["new_mm"], i * 24 + K_OF[(step - 1, j)] + 1)
                        dve.scalar_tensor_tensor(rb[:, j], ps[:, j, 0], cx[:, d, t:t + 1], bv[:, d, t], ALU.mult, ALU.add).then_inc(S["r"], 1)
                    for j, d, t in live:
                        dve.wait_ge(S["st_mm"], i * 24 + K_OF[(step, j)] + 1)
                        dve.wait_ge(S["o_mm"], i * 24 + K_OF[(step, j)] + 1)
                        dve.scalar_tensor_tensor(st[:, j], st[:, j], cx[:, EGL[d], t:t + 1], ps[:, j, 1], ALU.mult, ALU.add).then_inc(S["st_ev"], 1)
                dve.wait_ge(S["o_ev"], i * 24 + 24)
                dve.tensor_tensor(oc[0], oc[0], oc[1], ALU.add).then_inc(S["osum"], 1)
                dve.wait_ge(S["oss"], i + 1)
                c.link(dve.tensor_scalar(oms[:], ps[:, 0, 0, 0:NT], 1.0 / P, EPS, ALU.mult, ALU.add))
                dve.reciprocal(orr[:], oms[:]).then_inc(S["orr"], 1)
                dve.wait_ge(S["oroot"], i + 1)
                dve.tensor_tensor(diag[0], ident[:].unsqueeze(1).to_broadcast([P, NT, P]),
                                  ors[:].unsqueeze(2).to_broadcast([P, NT, P]), ALU.mult).then_inc(S["odiag"], 1)
                dve.wait_ge(S["obc"], i + 1)
                c.link(dve.scalar_tensor_tensor(three(oc[0]), three(oc[0]), nw[:], ps[:, 1:1 + NTB].rearrange("p a b n -> p a (b n)"),
                                                ALU.mult, ALU.mult))
                dve.sem_inc(S["onormed"], 1)
                dve.wait_ge(S["gated"], i + 1)
                dve.scalar_tensor_tensor(oc[0], oc[0], 0.5, zt, ALU.mult, ALU.mult).then_inc(S["out_done"], 1)
                c.end()
            dve.wait_ge(S["prm_in"], 16)
            dve.sem_inc(S["onormed"], 1)
            first = Chain(dve, S["fchain"], 0, K_FRONT)
            for u in range(UNITS):
                front(0, u, first, False)
            with dve.Fori(0, HEADS - 1) as i:
                main(i, True)
            main(HEADS - 1, False)


K_OF = {}
for _step in range(8):
    for _j, (_d, _g) in enumerate(DCHAINS):
        if _step < SEG[_g][1] // P:
            K_OF[(_step, _j)] = len(K_OF)
K_FRONT = len(CONV_AT) + 1
K_DN = 1 + 6 + 1 + 2 * 6 + 2


def merge(nc, proj, o_t, merged, w_br):
    NB = 3
    KB = BW // P
    NS = 3
    with Space(nc, "mg") as s:
        o_hi, o_lo = s.sb("o_hi", [NB * KB, T], F32R), s.sb("o_lo", [NB * KB, T], F32R)
        stage = s.sb("stage", [NS, T])
        w_raw = s.sb("w_raw", [2, KB, P])
        w_hi, w_lo = s.sb("w_hi", [2, KB, P], F32R), s.sb("w_lo", [2, KB, P], F32R)
        gate, total = s.sb("gate", [2, T]), s.sb("total", [2, T])
        acc = s.ps("acc", [2, 4, TB])
        o_in = [s.sem(f"o_in{b}") for b in range(NS)]
        w_in = [s.sem(f"w_in{b}") for b in range(2)]
        g_in = [s.sem(f"g_in{b}") for b in range(2)]
        stored = [s.sem(f"stored{b}") for b in range(2)]
        (o_hi_done, o_lo_done, hi_done, lo_done, mm_done, th_done, gated, summed) = (
            s.sem(x) for x in ("o_hi_done", "o_lo_done", "hi_done", "lo_done", "mm_done", "th_done", "gated", "summed"))
        g_prod = s.sem("g_prod")
        block = s.block()
        w_t = w_br.rearrange("b (k p) n -> p b k n", p=P)


        def columns(i, n):
            return bass.ds(i * (2 * P) + (n // NB) * P, P)

        def half(i, n):
            return i * 48 + (n // 2) * 16 + 16

        @block.sync
        def _(sp):
            for t in range(NB * KB):
                if t >= NS:
                    sp.wait_ge(o_hi_done, t - NS + 1)
                    sp.wait_ge(o_lo_done, t - NS + 1)
                sp.dma_start(stage[:, t % NS], o_t[t]).then_inc(o_in[t % NS], 16)

            def store(tile, i, n):
                sp.wait_ge(summed, i * 6 + n + 1)
                sp.dma_start(merged[bass.ds(tile, 1)].rearrange("a p n -> p (a n)"), total[:, n // NB])\
                    .then_inc(stored[n // NB], 16)

            def body(i, first):
                for n in range(2 * NB):
                    sp.wait_ge(hi_done, i * 6 + n + 1)
                    sp.wait_ge(lo_done, i * 6 + n + 1)
                    sp.dma_start(w_raw[:, n % 2], w_t[:, n % NB, :, columns(i, n)]).then_inc(w_in[n % 2], 16)
                    sp.wait_ge(gated, i * 6 + n + 1)
                    sp.dma_start(gate[:, n % 2], proj[bass.ds(i * 2 + (N_MIX + (n % NB) * KD + n // NB), 1)]
                                 .rearrange("a p n -> p (a n)")).then_inc(g_in[n % 2], 16)
                    if n == 1 and not first:
                        store(i * 2 - 1, i - 1, 2 * NB - 1)
                    if n == NB + 1:
                        store(i * 2, i, NB - 1)
            body(0, True)
            with sp.Fori(1, KD // 2) as i:
                body(i, False)
            store(KD - 1, KD // 2 - 1, 2 * NB - 1)
            for b in range(2):
                sp.wait_ge(stored[b], 16 + KD // 2 * 16)

        @block.scalar
        def _(act):
            for t in range(NB * KB):
                act.wait_ge(o_in[t % NS], t // NS * 16 + 16)
                act.copy(o_hi[:, t], stage[:, t % NS]).then_inc(o_hi_done, 1)
            act.sem_inc(hi_done, 2)
            with act.Fori(0, KD // 2) as i:
                for n in range(2 * NB):
                    b = n % 2
                    act.wait_ge(w_in[b], half(i, n))
                    act.wait_ge(mm_done, i * 6 + n + 1)
                    act.copy(w_hi[:, b], w_raw[:, b]).then_inc(hi_done, 1)
                    act.wait_ge(g_in[b], half(i, n))
                    act.activation(gate[:, b], gate[:, b], ACT.Tanh, scale=0.5).then_inc(th_done, 1)

        def o_low(eng, t):
            eng.wait_ge(o_hi_done, t + 1)
            if t:
                eng.wait_ge(o_lo_done, t)
            eng.tensor_tensor(o_lo[:, t], stage[:, t % NS], o_hi[:, t].bitcast(F32), ALU.subtract).then_inc(o_lo_done, 1)

        @block.gpsimd
        def _(pool):
            for t in range(0, NB * KB, 2):
                o_low(pool, t)
            pool.sem_inc(lo_done, 2)
            with pool.Fori(0, KD // 2) as i:
                for n in range(2 * NB):
                    b = n % 2
                    pool.wait_ge(hi_done, i * 6 + n + 3)
                    pool.tensor_tensor(w_lo[:, b], w_raw[:, b], w_hi[:, b].bitcast(F32), ALU.subtract).then_inc(lo_done, 1)

        @block.tensor
        def _(pe):
            pe.sem_inc(mm_done, 2)
            pe.wait_ge(o_lo_done, NB * KB)
            with pe.Fori(0, KD // 2) as i:
                for n in range(2 * NB):
                    b = n % 2
                    pe.wait_ge(lo_done, i * 6 + n + 3)
                    pe.wait_ge(gated, i * 6 + n + 1)
                    for k in range(KB):
                        for tb in range(NTB):
                            sl = slice(tb * TB, (tb + 1) * TB)
                            o = (n % NB) * KB + k
                            last = mm3(pe, acc[:, b, tb], w_hi[:, b, k], w_lo[:, b, k], o_hi[:, o, sl], o_lo[:, o, sl],
                                       k == 0, k == KB - 1)
                    last.then_inc(mm_done, 1)

        @block.vector
        def _(dve):
            for t in range(1, NB * KB, 2):
                o_low(dve, t)
            dve.sem_inc(gated, 2)
            for b in range(2):
                dve.sem_inc(stored[b], 16)
            three = lambda a: a.rearrange("p (a n) -> p a n", a=NTB)
            with dve.Fori(0, KD // 2) as i:
                for n in range(2 * NB):
                    b, row, first = n % 2, n // NB, n % NB == 0
                    dve.wait_ge(th_done, i * 6 + n + 1)
                    dve.wait_ge(mm_done, i * 6 + n + 3)
                    if first:
                        dve.wait_ge(stored[row], i * 16 + 16)
                        dve.scalar_tensor_tensor(three(total[:, row]), three(gate[:, b]), 1.0, acc[:, b, 0:NTB], ALU.add,
                                                 ALU.mult).then_inc(gated, 1)
                        dve.sem_inc(summed, 1)
                    else:
                        dve.scalar_tensor_tensor(three(gate[:, b]), three(gate[:, b]), 1.0, acc[:, b, 0:NTB], ALU.add,
                                                 ALU.mult).then_inc(g_prod, 1)
                        dve.wait_ge(g_prod, i * 4 + [0, 1, 2, 2, 3, 4][n])
                        dve.tensor_tensor(total[:, row], total[:, row], gate[:, b], ALU.add).then_inc(gated, 1)
                        dve.wait_ge(gated, i * 6 + n + 3)
                        dve.sem_inc(summed, 1)


def out_project(nc, merged, w_out, x_tm, rows):
    NH = D // TB
    with Space(nc, "wo") as s:
        w_hi, w_lo = s.sb("w_hi", [KD, D], F32R), s.sb("w_lo", [KD, D], F32R)
        w_raw = s.sb("w_raw", [2, D])
        m_raw = s.sb("m_raw", [2, KD, P])
        m_hi, m_lo = s.sb("m_hi", [2, KD, P], F32R), s.sb("m_lo", [2, KD, P], F32R)
        acc = s.ps("acc", [2, NH, TB])
        w_in = [s.sem(f"w_in{b}") for b in range(2)]
        m_in = [s.sem(f"m_in{b}") for b in range(2)]
        x_in = [s.sem(f"x_in{t}") for t in range(NT)]
        w_hi_done, w_lo_done, hi_done, lo_done, halved, mm_done, added = (
            s.sem(x) for x in ("w_hi_done", "w_lo_done", "hi_done", "lo_done", "halved", "mm_done", "added"))
        block = s.block()
        m_t = merged.rearrange("k p n -> p k n")

        def w_low(eng, k):
            eng.wait_ge(w_hi_done, k + 1)
            if k:
                eng.wait_ge(w_lo_done, k)
            eng.tensor_tensor(w_lo[:, k], w_raw[:, k % 2], w_hi[:, k].bitcast(F32), ALU.subtract).then_inc(w_lo_done, 1)

        @block.sync
        def _(sp):
            for k in range(KD):
                if k >= 2:
                    sp.wait_ge(w_hi_done, k - 1)
                    sp.wait_ge(w_lo_done, k - 1)
                sp.dma_start(w_raw[:, k % 2], w_out[k * P:(k + 1) * P, :]).then_inc(w_in[k % 2], 16)
            for t in range(NT):
                if t >= 2:
                    sp.wait_ge(lo_done, t - 1)
                sp.dma_start(m_raw[:, t % 2], m_t[:, :, t * P:(t + 1) * P]).then_inc(m_in[t % 2], 16)
                sp.dma_start(x_tm[:, t], rows[t]).then_inc(x_in[t], 16)

        @block.scalar
        def _(act):
            for k in range(KD):
                act.wait_ge(w_in[k % 2], k // 2 * 16 + 16)
                act.copy(w_hi[:, k], w_raw[:, k % 2]).then_inc(w_hi_done, 1)
            for t in range(NT):
                act.wait_ge(halved, t + 1)
                if t >= 2:
                    act.wait_ge(mm_done, t - 1)
                act.copy(m_hi[:, t % 2], m_raw[:, t % 2]).then_inc(hi_done, 1)

        @block.gpsimd
        def _(pool):
            for k in range(0, KD, 2):
                w_low(pool, k)
            for t in range(NT):
                pool.wait_ge(hi_done, t + 1)
                pool.tensor_tensor(m_lo[:, t % 2], m_raw[:, t % 2], m_hi[:, t % 2].bitcast(F32), ALU.subtract).then_inc(lo_done, 1)

        @block.tensor
        def _(pe):
            pe.wait_ge(w_lo_done, KD)
            for t in range(NT):
                b = t % 2
                pe.wait_ge(lo_done, t + 1)
                if t >= 2:
                    pe.wait_ge(added, t - 1)
                for k in range(KD):
                    for n in range(NH):
                        sl = slice(n * TB, (n + 1) * TB)
                        last = mm3(pe, acc[:, b, n], m_hi[:, b, k], m_lo[:, b, k], w_hi[:, k, sl], w_lo[:, k, sl],
                                   k == 0, k == KD - 1)
                last.then_inc(mm_done, 1)

        @block.vector
        def _(dve):
            def halve(t):
                dve.wait_ge(m_in[t % 2], t // 2 * 16 + 16)
                dve.tensor_scalar(m_raw[:, t % 2], m_raw[:, t % 2], 0.5, None, ALU.mult).then_inc(halved, 1)
            for k in range(1, KD, 2):
                w_low(dve, k)
            halve(0)
            for t in range(NT):
                if t + 1 < NT:
                    halve(t + 1)
                dve.wait_ge(mm_done, t + 1)
                dve.wait_ge(x_in[t], 16)
                xt = x_tm[:, t].rearrange("p (a n) -> p a n", a=NH)
                dve.tensor_tensor(xt, acc[:, t % 2], xt, ALU.add).then_inc(added, 1)


def mlp(nc, name, w1, w2, x_tm, u_hi, u_lo, tiles):
    TOK = len(tiles) * P
    HT = TOK // 2
    NG = FF // (2 * P)
    NP = len(tiles) * 2
    with Space(nc, name) as s:
        w1_raw = s.sb("w1_raw", [2, KD, P])
        w1_hi, w1_lo = s.sb("w1_hi", [2, KD, P], F32R), s.sb("w1_lo", [2, KD, P], F32R)
        w2_raw = s.sb("w2_raw", [2, D])
        w2_hi, w2_lo = s.sb("w2_hi", [4, D], F32R), s.sb("w2_lo", [4, D], F32R)
        rel = s.sb("rel", [2, TOK])
        h_hi, h_lo = s.sb("h_hi", [4, TOK], F32R), s.sb("h_lo", [4, TOK], F32R)
        ps1 = s.ps("ps1", [2, 2, TB])
        ps2 = s.ps("ps2", [4, TB])
        w1_in = [s.sem(f"w1_in{b}") for b in range(2)]
        w2_in = [s.sem(f"w2_in{b}") for b in range(2)]
        (w1_hi_done, w1_lo_done, w2_hi_done, w2_lo_done, up_done, relu_done, sq_done, hh_done, hl_done, part_done,
         added) = (s.sem(x) for x in ("w1_hi_done", "w1_lo_done", "w2_hi_done", "w2_lo_done", "up_done", "relu_done",
                                      "sq_done", "hh_done", "hl_done", "part_done", "added"))
        block = s.block()
        w1_t = w1.rearrange("(k p) n -> p k n", p=P)
        two = lambda a: a.rearrange("p (a n) -> p a n", a=2)


        def groups(eng, up, down, late=lambda g, par: None):
            def ahead(g, par):
                up(g + 1, 1 - par)
                down(g, par)
                late(g + 1, 1 - par)
            up(0, 0)
            late(0, 0)
            with eng.Fori(0, NG // 2 - 1) as i:
                ahead(i * 2, 0)
                ahead(i * 2 + 1, 1)
            ahead(NG - 2, 0)
            down(NG - 1, 1)

        @block.sync
        def _(sp):
            def load_w1(g, par):
                for j in range(2):
                    sp.wait_ge(w1_lo_done, g * 2 + j + 1)
                    sp.dma_start(w1_raw[:, j], w1_t[:, :, bass.ds(g * (2 * P) + j * P, P)]).then_inc(w1_in[j], 16)

            def load_w2(g, par):
                for j in range(2):
                    sp.wait_ge(w2_lo_done, g * 2 + j + 1)
                    sp.dma_start(w2_raw[:, j], w2[bass.ds(g * (2 * P) + j * P, P), :]).then_inc(w2_in[j], 16)
            groups(sp, load_w1, load_w2)

        @block.scalar
        def _(act):
            act.sem_inc(relu_done, 2)

            def up(g, par):
                for j in range(2):
                    m = g * 2 + j
                    act.wait_ge(w1_in[j], g * 16 + 16)
                    act.wait_ge(up_done, m + 1)
                    act.copy(w1_hi[:, j], w1_raw[:, j]).then_inc(w1_hi_done, 1)

            def square(g, par):
                for j in range(2):
                    m = g * 2 + j
                    act.wait_ge(up_done, m + 3)
                    act.wait_ge(hl_done, m + 1)
                    act.activation(two(rel[:, j]), ps1[:, j, :, 0:HT], ACT.Relu).then_inc(relu_done, 1)
                    act.wait_ge(sq_done, m + 1)
                    act.copy(h_hi[:, 2 * par + j], rel[:, j]).then_inc(hh_done, 1)

            def down(g, par):
                for j in range(2):
                    act.wait_ge(w2_in[j], g * 16 + 16)
                    act.wait_ge(part_done, g * NP + NP)
                    act.copy(w2_hi[:, 2 * par + j], w2_raw[:, j]).then_inc(w2_hi_done, 1)
            groups(act, up, down, square)

        @block.gpsimd
        def _(pool):
            pool.sem_inc(w1_lo_done, 2)
            pool.sem_inc(w2_lo_done, 2)
            pool.sem_inc(hl_done, 2)

            def up(g, par):
                for j in range(2):
                    m = g * 2 + j
                    pool.wait_ge(w1_hi_done, m + 1)
                    pool.tensor_tensor(w1_lo[:, j], w1_raw[:, j], w1_hi[:, j].bitcast(F32), ALU.subtract).then_inc(w1_lo_done, 1)

            def square(g, par):
                for j in range(2):
                    m = g * 2 + j
                    pool.wait_ge(relu_done, m + 3)
                    pool.wait_ge(part_done, g * NP + NP)
                    pool.tensor_tensor(rel[:, j], rel[:, j], rel[:, j], ALU.mult).then_inc(sq_done, 1)
                    pool.wait_ge(hh_done, m + 1)
                    pool.tensor_tensor(h_lo[:, 2 * par + j], rel[:, j], h_hi[:, 2 * par + j].bitcast(F32), ALU.subtract)\
                        .then_inc(hl_done, 1)

            def down(g, par):
                for j in range(2):
                    pool.wait_ge(w2_hi_done, g * 2 + j + 1)
                    pool.tensor_tensor(w2_lo[:, 2 * par + j], w2_raw[:, j], w2_hi[:, 2 * par + j].bitcast(F32), ALU.subtract)\
                        .then_inc(w2_lo_done, 1)
            groups(pool, up, down, square)

        @block.tensor
        def _(pe):
            pe.sem_inc(up_done, 2)
            pe.sem_inc(part_done, 2 * NP)

            def up(g, par):
                for j in range(2):
                    m = g * 2 + j
                    pe.wait_ge(w1_lo_done, m + 3)
                    pe.wait_ge(relu_done, m + 1)
                    for k in range(KD):
                        for t in range(2):
                            sl = slice(t * HT, (t + 1) * HT)
                            last = mm3(pe, ps1[:, j, t, 0:HT], w1_hi[:, j, k], w1_lo[:, j, k], u_hi[:, k, sl], u_lo[:, k, sl],
                                       k == 0, k == KD - 1)
                    last.then_inc(up_done, 1)

            def down(g, par):
                pe.wait_ge(hl_done, g * 2 + 4)
                pe.wait_ge(w2_lo_done, g * 2 + 4)
                for t in range(len(tiles)):
                    for n in range(2):
                        q = 2 * t + n
                        pe.wait_ge(added, g * NP + q + 1)
                        for j in range(2):
                            a = 2 * par + j
                            last = mm3(pe, ps2[:, q % 4], h_hi[:, a, t * P:(t + 1) * P], h_lo[:, a, t * P:(t + 1) * P],
                                       w2_hi[:, a, n * TB:(n + 1) * TB], w2_lo[:, a, n * TB:(n + 1) * TB], j == 0, j == 1)
                        last.then_inc(part_done, 1)
            groups(pe, up, down)

        @block.vector
        def _(dve):
            dve.sem_inc(added, 4)

            def down(g, par):
                for t in range(len(tiles)):
                    for n in range(2):
                        q = 2 * t + n
                        dve.wait_ge(part_done, g * NP + (2 * NP + q + 1))
                        xt = x_tm[:, tiles[t], n * TB:(n + 1) * TB]
                        dve.tensor_tensor(xt, ps2[:, q % 4], xt, ALU.add).then_inc(added, 1)
            groups(dve, lambda g, par: None, down)


def final_norm(nc, x_tm, gain, outs):
    with Space(nc, "fn") as s:
        junk, ss, ms, rr, rstd, g = s.sb("junk", [D]), s.sb("ss", [NT]), s.sb("ms", [NT]), s.sb("rr", [NT]), s.sb("rstd", [NT]), s.sb("g", [D])
        g_in, squared, mean, recip, rooted, normed, stored = (
            s.sem(x) for x in ("g_in", "squared", "mean", "recip", "rooted", "normed", "stored"))
        block = s.block()

        @block.sync
        def _(sp):
            sp.dma_start(g[:], gain.rearrange("(a n) -> a n", a=1).to_broadcast([P, D])).then_inc(g_in, 16)
            for t in range(NT):
                sp.wait_ge(normed, t + 1)
                sp.dma_start(outs[t], x_tm[:, t]).then_inc(stored, 16)
            sp.wait_ge(stored, NT * 16)

        @block.scalar
        def _(act):
            for t in range(NT):
                if t:
                    act.wait_ge(squared, t)
                act.activation(junk[:], x_tm[:, t], ACT.Square, accum_out=ss[:, t:t + 1]).then_inc(squared, 1)
                if t % 4 == 3:
                    act.wait_ge(recip, t // 4 + 1)
                    act.activation(rstd[:, t - 3:t + 1], rr[:, t - 3:t + 1], ACT.Sqrt).then_inc(rooted, 1)

        @block.vector
        def _(dve):
            dve.wait_ge(g_in, 16)
            for a in range(0, NT, 4):
                sl = slice(a, a + 4)
                dve.wait_ge(squared, a + 4)
                dve.tensor_scalar(ms[:, sl], ss[:, sl], 1.0 / D, EPS, ALU.mult, ALU.add).then_inc(mean, 1)
                dve.wait_ge(mean, a // 4 + 1)
                dve.reciprocal(rr[:, sl], ms[:, sl]).then_inc(recip, 1)
                dve.wait_ge(rooted, a // 4 + 1)
                for t in range(a, a + 4):
                    dve.scalar_tensor_tensor(x_tm[:, t], x_tm[:, t], rstd[:, t:t + 1], g[:], ALU.mult, ALU.mult).then_inc(normed, 1)


def trunk(nc, outs, x_prompt, x_sample, norm1, w_in, na_rpb, dn_conv_w, dn_a_log, dn_dt_bias, dn_norm, lru_conv_w,
          lru_conv_b, lru_w_r, lru_b_r, lru_w_i, lru_b_i, lru_lam, w_br, w_out, norm2, w_mlp1, w_mlp2, norm_f):
    with ExitStack() as whole:
        def scratch(name, shape):
            return nc.dram_tensor(name, shape, F32, kind="Internal").ap()

        proj = scratch("proj", (N_MIX + N_GATE, P, T))
        o_t = scratch("o_t", (3 * BW // P, P, T))
        merged = scratch("merged", (KD, P, T))
        pad = scratch("rpb_pad", (8 * NDR, P))
        bias_d = scratch("bias_table", (NH_PAIR, P, NDR, GRID))
        g_rows = scratch("g_rows", (4 * HEADS, T))
        ident = whole.enter_context(nc.sbuf_tensor("ident", [P, P], F32))
        ones = whole.enter_context(nc.sbuf_tensor("ones", [P, P], F32))
        constants(nc, ident, ones)
        rows = [x_prompt[0, t * P:(t + 1) * P, :] for t in range(8)] + [x_sample[0, t * P:(t + 1) * P, :] for t in range(4)]
        with ExitStack() as held:
            u_hi = held.enter_context(nc.sbuf_tensor("u_hi", [P, KD, T], F32R))
            u_lo = held.enter_context(nc.sbuf_tensor("u_lo", [P, KD, T], F32R))
            with nc.sbuf_tensor("x_in", [P, NT, D], F32) as x_in:
                norm_transpose(nc, "n1", x_in, rows, norm1[0], u_hi, u_lo, ident, list(range(NT)))
            project(nc, "pz", u_hi, u_lo, w_in[0], TILE_Z * P, TILE_LRU - TILE_Z, proj, TILE_Z)
            project(nc, "px", u_hi, u_lo, w_in[0], COL_LRU, N_MIX - TILE_LRU, proj, TILE_LRU)
            project_rglru(nc, u_hi, u_lo, w_in[0], proj, o_t, lru_conv_w[0], lru_conv_b[0], lru_w_r[0], lru_b_r[0],
                          lru_w_i[0], lru_b_i[0], lru_lam[0])
        na_bias(nc, na_rpb[0], pad, bias_d)
        with ExitStack() as held:
            cols = held.enter_context(nc.sbuf_tensor("cols", [P, HEADS, 4, NT], F32))
            neg_strict = held.enter_context(nc.sbuf_tensor("neg_strict", [P, 2, P], F32))
            incl = held.enter_context(nc.sbuf_tensor("incl", [P, 2, P], F32))
            join = held.enter_context(nc.sbuf_tensor("join", [P, LEVELS, 2, P], U8))
            attention(nc, proj, bias_d, o_t, ident, (neg_strict, incl, join))
            delta_prep(nc, proj, g_rows, cols, dn_a_log[0], dn_dt_bias[0], ident)
            deltanet(nc, proj, g_rows, cols, (neg_strict, incl, join), o_t, dn_conv_w[0], dn_norm[0], ident, ones)
        merge(nc, proj, o_t, merged, w_br[0])
        with nc.sbuf_tensor("x_tm", [P, NT, D], F32) as x_tm:
            out_project(nc, merged, w_out[0], x_tm, rows)
            half = NT // 2
            with ExitStack() as held:
                u_hi = held.enter_context(nc.sbuf_tensor("v_hi", [P, KD, half * P], F32R))
                u_lo = held.enter_context(nc.sbuf_tensor("v_lo", [P, KD, half * P], F32R))
                for n in range(2):
                    tiles = list(range(n * half, (n + 1) * half))
                    norm_transpose(nc, f"n2{n}", x_tm, None, norm2[0], u_hi, u_lo, ident, tiles)
                    mlp(nc, f"m{n}", w_mlp1[0], w_mlp2[0], x_tm, u_hi, u_lo, tiles)
            dst = [outs[0][0, t * P:(t + 1) * P, :] for t in range(8)] + [outs[1][0, t * P:(t + 1) * P, :] for t in range(4)]
            final_norm(nc, x_tm, norm_f, dst)


_INS = ['x_prompt', 'x_sample', 'norm1', 'w_in', 'na_rpb', 'dn_conv_w', 'dn_a_log', 'dn_dt_bias', 'dn_norm', 'lru_conv_w',
        'lru_conv_b', 'lru_w_r', 'lru_b_r', 'lru_w_i', 'lru_b_i', 'lru_lam', 'w_br', 'w_out', 'norm2', 'w_mlp1',
        'w_mlp2', 'norm_f']
_OUTS = [(1, 1024, 1024), (1, 512, 1024)]


def kernel(**inputs):
    import numpy as _np
    import concourse.bacc as _bacc
    from concourse import mybir as _mybir
    from concourse.bass_utils import run_bass_kernel_spmd as _run

    nc = _bacc.Bacc("TRN2", target_bir_lowering=False, num_devices=1)
    arrays, aps = {}, {}
    for name in _INS:
        a = _np.ascontiguousarray(inputs[name])
        arrays[f"in_{name}_dram"] = a
        aps[name] = nc.dram_tensor(f"in_{name}_dram", a.shape, _mybir.dt.from_np(a.dtype), kind="ExternalInput").ap()
    outs = [nc.dram_tensor(f"out_{i}_dram", shape, _mybir.dt.float32, kind="ExternalOutput").ap()
            for i, shape in enumerate(_OUTS)]
    trunk(nc, outs=outs, **aps)
    r = _run(nc, [arrays], core_ids=[0])
    return tuple(r.results[0][f"out_{i}_dram"] for i in range(len(_OUTS)))
```
